# Optimizing a Trainium2 kernel written in Bass

```python
import math
import jax
import jax.numpy as jnp
from jax import lax
import numpy as np
import jax, jax.numpy as jnp

D_MODEL = 1024
BATCH = 1
SEQ = 256
DEPTH = 2

F32 = jnp.float32
PLE_DIM = 256
EPS = 1e-6
NEG = -1e30
TINY = 1e-30

SSD_W = D_MODEL
SSD_HEAD_DIM = 64
SSD_H = SSD_W // SSD_HEAD_DIM
SSD_G = 2
SSD_HG = SSD_H // SSD_G
SSD_N = 128
SSD_CONV = 5
SSD_XBC = SSD_W + 2 * SSD_G * SSD_N
SSD_CHUNK = 64

HG_W = D_MODEL
HG_HEAD_DIM = 128
HG_H = HG_W // HG_HEAD_DIM
HG_CHUNK = 16

ML_W = D_MODEL
ML_HEAD_DIM = 128
ML_H = ML_W // ML_HEAD_DIM
ML_CHUNK = 64

N_BRANCH = 3
D_FF = 2816
FFN_CONV = 3

IN_SIZES = (SSD_W, SSD_XBC, 2 * SSD_H,
            HG_W, 2 * HG_W, HG_W, HG_W,
            ML_W, ML_W, ML_W, 2 * ML_H, 2 * ML_H, ML_W,
            N_BRANCH * D_MODEL)
N_IN = sum(IN_SIZES)


def _rmsnorm(x, g):
    xf = x.astype(F32)
    y = xf * lax.rsqrt(jnp.mean(xf * xf, axis=-1, keepdims=True) + EPS)
    return (y * g.astype(F32)).astype(x.dtype)

def _group_rmsnorm(x, g, n_groups):
    shp = x.shape
    xf = x.astype(F32).reshape(shp[:-1] + (n_groups, shp[-1] // n_groups))
    xf = xf * lax.rsqrt(jnp.mean(xf * xf, axis=-1, keepdims=True) + EPS)
    return (xf.reshape(shp) * g.astype(F32)).astype(x.dtype)

def _head_layernorm(x, g, n_heads):
    shp = x.shape
    xf = x.astype(F32).reshape(shp[:-1] + (n_heads, shp[-1] // n_heads))
    xf = xf - jnp.mean(xf, axis=-1, keepdims=True)
    xf = xf * lax.rsqrt(jnp.mean(xf * xf, axis=-1, keepdims=True) + EPS)
    return (xf.reshape(shp) * g.astype(F32)).astype(x.dtype)

def _dwconv(x, w, b):
    width = w.shape[0]
    pad = width // 2
    n_s = x.shape[1]
    xp = jnp.pad(x, ((0, 0), (pad, pad), (0, 0)))
    y = b
    for j in range(width):
        y = y + xp[:, j:j + n_s, :] * w[j]
    return y

def _split(a, sizes):
    idx, acc = [], 0
    for n in sizes[:-1]:
        acc += n
        idx.append(acc)
    return jnp.split(a, idx, axis=-1)

def _flip(a):
    return jnp.flip(a, axis=1)

def _chunk(a, size):
    n_b, n_s = a.shape[:2]
    return a.reshape((n_b, n_s // size, size) + a.shape[2:]).swapaxes(0, 1)

def _unchunk(a):
    n_c, n_b, size = a.shape[:3]
    return a.swapaxes(0, 1).reshape((n_b, n_c * size) + a.shape[3:])

def _ssd_scan(x, dt, A, bm, cm):
    x, dt, bm, cm = x.astype(F32), dt.astype(F32), bm.astype(F32), cm.astype(F32)
    n_b, _, n_g, n_hg, n_p = x.shape
    log_a = dt * A.astype(F32)
    xdt = x * dt[..., None]
    mask = jnp.tril(jnp.ones((SSD_CHUNK, SSD_CHUNK), dtype=bool))

    def body(state, inp):
        xc, ac, bc, cc = inp
        acum = jnp.cumsum(ac, axis=1)
        act = jnp.moveaxis(acum, 1, -1)
        seg = jnp.exp(jnp.where(mask, act[..., :, None] - act[..., None, :], NEG))
        cb = jnp.einsum('blgn,bsgn->bgls', cc, bc)
        y = jnp.einsum('bgls,bghls,bsghp->blghp', cb, seg, xc)
        y = y + jnp.einsum('blgn,bghpn->blghp', cc, state) * jnp.exp(acum)[..., None]
        to_end = jnp.exp(acum[:, -1:] - acum)
        state = (state * jnp.exp(acum[:, -1])[..., None, None]
                 + jnp.einsum('bsgn,bsgh,bsghp->bghpn', bc, to_end, xc))
        return state, y

    state0 = jnp.zeros((n_b, n_g, n_hg, n_p, bm.shape[-1]), F32)
    _, ys = lax.scan(body, state0, (_chunk(xdt, SSD_CHUNK), _chunk(log_a, SSD_CHUNK),
                                    _chunk(bm, SSD_CHUNK), _chunk(cm, SSD_CHUNK)))
    return _unchunk(ys)

def _hgrn2_scan(q, k, v, log_f):
    n_b, _, n_h, n_k = q.shape
    n_v = v.shape[-1]
    mask = jnp.tril(jnp.ones((HG_CHUNK, HG_CHUNK), dtype=bool))[None, :, :, None, None]

    def body(state, inp):
        qc, kc, vc, fc = inp
        b = jnp.cumsum(fc, axis=1)
        o = jnp.einsum('blhk,bhkv->blhv', qc * jnp.exp(b), state)
        w = jnp.exp(jnp.where(mask, b[:, :, None] - b[:, None, :], NEG))
        att = jnp.einsum('bthk,btshk,bshk->bhts', qc, w, kc)
        o = o + jnp.einsum('bhts,bshv->bthv', att, vc)
        b_end = b[:, -1]
        state = (state * jnp.exp(b_end)[..., None]
                 + jnp.einsum('bshk,bshv->bhkv', kc * jnp.exp(b_end[:, None] - b), vc))
        return state, o

    state0 = jnp.zeros((n_b, n_h, n_k, n_v), F32)
    _, ys = lax.scan(body, state0, (_chunk(q, HG_CHUNK), _chunk(k, HG_CHUNK),
                                    _chunk(v, HG_CHUNK), _chunk(log_f, HG_CHUNK)))
    return _unchunk(ys)

def _mlstm_scan(q, k, v, ig, log_f):
    n_b, _, n_h, n_d = q.shape
    mask = jnp.tril(jnp.ones((ML_CHUNK, ML_CHUNK), dtype=bool))

    def body(carry, inp):
        c, n, m = carry
        qc, kc, vc, ic, fc = inp
        bt = jnp.moveaxis(jnp.cumsum(fc, axis=1), 1, -1)
        it = jnp.moveaxis(ic, 1, -1)
        dmat = jnp.where(mask, bt[..., :, None] - bt[..., None, :] + it[..., None, :], NEG)
        inter = bt + m[..., None]
        m_t = jnp.maximum(inter, jnp.max(dmat, axis=-1))
        sc = jnp.einsum('bthd,bshd->bhts', qc, kc) * jnp.exp(dmat - m_t[..., None])
        w_inter = jnp.exp(inter - m_t)
        num = (jnp.einsum('bhts,bshd->bthd', sc, vc)
               + jnp.einsum('bht,bthk,bhvk->bthv', w_inter, qc, c))
        den = jnp.sum(sc, axis=-1) + w_inter * jnp.einsum('bthk,bhk->bht', qc, n)
        denom = jnp.maximum(jnp.abs(den), jnp.exp(-m_t))
        h = num / jnp.moveaxis(denom, -1, 1)[..., None]
        m_new = m_t[..., -1]
        decay = jnp.exp(bt[..., -1] + m - m_new)
        wk = jnp.exp(bt[..., -1:] - bt + it - m_new[..., None])
        c = c * decay[..., None, None] + jnp.einsum('bhs,bshv,bshk->bhvk', wk, vc, kc)
        n = n * decay[..., None] + jnp.einsum('bhs,bshk->bhk', wk, kc)
        return (c, n, m_new), h

    carry0 = (jnp.zeros((n_b, n_h, n_d, n_d), F32), jnp.zeros((n_b, n_h, n_d), F32),
              jnp.full((n_b, n_h), NEG, F32))
    _, ys = lax.scan(body, carry0, (_chunk(q, ML_CHUNK), _chunk(k, ML_CHUNK), _chunk(v, ML_CHUNK),
                                    _chunk(ig, ML_CHUNK), _chunk(log_f, ML_CHUNK)))
    return _unchunk(ys)

def _ssd_branch(z, xbc, dt_raw, conv_w, conv_b, dt_bias, a_log, d_skip, norm_g):
    n_b, n_s, _ = z.shape
    xbc = jax.nn.silu(_dwconv(xbc, conv_w, conv_b))
    xs, bm, cm = _split(xbc, (SSD_W, SSD_G * SSD_N, SSD_G * SSD_N))
    xs = xs.reshape(n_b, n_s, SSD_G, SSD_HG, SSD_HEAD_DIM)
    bm = bm.reshape(n_b, n_s, SSD_G, SSD_N)
    cm = cm.reshape(n_b, n_s, SSD_G, SSD_N)
    dt = jax.nn.softplus(dt_raw.astype(F32).reshape(n_b, n_s, 2, SSD_G, SSD_HG)
                         + dt_bias.astype(F32).reshape(2, SSD_G, SSD_HG))
    A = -jnp.exp(a_log.astype(F32)).reshape(2, SSD_G, SSD_HG)
    y_f = _ssd_scan(xs, dt[:, :, 0], A[0], bm, cm)
    y_b = _flip(_ssd_scan(_flip(xs), _flip(dt[:, :, 1]), A[1], _flip(bm), _flip(cm)))
    y = y_f + y_b + xs.astype(F32) * d_skip.astype(F32).reshape(SSD_G, SSD_HG, 1)
    y = y.reshape(n_b, n_s, SSD_W).astype(z.dtype)
    return _group_rmsnorm(y * jax.nn.silu(z), norm_g, SSD_G)

def _hgrn2_branch(q_raw, f_raw, i_in, g_out, lb, norm_g):
    n_b, n_s, _ = q_raw.shape
    hshape = (n_b, n_s, HG_H, HG_HEAD_DIM)
    q = jax.nn.silu(q_raw.astype(F32)).reshape(hshape)
    v = i_in.astype(F32).reshape(hshape)
    f_raw = f_raw.astype(F32).reshape(n_b, n_s, 2, HG_W)
    lb = lb.astype(F32)
    f = lb + (1.0 - lb) * jax.nn.sigmoid(f_raw)
    log_f = jnp.log(jnp.maximum(f, TINY))
    k = (1.0 - lb) * jax.nn.sigmoid(-f_raw)
    log_f = log_f.reshape(n_b, n_s, 2, HG_H, HG_HEAD_DIM)
    k = k.reshape(n_b, n_s, 2, HG_H, HG_HEAD_DIM)
    o_f = _hgrn2_scan(q, k[:, :, 0], v, log_f[:, :, 0])
    o_b = _flip(_hgrn2_scan(_flip(q), _flip(k[:, :, 1]), _flip(v), _flip(log_f[:, :, 1])))
    o = _group_rmsnorm((o_f + o_b).reshape(n_b, n_s, HG_W), norm_g, HG_H)
    return (o * jax.nn.silu(g_out.astype(F32))).astype(q_raw.dtype)

def _mlstm_branch(q, k, v, ig_raw, fg_raw, o_raw, i_bias, f_bias, norm_g):
    n_b, n_s, _ = q.shape
    hshape = (n_b, n_s, ML_H, ML_HEAD_DIM)
    qf = q.astype(F32).reshape(hshape)
    kf = k.astype(F32).reshape(hshape) * (ML_HEAD_DIM ** -0.5)
    vf = v.astype(F32).reshape(hshape)
    ig = ig_raw.astype(F32).reshape(n_b, n_s, 2, ML_H) + i_bias.astype(F32)
    log_f = jax.nn.log_sigmoid(fg_raw.astype(F32).reshape(n_b, n_s, 2, ML_H) + f_bias.astype(F32))
    h_f = _mlstm_scan(qf, kf, vf, ig[:, :, 0], log_f[:, :, 0])
    h_b = _flip(_mlstm_scan(_flip(qf), _flip(kf), _flip(vf), _flip(ig[:, :, 1]), _flip(log_f[:, :, 1])))
    hn = _head_layernorm((h_f + h_b).reshape(n_b, n_s, ML_W), norm_g, ML_H)
    return (hn * jax.nn.sigmoid(o_raw.astype(F32))).astype(q.dtype)

def first_inputs(seed: int = 0) -> dict:
    key = jax.random.key(seed)
    ks = iter(jax.random.split(key, 40))

    def nrm(shape, scale):
        return jax.random.normal(next(ks), shape, F32) * scale

    def gain(shape):
        return 1.0 + nrm(shape, 0.02)

    x = nrm((BATCH, SEQ, D_MODEL), 1.0)
    p = nrm((DEPTH, BATCH, SEQ, PLE_DIM), 1.0)
    norm_mix_g = gain((DEPTH, D_MODEL))
    w_in = nrm((DEPTH, D_MODEL, N_IN), D_MODEL ** -0.5)
    ssd_conv_w = nrm((DEPTH, SSD_CONV, SSD_XBC), SSD_CONV ** -0.5)
    ssd_conv_b = nrm((DEPTH, SSD_XBC), 0.02)
    dt0 = jnp.exp(jax.random.uniform(next(ks), (DEPTH, 2, SSD_H), F32,
                                     minval=math.log(1e-3), maxval=math.log(1e-1)))
    ssd_dt_bias = dt0 + jnp.log(-jnp.expm1(-dt0))
    ssd_a_log = jnp.log(jax.random.uniform(next(ks), (DEPTH, 2, SSD_H), F32, minval=1.0, maxval=16.0))
    ssd_d = gain((DEPTH, SSD_H))
    ssd_norm_g = gain((DEPTH, SSD_W))
    hg_lb_raw = nrm((DEPTH, 2, HG_W), 0.5)
    hg_norm_g = gain((DEPTH, HG_W))
    ml_i_bias = nrm((DEPTH, 2, ML_H), 0.1)
    ml_f_bias = jnp.linspace(3.0, 6.0, ML_H, dtype=F32) + nrm((DEPTH, 2, ML_H), 0.1)
    ml_norm_g = gain((DEPTH, ML_W))
    w_br_ssd = nrm((DEPTH, SSD_W, D_MODEL), SSD_W ** -0.5)
    w_br_hg = nrm((DEPTH, HG_W, D_MODEL), HG_W ** -0.5)
    w_br_ml = nrm((DEPTH, ML_W, D_MODEL), ML_W ** -0.5)
    w_out = nrm((DEPTH, D_MODEL, D_MODEL), D_MODEL ** -0.5)
    norm_ffn_g = gain((DEPTH, D_MODEL))
    w_up = nrm((DEPTH, D_MODEL, 2 * D_FF), D_MODEL ** -0.5)
    ffn_conv_w = nrm((DEPTH, FFN_CONV, 2 * D_FF), FFN_CONV ** -0.5)
    ffn_conv_b = nrm((DEPTH, 2 * D_FF), 0.02)
    w_down = nrm((DEPTH, D_FF, D_MODEL), D_FF ** -0.5)
    w_ple = nrm((DEPTH, PLE_DIM, D_MODEL), PLE_DIM ** -0.5)
    w_ple_gate = nrm((DEPTH, D_MODEL, D_MODEL), D_MODEL ** -0.5)
    final_norm_g = gain((D_MODEL,))
    return {'x': x, 'p': p, 'norm_mix_g': norm_mix_g, 'w_in': w_in,
            'ssd_conv_w': ssd_conv_w, 'ssd_conv_b': ssd_conv_b, 'ssd_dt_bias': ssd_dt_bias,
            'ssd_a_log': ssd_a_log, 'ssd_d': ssd_d, 'ssd_norm_g': ssd_norm_g,
            'hg_lb_raw': hg_lb_raw, 'hg_norm_g': hg_norm_g,
            'ml_i_bias': ml_i_bias, 'ml_f_bias': ml_f_bias, 'ml_norm_g': ml_norm_g,
            'w_br_ssd': w_br_ssd, 'w_br_hg': w_br_hg, 'w_br_ml': w_br_ml, 'w_out': w_out,
            'norm_ffn_g': norm_ffn_g, 'w_up': w_up, 'ffn_conv_w': ffn_conv_w, 'ffn_conv_b': ffn_conv_b,
            'w_down': w_down, 'w_ple': w_ple, 'w_ple_gate': w_ple_gate, 'final_norm_g': final_norm_g}

def first_block(x, p, norm_mix_g, w_in, ssd_conv_w, ssd_conv_b, ssd_dt_bias, ssd_a_log, ssd_d,
              ssd_norm_g, hg_lb_raw, hg_norm_g, ml_i_bias, ml_f_bias, ml_norm_g,
              w_br_ssd, w_br_hg, w_br_ml, w_out, norm_ffn_g, w_up, ffn_conv_w, ffn_conv_b,
              w_down, w_ple, w_ple_gate, final_norm_g):
    n_b, n_s, _ = x.shape
    lb_soft = jax.nn.softmax(hg_lb_raw.astype(F32), axis=0)
    hg_lb = jnp.cumsum(lb_soft, axis=0) - lb_soft[0:1]
    h = x
    for l in range(DEPTH):
        u = _rmsnorm(h, norm_mix_g[l])
        (s_z, s_xbc, s_dt, g_q, g_f, g_i, g_g, m_q, m_k, m_v, m_i, m_f, m_o,
         gates) = _split(u @ w_in[l], IN_SIZES)
        y_ssd = _ssd_branch(s_z, s_xbc, s_dt, ssd_conv_w[l], ssd_conv_b[l], ssd_dt_bias[l],
                            ssd_a_log[l], ssd_d[l], ssd_norm_g[l])
        y_hg = _hgrn2_branch(g_q, g_f, g_i, g_g, hg_lb[l], hg_norm_g[l])
        y_ml = _mlstm_branch(m_q, m_k, m_v, m_i, m_f, m_o, ml_i_bias[l], ml_f_bias[l], ml_norm_g[l])
        gate = jax.nn.sigmoid(gates.reshape(n_b, n_s, N_BRANCH, D_MODEL))
        merged = (gate[:, :, 0] * (y_ssd @ w_br_ssd[l])
                  + gate[:, :, 1] * (y_hg @ w_br_hg[l])
                  + gate[:, :, 2] * (y_ml @ w_br_ml[l]))
        h = h + merged @ w_out[l]
        u = _rmsnorm(h, norm_ffn_g[l])
        up = _dwconv(u @ w_up[l], ffn_conv_w[l], ffn_conv_b[l])
        a_half, v_half = jnp.split(up, 2, axis=-1)
        h = h + (jax.nn.silu(a_half) * v_half) @ w_down[l]
        h = h + (p[l] @ w_ple[l]) * jax.nn.sigmoid(h @ w_ple_gate[l])
    return _rmsnorm(h, final_norm_g)


DEPTH_2 = 1

MIX_WIDTH = D_MODEL
ATTN_WIDTH = MIX_WIDTH // 2
POOL_WIDTH = MIX_WIDTH - ATTN_WIDTH
N_DIFF_HEADS = 4
DIFF_HEAD_DIM = ATTN_WIDTH // (2 * N_DIFF_HEADS)
DIFF_VALUE_DIM = 2 * DIFF_HEAD_DIM
ROT_DIM = DIFF_HEAD_DIM // 4
ROPE_THETA = 500000.0
Q_BLOCK = 128
POOL_WINDOWS = (2, 4, 8, 16)
N_POOL_GROUPS = len(POOL_WINDOWS)
POOL_GROUP_DIM = POOL_WIDTH // N_POOL_GROUPS
IN_COLS = 3 * ATTN_WIDTH + POOL_WIDTH
N_EXPERT_GROUPS = 4
EXPERTS_PER_GROUP = 8
N_EXPERTS = N_EXPERT_GROUPS * EXPERTS_PER_GROUP
TOP_K_IN_GROUP = 2
D_EXPERT = D_MODEL // 2
MOE_BLOCK = 128
RMS_EPS = 1e-6
N_MOD = 6


def rms_norm(x, g):
    xf = x.astype(jnp.float32)
    y = xf * lax.rsqrt(jnp.mean(xf * xf, axis=-1, keepdims=True) + RMS_EPS)
    return (y * g.astype(jnp.float32)).astype(x.dtype)

def lambda_init_for(layer_idx):
    return 0.8 - 0.6 * math.exp(-0.3 * layer_idx)

def rope_tables(seq_len):
    pos = jnp.arange(seq_len, dtype=jnp.float32)
    inv_freq = ROPE_THETA ** (-jnp.arange(0, ROT_DIM, 2, dtype=jnp.float32) / ROT_DIM)
    ang = pos[:, None] * inv_freq[None, :]
    return jnp.cos(ang), jnp.sin(ang)

def apply_partial_rope(t, cos, sin):
    half = ROT_DIM // 2
    cs = cos[None, :, None, None, :].astype(t.dtype)
    sn = sin[None, :, None, None, :].astype(t.dtype)
    t1 = t[..., :half]
    t2 = t[..., half:ROT_DIM]
    return jnp.concatenate([t1 * cs - t2 * sn, t2 * cs + t1 * sn, t[..., ROT_DIM:]], axis=-1)

def diff_attention(q, k, v, lam, subln_g, lambda_init):
    B, S = q.shape[0], q.shape[1]
    cos, sin = rope_tables(S)
    q = apply_partial_rope(q, cos, sin) * (DIFF_HEAD_DIM ** -0.5)
    k = apply_partial_rope(k, cos, sin)
    nqb = S // Q_BLOCK
    qb = q.reshape(B, nqb, Q_BLOCK, N_DIFF_HEADS, 2, DIFF_HEAD_DIM).transpose(1, 0, 3, 4, 2, 5)
    kt = k.transpose(0, 2, 3, 1, 4)
    vt = v.transpose(0, 2, 1, 3)

    def block(qblk):
        s = jnp.einsum('bhcqd,bhckd->bhcqk', qblk, kt).astype(jnp.float32)
        a = jax.nn.softmax(s, axis=-1)
        w = a[:, :, 0] - lam * a[:, :, 1]
        return jnp.einsum('bhqk,bhkv->bhqv', w.astype(vt.dtype), vt)

    o = lax.map(block, qb)
    o = o.transpose(1, 0, 3, 2, 4).reshape(B, S, N_DIFF_HEADS, DIFF_VALUE_DIM)
    o = rms_norm(o, subln_g) * (1.0 - lambda_init)
    return o.reshape(B, S, N_DIFF_HEADS * DIFF_VALUE_DIM)

def multiscale_pool(u, w_pool, pool_scale):
    B, S = u.shape[0], u.shape[1]
    uf = u.astype(jnp.float32)
    cs = jnp.concatenate([jnp.zeros_like(uf[:, :1]), jnp.cumsum(uf, axis=1)], axis=1)
    pos = jnp.arange(S)
    outs = []
    for g, w in enumerate(POOL_WINDOWS):
        left = w // 2
        right = w - 1 - left
        lo = jnp.clip(pos - left, 0, S)
        hi = jnp.clip(pos + right + 1, 0, S)
        cnt = (hi - lo).astype(jnp.float32)
        mean = (cs[:, hi, g] - cs[:, lo, g]) / cnt[None, :, None]
        outs.append(mean - uf[:, :, g])
    d = jnp.stack(outs, axis=2).astype(u.dtype)
    y = jnp.einsum('bsgc,gcd->bsgd', d, w_pool) * pool_scale
    return y.reshape(B, S, N_POOL_GROUPS * POOL_GROUP_DIM)

def grouped_expert_ffn(xt, flat_e, flat_tok, flat_w, w_gate, w_up, w_down):
    N, D = xt.shape
    NK = flat_e.shape[0]
    order = jnp.argsort(flat_e)
    sorted_e = flat_e[order]
    counts = jax.ops.segment_sum(jnp.ones((NK,), jnp.int32), flat_e, num_segments=N_EXPERTS)
    starts = jnp.cumsum(counts) - counts
    padded = ((counts + MOE_BLOCK - 1) // MOE_BLOCK) * MOE_BLOCK
    pad_ends = jnp.cumsum(padded)
    pad_starts = pad_ends - padded
    rank = jnp.arange(NK, dtype=jnp.int32) - starts[sorted_e]
    dest = pad_starts[sorted_e] + rank
    n_blocks = -(-NK // MOE_BLOCK) + N_EXPERTS
    P = n_blocks * MOE_BLOCK
    row_tok = jnp.full((P,), N, jnp.int32).at[dest].set(flat_tok[order])
    row_w = jnp.zeros((P,), jnp.float32).at[dest].set(flat_w[order])
    block_e = jnp.minimum(
        jnp.searchsorted(pad_ends, jnp.arange(n_blocks, dtype=jnp.int32) * MOE_BLOCK, side='right'),
        N_EXPERTS - 1).astype(jnp.int32)
    x_pad = jnp.concatenate([xt, jnp.zeros((1, D), xt.dtype)], axis=0)
    xb = x_pad[row_tok].reshape(n_blocks, MOE_BLOCK, D)

    def expert_block(args):
        xblk, e = args
        hid = jax.nn.silu(xblk @ w_gate[e]) * (xblk @ w_up[e])
        return hid @ w_down[e]

    yb = lax.map(expert_block, (xb, block_e)).reshape(P, D)
    y = jnp.zeros((N + 1, D), jnp.float32).at[row_tok].add(yb.astype(jnp.float32) * row_w[:, None])
    return y[:N].astype(xt.dtype)

def hierarchical_moe(h, w_rg, b_rg, w_re, b_re, w_gate, w_up, w_down):
    B, S, D = h.shape
    N = B * S
    xt = h.reshape(N, D)
    g_logits = (xt @ w_rg).astype(jnp.float32) + b_rg.astype(jnp.float32)
    g_prob = jax.nn.softmax(g_logits, axis=-1)
    _, g_idx = lax.top_k(g_logits, 1)
    g_sel = g_idx[:, 0]
    tok = jnp.arange(N)
    g_p = g_prob[tok, g_sel]
    e_logits = ((xt @ w_re).astype(jnp.float32) + b_re.astype(jnp.float32)).reshape(N, N_EXPERT_GROUPS, EXPERTS_PER_GROUP)
    e_in = e_logits[tok, g_sel]
    e_prob = jax.nn.softmax(e_in, axis=-1)
    top_p, top_i = lax.top_k(e_prob, TOP_K_IN_GROUP)
    top_p = top_p / jnp.sum(top_p, axis=-1, keepdims=True)
    weights = g_p[:, None] * top_p
    expert_id = (g_sel[:, None] * EXPERTS_PER_GROUP + top_i).astype(jnp.int32)
    flat_tok = jnp.repeat(jnp.arange(N, dtype=jnp.int32), TOP_K_IN_GROUP)
    y = grouped_expert_ffn(xt, expert_id.reshape(-1), flat_tok, weights.reshape(-1), w_gate, w_up, w_down)
    return y.reshape(B, S, D)

def second_inputs(seed: int = 0) -> dict:
    key = jax.random.key(seed)
    ks = jax.random.split(key, 24)
    f32 = jnp.float32
    D = D_MODEL
    nrm = lambda k, shape, s: jax.random.normal(k, shape, f32) * s
    return {
        "x": nrm(ks[0], (BATCH, SEQ, D), 1.0),
        "c": nrm(ks[1], (BATCH, D), 1.0),
        "w_ada": nrm(ks[2], (DEPTH_2, D, N_MOD * D), 0.3 * D ** -0.5),
        "b_ada": nrm(ks[3], (DEPTH_2, N_MOD * D), 0.02),
        "norm1_g": 1.0 + nrm(ks[4], (DEPTH_2, D), 0.02),
        "w_in": nrm(ks[5], (DEPTH_2, D, IN_COLS), D ** -0.5),
        "lambda_q1": nrm(ks[6], (DEPTH_2, DIFF_HEAD_DIM), 0.1),
        "lambda_k1": nrm(ks[7], (DEPTH_2, DIFF_HEAD_DIM), 0.1),
        "lambda_q2": nrm(ks[8], (DEPTH_2, DIFF_HEAD_DIM), 0.1),
        "lambda_k2": nrm(ks[9], (DEPTH_2, DIFF_HEAD_DIM), 0.1),
        "subln_g": 1.0 + nrm(ks[10], (DEPTH_2, DIFF_VALUE_DIM), 0.02),
        "w_pool": nrm(ks[11], (DEPTH_2, N_POOL_GROUPS, POOL_GROUP_DIM, POOL_GROUP_DIM), POOL_GROUP_DIM ** -0.5),
        "pool_scale": 1.0 + nrm(ks[12], (DEPTH_2, N_POOL_GROUPS, POOL_GROUP_DIM), 0.1),
        "w_out": nrm(ks[13], (DEPTH_2, MIX_WIDTH, D), MIX_WIDTH ** -0.5),
        "norm2_g": 1.0 + nrm(ks[14], (DEPTH_2, D), 0.02),
        "w_router_group": nrm(ks[15], (DEPTH_2, D, N_EXPERT_GROUPS), D ** -0.5),
        "b_router_group": nrm(ks[16], (DEPTH_2, N_EXPERT_GROUPS), 0.01),
        "w_router_expert": nrm(ks[17], (DEPTH_2, D, N_EXPERTS), D ** -0.5),
        "b_router_expert": nrm(ks[18], (DEPTH_2, N_EXPERTS), 0.01),
        "w_gate": nrm(ks[19], (DEPTH_2, N_EXPERTS, D, D_EXPERT), D ** -0.5),
        "w_up": nrm(ks[20], (DEPTH_2, N_EXPERTS, D, D_EXPERT), D ** -0.5),
        "w_down": nrm(ks[21], (DEPTH_2, N_EXPERTS, D_EXPERT, D), D_EXPERT ** -0.5),
        "final_g": 1.0 + nrm(ks[22], (D,), 0.02),
    }

def second_block(x, c, w_ada, b_ada, norm1_g, w_in, lambda_q1, lambda_k1, lambda_q2, lambda_k2,
              subln_g, w_pool, pool_scale, w_out, norm2_g, w_router_group, b_router_group,
              w_router_expert, b_router_expert, w_gate, w_up, w_down, final_g):
    B, S, D = x.shape
    A = ATTN_WIDTH
    for l in range(DEPTH_2):
        lambda_init = lambda_init_for(l)
        mod = jax.nn.silu(c) @ w_ada[l] + b_ada[l]
        sh1, sc1, g1, sh2, sc2, g2 = jnp.split(mod, N_MOD, axis=-1)
        h = rms_norm(x, norm1_g[l]) * (1.0 + sc1[:, None]) + sh1[:, None]
        z = h @ w_in[l]
        q = z[..., :A].reshape(B, S, N_DIFF_HEADS, 2, DIFF_HEAD_DIM)
        k = z[..., A:2 * A].reshape(B, S, N_DIFF_HEADS, 2, DIFF_HEAD_DIM)
        v = z[..., 2 * A:3 * A].reshape(B, S, N_DIFF_HEADS, DIFF_VALUE_DIM)
        u = z[..., 3 * A:].reshape(B, S, N_POOL_GROUPS, POOL_GROUP_DIM)
        lam = (jnp.exp(jnp.sum(lambda_q1[l].astype(jnp.float32) * lambda_k1[l].astype(jnp.float32)))
               - jnp.exp(jnp.sum(lambda_q2[l].astype(jnp.float32) * lambda_k2[l].astype(jnp.float32)))
               + lambda_init)
        a_out = diff_attention(q, k, v, lam, subln_g[l], lambda_init)
        p_out = multiscale_pool(u, w_pool[l], pool_scale[l])
        mix = jnp.concatenate([a_out, p_out], axis=-1) @ w_out[l]
        x = x + g1[:, None] * mix
        h = rms_norm(x, norm2_g[l]) * (1.0 + sc2[:, None]) + sh2[:, None]
        y = hierarchical_moe(h, w_router_group[l], b_router_group[l], w_router_expert[l],
                             b_router_expert[l], w_gate[l], w_up[l], w_down[l])
        x = x + g2[:, None] * y
    return rms_norm(x, final_g)


def setup_inputs(seed=0):
    out = dict(first_inputs(seed))
    for name, value in second_inputs(seed + 1).items():
        if name != "x":
            out[name + "_2"] = value
    return out


def reference(
    x, p, norm_mix_g, w_in, ssd_conv_w, ssd_conv_b, ssd_dt_bias, ssd_a_log, ssd_d, ssd_norm_g,
    hg_lb_raw, hg_norm_g, ml_i_bias, ml_f_bias, ml_norm_g, w_br_ssd, w_br_hg, w_br_ml, w_out,
    norm_ffn_g, w_up, ffn_conv_w, ffn_conv_b, w_down, w_ple, w_ple_gate, final_norm_g, c_2,
    w_ada_2, b_ada_2, norm1_g_2, w_in_2, lambda_q1_2, lambda_k1_2, lambda_q2_2, lambda_k2_2,
    subln_g_2, w_pool_2, pool_scale_2, w_out_2, norm2_g_2, w_router_group_2, b_router_group_2,
    w_router_expert_2, b_router_expert_2, w_gate_2, w_up_2, w_down_2, final_g_2,
):
    x = first_block(
        x, p, norm_mix_g, w_in, ssd_conv_w, ssd_conv_b, ssd_dt_bias, ssd_a_log, ssd_d,
        ssd_norm_g, hg_lb_raw, hg_norm_g, ml_i_bias, ml_f_bias, ml_norm_g, w_br_ssd, w_br_hg,
        w_br_ml, w_out, norm_ffn_g, w_up, ffn_conv_w, ffn_conv_b, w_down, w_ple, w_ple_gate,
        final_norm_g,
    )
    return second_block(
        x, c_2, w_ada_2, b_ada_2, norm1_g_2, w_in_2, lambda_q1_2, lambda_k1_2, lambda_q2_2,
        lambda_k2_2, subln_g_2, w_pool_2, pool_scale_2, w_out_2, norm2_g_2, w_router_group_2,
        b_router_group_2, w_router_expert_2, b_router_expert_2, w_gate_2, w_up_2, w_down_2,
        final_g_2,
    )


_drawn_inputs = setup_inputs


def setup_inputs(seed=0):
    import zlib

    import numpy as np

    out = dict(_drawn_inputs(seed))
    spreads = {}
    factors = {'ssd_d': 6.849,
     'ssd_norm_g': 3.826,
     'hg_lb_raw': 5.278,
     'hg_norm_g': 6.539,
     'ml_i_bias': 8.0,
     'ml_norm_g': 7.413,
     'norm_ffn_g': 2.998,
     'ffn_conv_b': 3.005,
     'norm1_g_2': 8.0,
     'lambda_q1_2': 8.0,
     'lambda_k1_2': 8.0,
     'lambda_q2_2': 3.501,
     'lambda_k2_2': 8.0,
     'subln_g_2': 8.0,
     'pool_scale_2': 4.29,
     'norm2_g_2': 6.824,
     'b_router_group_2': 8.0,
     'b_router_expert_2': 8.0,
     'final_g_2': 2.957}
    for name, (base, spread) in spreads.items():
        noise = np.random.default_rng([zlib.crc32(name.encode()), seed]).standard_normal(out[name].shape)
        drawn = base * np.exp(spread * noise) if base else spread * noise
        out[name] = jnp.asarray(drawn.astype(out[name].dtype))
    for name, factor in factors.items():
        out[name] = (out[name] * factor).astype(out[name].dtype)
    return out
```

```python
from contextlib import ExitStack

import numpy as np

import concourse.bass as bass
from concourse import mybir

F32 = mybir.dt.float32
U32 = mybir.dt.uint32
ALU = mybir.AluOpType
ACT = mybir.ActivationFunctionType
AX_X = mybir.AxisListType.X

P = 128
D = 1024
S = 256
KC = D // P
T = S // P
DEPTH = 2
EPS = 1e-6
NEG = -1e30
TINY = 1e-30
LN_FLOOR = 2.0 ** -60
SSD_H, HG_H, ML_H = 16, 8, 8
SSD_CONV, FFN_CONV = 5, 3
FF = 2816
FC = FF // P
UC = 2 * P
UNIT = KC * UC
RING = 3
GBANKS = 3

KINDS = (["rows"] + ["z"] * 4 + ["xbc"] * 6 + ["hf"] * 8 + ["hq"] * 4 + ["hi"] * 4 + ["hg"] * 4
         + ["mq"] * 4 + ["mk"] * 4 + ["mv"] * 4 + ["mo"] * 4
         + ["gs", "bs"] * 4 + ["gh"] * 4 + ["gm"] * 4 + ["bh"] * 4 + ["bm"] * 4
         + ["out"] * 4 + ["up"] * 22 + ["down"] * 12 + ["ple"] + ["pleg"] * 4)
UNITS = len(KINDS)
OF = {k: KINDS.index(k) for k in dict.fromkeys(KINDS)}


def bank_uses():
    use, out = 0, []
    for n, kind in enumerate(KINDS):
        if kind == "ple":
            out.append(None)
        elif kind == "down":
            out.append(use)
            if (n - OF["down"]) % 3 == 2:
                use += 1
        else:
            out.append(use)
            use += 1
    return out, use


USE, USES = bank_uses()
assert UNITS % RING == 0 and USES % GBANKS == 0
USES_PER_BANK = USES // GBANKS

PAR = {}
_at = 0
for _name, _n in (("mix_g", 8), ("conv_w", 60), ("conv_b", 12), ("ssd_d", 8), ("ssd_g", 8), ("hg_g", 8),
                  ("ml_g", 8), ("ffn_g", 8), ("fconv_w", 132), ("fconv_b", 44), ("row_b", 1), ("a_log", 1),
                  ("lb_raw", 32), ("lb_mask", 2), ("p", 512)):
    PAR[_name] = _at
    _at += _n
NPAR = _at

CON = {}
_at = 0
for _name, _n in (("ident", 128), ("ones", 128), ("fw", 512), ("bw", 512), ("mf", 256), ("mb", 256),
                  ("lev", 896)):
    CON[_name] = _at
    _at += _n
NCON = _at


HEADS2, HD2 = 4, 64
GROUPS, PER_GROUP = 4, 8
EXPERTS = GROUPS * PER_GROUP
LAMBDA_INIT = 0.8 - 0.6
ADA_UNITS = 6 * D // UC
WIN2, WOUT2, ROUTER = ADA_UNITS, ADA_UNITS + 8, ADA_UNITS + 12
MOE = ROUTER + 1
UNITS2 = MOE + EXPERTS * 6
ALL_UNITS = DEPTH * UNITS + UNITS2

PAR2 = {}
_at = 0
for _name, _n in (("c", 8), ("b_ada", 48), ("fin1_g", 8), ("n1_g", 8), ("n2_g", 8), ("fin2_g", 8), ("sub_g", 1),
                  ("pool_s", 4), ("lam", 4), ("w_pool", 512), ("b_route", 36)):
    PAR2[_name] = _at
    _at += _n
NPAR2 = _at

CON2 = {}
_at = 0
for _name, _n in (("cos", 256), ("sin", 256), ("rot", 128), ("cnt", 1024), ("iota", 8)):
    CON2[_name] = _at
    _at += _n
NCON2 = _at


def moe_order():
    out = [(0, j) for j in range(4)]
    for e in range(1, EXPERTS):
        out += [(e, j) for j in range(4)] + [(e - 1, 4), (e - 1, 5)]
    return out + [(EXPERTS - 1, 4), (EXPERTS - 1, 5)]


def constants2():
    c = np.zeros((P, NCON2), np.float32)
    rot_dim = HD2 // 4
    hf = rot_dim // 2
    pos = np.arange(S, dtype=np.float32)
    inv = np.power(np.float32(500000.0), -np.arange(0, rot_dim, 2, dtype=np.float32) / np.float32(rot_dim)).astype(np.float32)
    ang = (pos[:, None] * inv[None, :]).astype(np.float32)
    cos, sin = np.cos(ang).astype(np.float32), np.sin(ang).astype(np.float32)
    ct, sn, rot = np.ones((P, S), np.float32), np.zeros((P, S), np.float32), np.zeros((P, P), np.float32)
    for base in (0, HD2):
        for i in range(hf):
            ct[base + i], ct[base + i + hf] = cos[:, i], cos[:, i]
            sn[base + i], sn[base + i + hf] = -sin[:, i], sin[:, i]
            rot[base + i + hf, base + i] = 1.0
            rot[base + i, base + i + hf] = 1.0
    c[:, 0:256], c[:, 256:512], c[:, 512:640] = ct, sn, rot
    t = np.arange(S)
    for g in range(4):
        w = 2 << g
        left, right = w // 2, w - 1 - w // 2
        cnt = (np.clip(t + right + 1, 0, S) - np.clip(t - left, 0, S)).astype(np.float32)
        c[:, 640 + g * S:640 + (g + 1) * S] = np.float32(1.0) / cnt
    c[:, CON2["iota"]:] = np.arange(8, dtype=np.float32)
    return c


def constants():
    c = np.zeros((P, NCON), np.float32)
    i = np.arange(P)
    s, t = i[:, None], i[None, :]

    def put(name, a):
        c[:, CON[name]:CON[name] + a.shape[1]] = a

    one, zero = np.ones((P, P), np.float32), np.zeros((P, P), np.float32)
    le, ge = (s <= t).astype(np.float32), (s >= t).astype(np.float32)
    put("ident", np.eye(P, dtype=np.float32))
    put("ones", one)
    put("fw", np.concatenate([le, one, zero, le], 1))
    put("bw", np.concatenate([ge, zero, one, ge], 1))
    put("mf", np.concatenate([np.where(s <= t, 0, NEG).astype(np.float32), zero], 1))
    put("mb", np.concatenate([zero, np.where(s >= t, 0, NEG).astype(np.float32)], 1))
    lev = [((s // (2 * m) == t // (2 * m)) & (s // m != t // m)).astype(np.float32)
           for m in (1, 2, 4, 8, 16, 32, 64)]
    put("lev", np.concatenate(lev, 1))
    return c


class Signal:

    def __init__(self, sem, per_layer, credit=0):
        self.sem, self.per, self.credit = sem, per_layer, credit

    def at(self, lay, n):
        return lay * self.per + (self.credit + n)


class Steps:

    def __init__(self, eng, sem):
        self.eng, self.sem, self.n = eng, sem, 0

    def done(self, ins):
        ins.then_inc(self.sem, 1)
        self.n += 1

    def wait(self, back=0):
        self.eng.wait_ge(self.sem, self.n - back)


def program(nc, stream, par_d, con_d, x_d, par2_d, con2_d, out, upto=None):
    ctx = ExitStack()
    with ctx:
        def sb(name, shape, dt=F32):
            return ctx.enter_context(nc.sbuf_tensor(name, shape, dt))

        def sem(name):
            return ctx.enter_context(nc.semaphore(name))

        ring = sb("ring", [P, RING, UNIT])
        h = sb("h", [P, KC, S])
        u = sb("u", [P, KC, S])
        par = sb("par", [P, NPAR])
        con = sb("con", [P, NCON])
        arena = sb("arena", [P, 130, S])
        rows = sb("rows", [96, S])
        rtmp = sb("rtmp", [96, 2, S])
        dtr = sb("dtr", [32, S])
        tok = sb("tok", [P, T, P])
        ctok = sb("ctok", [P, T, 48])
        ntok = sb("ntok", [P, T, 48])
        arow = sb("arow", [16, 2, S])
        mrow = sb("mrow", [8, 4, 2, S])
        etok = sb("etok", [P, T, 2, 8])
        rstd = sb("rstd", [P, 2, 2, S])
        small = sb("small", [P, 256])
        rowt = sb("rowt", [EXPERTS, S])
        mod = sb("mod", [P, 80])
        eps = sb("eps", [P, 1])
        nega = sb("nega", [32, 2])
        lb = sb("lb", [P, 3, 16])

        def chunks(at, n):
            return arena[:, at:at + n, :]

        def flat(at, n):
            return arena[:, at:at + n, :].rearrange("p c s -> p (c s)")

        Z, XBC, XTOK, CB = 0, 8, 20, 28
        SE = (32, 35)
        SW = (38, 40)
        HF, HQ, HV, HG, HK, HVT = 42, 58, 66, 74, 82, 98
        HE = (8, 16)
        HATT = 24
        MQ, MK, MV, MO, MERGED, GS = 106, 114, 66, 32, 122, 40
        MVT, ME, MA, HSUM, GH, GM = 42, (51, 54), (82, 85), 98, 88, 8
        HID, FT, PLE, PLG = 8, (98, 100), 42, 50
        SQ = 106

        Q2, K2, V2, U2, V2T, O2, P2 = 0, 4, 8, 12, 16, 20, 24
        PADA, PADB, EA, WA, WAT, RD = 28, 33, (38, 42), (46, 48), (50, 52), 54
        HIDE, SG2, WB = (28, 32), 36, 40
        CON2_AT, PAR2_AT = 114, 121

        banks = [ctx.enter_context(nc.psum_tensor(f"bank{i}", [P, 512], F32)) for i in range(8)]
        G, A = banks[:GBANKS], banks[GBANKS:]
        E4 = G + [A[4]]
        ident = con[:, CON["ident"]:CON["ident"] + P]
        ones = con[:, CON["ones"]:CON["ones"] + P]

        v2tok = flat(V2T, 4).rearrange("p (i n) -> p i n", i=T)
        xtok = flat(XTOK, 8).rearrange("p (i n) -> p i n", i=T)
        hvtok = flat(HVT, 8).rearrange("p (i n) -> p i n", i=T)
        hatt = flat(HATT, 8).rearrange("p (i a s) -> p i a s", i=T, a=4)
        mvtok = flat(MVT, 9)[:, 0:T * 8 * 129].rearrange("p (i a e) -> p i a e", i=T, a=8)
        hsum = flat(HSUM, 8).rearrange("p (i a e) -> p i a e", i=T, a=8)

        def half(x, m, which):
            return x.rearrange("p (n two m) -> p n two m", two=2, m=m)[:, :, which, :]

        def cn(name, a, b):
            return con[:, CON[name] + a:CON[name] + b]

        def pc(name, i=0):
            return par[:, PAR[name] + i:PAR[name] + i + 1]

        def c2(name, a, b):
            at = CON2[name]
            return flat(CON2_AT, 7)[:, at + a:at + b]

        def p2(name, i=0, n=1):
            at = PAR2[name]
            return flat(PAR2_AT, 3)[:, at + i:at + i + n]

        def signal(name, per_layer, credit=0):
            return Signal(sem(name), per_layer, credit)

        landed = [sem(f"weights_landed{i}") for i in range(RING)]
        par_in, con_in, x_in, stored = sem("par_landed"), sem("constants_landed"), sem("x_landed"), sem("stored")
        dve_step, act_step, eps_set = sem("dve_step"), sem("act_step"), sem("eps_set")
        unit_done = signal("unit_done", UNITS)
        freed = [signal(f"bank{i}_read", USES_PER_BANK) for i in range(GBANKS)]
        center = signal("center_taps_done", 6 + 22)
        sq_ready = signal("squares_ready", 2)
        ss_ready = signal("square_sums_ready", 2)
        rs_ready = signal("rstd_ready", 2)
        u_ready = signal("u_ready", 2)
        lb_in = signal("lb_shifted", 1)
        lb_exp = signal("lb_exponentials", 1)
        nega_exp = signal("a_exponential", 1)
        sp_abs = signal("softplus_abs", 1)
        sp_ln = signal("softplus_log", 1)
        rows_ok = signal("rows_ready", 1)
        rowsT = signal("rows_transposed", 1)
        tok_ok = signal("rows_by_token_copied", 1)
        cum_ok = signal("cumulative_sums_ready", 3)
        m_ok = signal("m_rows_ready", 1)
        em_ok = signal("exp_minus_m_ready", 1)
        emT = signal("exp_minus_m_transposed", 1)
        rows_fin = signal("row_scalars_ready", 1)
        xs_ok = signal("xs_ready", 1)
        xT = signal("xs_transposed", 4)
        xT_cp = signal("xs_by_token_copied", 4)
        cb_ok = signal("cb_ready", 2)
        cb_cp = signal("cb_copied", 2)
        bc_ok = signal("decay_row_spread", SSD_H)
        arg_ok = signal("decay_arguments_ready", SSD_H)
        exp_ok = signal("decays_ready", SSD_H)
        att_ok = signal("ssd_weights_ready", SSD_H)
        y_ok = signal("ssd_sums_ready", SSD_H)
        y_cp = signal("ssd_sums_read", SSD_H // 2)
        yz_ok = signal("ssd_gated", 1)
        ysq = signal("ssd_squares_ready", 1)
        yss = signal("ssd_square_sums_ready", 1)
        yrs = signal("ssd_rstd_ready", 1)
        ys_fin = signal("ssd_branch_ready", 1)
        hsig = signal("hg_sigmoids_ready", 1)
        hsilu = signal("hg_silus_ready", 1)
        hclamp = signal("hg_forget_clamped", 1)
        hln = signal("hg_forget_logs_ready", 1)
        hvT = signal("hg_v_transposed", 4)
        hvT_cp = signal("hg_v_by_token_copied", 4)
        HSTEPS = 18
        hargs = signal("hg_arguments_ready", 16)
        hexp = signal("hg_decays_ready", 16)
        hqk = signal("hg_operands_ready", HSTEPS)
        hprod = signal("hg_products_ready", HSTEPS)
        hcp = signal("hg_weights_copied", HSTEPS)
        ho_ok = signal("hg_sums_ready", 4)
        ho_cp = signal("hg_sums_copied", 4)
        hsq = signal("hg_squares_ready", 1)
        hss = signal("hg_square_sums_ready", 1)
        hrs = signal("hg_rstd_ready", 1)
        yh_fin = signal("hg_branch_ready", 1)
        mvT = signal("ml_v_transposed", 4)
        mvT_cp = signal("ml_v_by_token_copied", 5)
        msig = signal("ml_output_gate_ready", 1)
        mbc = signal("ml_row_spread", ML_H)
        mqk = signal("ml_qk_ready", ML_H)
        marg = signal("ml_arguments_ready", ML_H)
        mexp = signal("ml_decays_ready", ML_H)
        matt = signal("ml_weights_ready", ML_H)
        mnum = signal("ml_sums_ready", ML_H)
        mh_cp = signal("ml_sums_read", ML_H)
        mcen = signal("ml_centred", 1)
        msq = signal("ml_squares_ready", 1)
        mvar = signal("ml_variance_ready", 1)
        mrs = signal("ml_rstd_ready", 1)
        mhn = signal("ml_normalised", 1)
        mhT = signal("ml_transposed", 4)
        ym_fin = signal("ml_branch_ready", 1)
        merge_ok = signal("merged_ready", 1)
        silu_ok = signal("ffn_silu_ready", 22)
        hid_ok = signal("ffn_hidden_ready", 22)
        ple_cp = signal("ple_copied", 1)
        h_fin = signal("h_ready", 1)

        par2_in = sem("par2_landed")
        cs_ok = sem("silu_c_ready")
        mod_ok = sem("modulation_ready")
        lam_in, lam_mm, lam_exp = sem("lambda_products"), sem("lambda_sums"), sem("lambda_exponentials")
        rope_mm, rope_ok = sem("rope_turned"), sem("rope_done")
        v2T, v2T_cp = sem("v2_transposed"), sem("v2_copied")
        sc_ok, sc_max, sc_exp, w2_ok = sem("scores_ready"), sem("score_maxima"), sem("score_exps"), sem("diff_weights_ready")
        w2T, w2T_cp, o2_ok, o2_cp = sem("diff_weights_transposed"), sem("diff_weights_copied"), sem("diff_sums"), sem("diff_sums_copied")
        o2_sq, o2_ss, o2_rs, o2_fin = sem("diff_squares"), sem("diff_square_sums"), sem("diff_rstd"), sem("diff_out")
        pool_d, pool_mm, pool_fin = sem("pool_means"), sem("pool_products"), sem("pool_out")
        r_mm, r_sh, r_exp, r_w, r_T, r_wT = (sem(f"route_{n}") for n in
                                             ("logits", "shifted", "exps", "weights", "transposed", "rows"))
        wb_mm, wb_cp = sem("expert_row_spread"), sem("expert_row_copied")
        e4_freed = sem("expert_bank3_read")
        gate_ok, hide_ok, y2_ok, y2_fin = sem("expert_gate"), sem("expert_hidden"), sem("experts_summed"), sem("x_final")

        B2 = DEPTH * UNITS

        def done2(m):
            return unit_done.sem, B2 + m + 1

        def landed2(m):
            return landed[m % RING], 16 * ((B2 + m) // RING + 1)

        def use2(m):
            k = m - WIN2
            return k % GBANKS, DEPTH * USES_PER_BANK + k // GBANKS

        G2 = DEPTH * USES_PER_BANK + 12 // GBANKS

        def evac(lay, unit):
            k = USE[unit]
            s = freed[k % GBANKS]
            return s.sem, s.at(lay, k // GBANKS + 1)

        def last(kind):
            return OF[kind] + KINDS.count(kind) - 1

        sched = [("norm", 0), ("unit", 0), ("lb", 0), ("rows", 0)]
        for n in range(1, OF["hf"]):
            sched.append(("unit", n))
            if n in (3, 6, 9):
                sched.append((f"rows{n // 3}", 0))
        sched.append(("silu_x", 0))
        for i in range(22):
            if i < 20:
                sched.append(("unit", OF["hf"] + i))
            if i == 1:
                sched.append(("xs_turn", 0))
            if i == 2:
                sched.append(("cb", 0))
            k = i - 3
            if 0 <= k < SSD_H:
                sched.append(("bc", k))
            if 0 <= k - 1 < SSD_H:
                sched.append(("seg", k - 1))
            if 0 <= k - 2 < SSD_H:
                sched.append(("y", k - 2))
        sched += [("hprep", 0), ("ssd_norm", 0), ("hclamp", 0), ("hvt", 0), ("hlog", 0)]
        for i in range(24):
            sched.append(("unit", OF["mq"] + i))
            k = i - 4
            if 0 <= k < HSTEPS:
                sched.append(("hgA", k))
            if 0 <= k - 1 < HSTEPS:
                sched.append(("hgB", k - 1))
            if 0 <= k - 2 < HSTEPS:
                sched.append(("hgC", k - 2))
            if k - 2 == 8:
                sched.append(("ho", 0))
        sched += [("ho", 1), ("hnorm", 0), ("mvt", 0)]
        for i in range(10):
            if i < 8:
                sched.append(("unit", OF["gh"] + i))
                sched.append(("mlA", i))
            if 0 <= i - 1 < 8:
                sched.append(("mlB", i - 1))
            if 0 <= i - 2 < 8:
                sched.append(("mlC", i - 2))
        for i in range(4):
            sched.append(("unit", OF["bh"] + i))
        sched += [("mlnorm", 0), ("mlturn", 0)]
        sched += [("unit", OF["bm"] + i) for i in range(4)]
        sched += [("unit", OF["out"] + i) for i in range(4)] + [("norm", 1)]
        for i in range(23):
            if i < 22:
                sched.append(("unit", OF["up"] + i))
            if i >= 1:
                sched.append(("hid", i - 1))
        sched += [("unit", n) for n in range(OF["down"], UNITS)] + [("ple_add", 0)]
        SECOND = ("ada", "attn", "route", "last")
        second = not upto or upto in SECOND
        n_layers = DEPTH if second else 1
        if upto and not second:
            cut = [i for i, s in enumerate(sched) if s[0] == upto][-1]
            sched = sched[:cut + 1]
        n_units = max([n for k, n in sched if k == "unit"]) + 1
        assert upto and not second or [n for k, n in sched if k == "unit"] == list(range(UNITS))

        block = ctx.enter_context(nc.Block())

        @block.sync
        def _(sp):
            total = n_units if upto and upto not in SECOND else ALL_UNITS
            for n in range(RING):
                sp.dma_start(ring[:, n, :], stream[n]).then_inc(landed[n], 16)
            with sp.Fori(1, total // RING) as i:
                for r in range(RING):
                    sp.wait_ge(unit_done.sem, i * RING + (r - RING + 1))
                    sp.dma_start(ring[:, r, :], stream[i * RING + r]).then_inc(landed[r], 16)
            for n in range(total // RING * RING, total):
                sp.wait_ge(unit_done.sem, n - RING + 1)
                sp.dma_start(ring[:, n % RING, :], stream[n]).then_inc(landed[n % RING], 16)
            if not upto:
                sp.wait_ge(y2_fin, 2)
                sp.dma_start(out, flat(0, KC)).then_inc(stored, 16)
                sp.wait_ge(stored, 16)

        @block.gpsimd
        def _(pool):
            pool.dma_start(con[:], con_d).then_inc(con_in, 16)
            pool.dma_start(h[:].rearrange("p c s -> p (c s)"), x_d).then_inc(x_in, 16)
            for lay in range(n_layers):
                if lay:
                    pool.wait_ge(h_fin.sem, h_fin.at(lay, 0))
                pool.dma_start(par[:], par_d[lay]).then_inc(par_in, 16)
            if second:
                pool.wait_ge(hid_ok.sem, hid_ok.at(DEPTH, 0))
                pool.dma_start(flat(CON2_AT, 7)[:, 0:NCON2], con2_d).then_inc(par2_in, 16)
                pool.dma_start(flat(PAR2_AT, 3)[:, 0:NPAR2], par2_d).then_inc(par2_in, 16)

        @block.tensor
        def _(pe):
            RHS = {"bs": Z, "bh": HQ, "bm": MO, "out": MERGED}
            NEED = {"rows": (u_ready, 1), "up": (u_ready, 2), "bs": (ys_fin, 1), "bh": (yh_fin, 1),
                    "bm": (ym_fin, 1), "out": (merge_ok, 1), "down": (hid_ok, 22)}

            def unit(lay, n):
                kind = KINDS[n]
                sub = (n - OF["down"]) % 3 if kind == "down" else 0
                pe.wait_ge(landed[n % RING], 16 * (lay * (UNITS // RING) + n // RING + 1))
                if n == OF[kind] and kind in NEED:
                    need, count = NEED[kind]
                    pe.wait_ge(need.sem, need.at(lay, count))
                slot = ring[:, n % RING, :]
                if kind == "ple":
                    pe.wait_ge(ym_fin.sem, ym_fin.at(lay, 1))
                    w = slot.rearrange("p (k m) -> p k m", k=2)
                    pin = par[:, PAR["p"]:PAR["p"] + 512].rearrange("p (k s) -> p k s", k=2)
                    for c in range(KC):
                        for k in range(2):
                            mm = pe.matmul(A[c // 2][:, c % 2 * S:c % 2 * S + S], w[:, k, c * P:(c + 1) * P],
                                           pin[:, k, :], start=(k == 0), stop=(k == 1))
                    mm.then_inc(unit_done.sem, 1)
                    return
                use = USE[n]
                bank = G[use % GBANKS]
                if sub == 0 and (lay or use >= GBANKS):
                    f = freed[use % GBANKS]
                    pe.wait_ge(f.sem, f.at(lay, use // GBANKS))
                if n == OF["pleg"]:
                    pe.wait_ge(*evac(lay, last("down")))
                w = slot.rearrange("p (k m) -> p k m", k=KC)
                x = u if kind not in RHS else chunks(RHS[kind], KC)
                x = h if kind == "pleg" else x
                if kind == "rows":
                    for k in range(KC):
                        mm = pe.matmul(bank[0:96, 0:S], w[:, k, 0:96], u[:, k, :], start=(k == 0), stop=(k == KC - 1))
                elif kind == "down":
                    ks = min(KC, FC - KC * sub)
                    x = chunks(HID + KC * sub, ks)
                    for c in range(2):
                        for k in range(ks):
                            mm = pe.matmul(bank[:, c * S:(c + 1) * S], w[:, k, c * P:(c + 1) * P], x[:, k, :],
                                           start=(sub == 0 and c == 0 and k == 0), stop=(sub == 2 and k == ks - 1),
                                           skip_group_check=True)
                else:
                    for c in range(2):
                        for k in range(KC):
                            mm = pe.matmul(bank[:, c * S:(c + 1) * S], w[:, k, c * P:(c + 1) * P], x[:, k, :],
                                           start=(k == 0), stop=(k == KC - 1))
                mm.then_inc(unit_done.sem, 1)

            def turn(src, done, lay, wait):
                for q in range(4):
                    for c in range(4):
                        mm = pe.transpose(A[q][:, c * P:(c + 1) * P],
                                          src[:, q % 2 * 4 + c, q // 2 * P:(q // 2 + 1) * P], ident)
                    mm.then_inc(done.sem, 1)

            def item(kind, k, lay):
                if kind == "unit":
                    unit(lay, k)
                elif kind == "norm":
                    pe.wait_ge(sq_ready.sem, sq_ready.at(lay, k + 1))
                    for c in range(KC):
                        mm = pe.matmul(A[4][:, 0:S], ones, arena[:, SQ + c, :], start=(c == 0), stop=(c == KC - 1))
                    mm.then_inc(ss_ready.sem, 1)
                elif kind == "rows1":
                    pe.wait_ge(rows_ok.sem, rows_ok.at(lay, 1))
                    for i in range(T):
                        pe.transpose(A[3][:, i * P:i * P + 96], rows[0:96, i * P:(i + 1) * P], ident[0:96, 0:96])
                        mm = pe.transpose(A[3][:, i * P + 96:(i + 1) * P], dtr[0:32, i * P:(i + 1) * P], ident[0:32, 0:32])
                    mm.then_inc(rowsT.sem, 1)
                elif kind == "rows2":
                    pe.wait_ge(tok_ok.sem, tok_ok.at(lay, 1))
                    tri = ("fw", "bw")
                    for i in range(T):
                        for d, src, dst in ((0, 0, 0), (1, 16, 16), (0, 64, 32), (1, 72, 40)):
                            n = 16 if src < 64 else 8
                            for j in range(T):
                                mm = pe.matmul(A[2][:, i * 48 + dst:i * 48 + dst + n],
                                               cn(tri[d], j * S + i * P, j * S + (i + 1) * P),
                                               tok[:, j, src:src + n], start=(j == 0), stop=(j == T - 1))
                    mm.then_inc(cum_ok.sem, 1)
                    for d in range(2):
                        for j in range(T):
                            mm = pe.matmul(A[1][0:16, d * S:(d + 1) * S], tok[:, j, 16 * d:16 * d + 16],
                                           cn(tri[d], j * S, (j + 1) * S), start=(j == 0), stop=(j == T - 1))
                    mm.then_inc(cum_ok.sem, 1)
                    for d in range(2):
                        for j in range(T):
                            pe.matmul(A[0][0:8, d * S:(d + 1) * S], tok[:, j, 64 + 8 * d:72 + 8 * d],
                                      cn(tri[d], j * S, (j + 1) * S), start=(j == 0), stop=(j == T - 1))
                        for j in range(T):
                            mm = pe.matmul(A[4][0:8, d * S + j * P:d * S + (j + 1) * P],
                                           tok[:, j, 32 + 8 * d:40 + 8 * d], ident, start=True, stop=True)
                    mm.then_inc(cum_ok.sem, 1)
                elif kind == "rows3":
                    pe.wait_ge(em_ok.sem, em_ok.at(lay, 1))
                    for i in range(T):
                        for d in range(2):
                            mm = pe.transpose(A[3][:, (2 * i + d) * 8:(2 * i + d) * 8 + 8],
                                              mrow[0:8, 0, d, i * P:(i + 1) * P], ident[0:8, 0:8])
                    mm.then_inc(emT.sem, 1)
                elif kind == "xs_turn":
                    pe.wait_ge(xs_ok.sem, xs_ok.at(lay, 1))
                    pe.wait_ge(rows_fin.sem, rows_fin.at(lay, 1))
                    turn(chunks(XBC, KC), xT, lay, None)
                elif kind == "cb":
                    pe.wait_ge(xT_cp.sem, xT_cp.at(lay, 4))
                    for g in range(2):
                        for i in range(T):
                            mm = pe.matmul(A[g][:, i * S:(i + 1) * S], arena[:, XBC + 8 + g, i * P:(i + 1) * P],
                                           arena[:, XBC + 10 + g, :], start=True, stop=True)
                        mm.then_inc(cb_ok.sem, 1)
                elif kind == "bc":
                    if k < 2:
                        pe.wait_ge(cb_cp.sem, cb_cp.at(lay, k + 1))
                    else:
                        pe.wait_ge(arg_ok.sem, arg_ok.at(lay, k - 1))
                    pe.matmul(A[k % 2][:, :], ident[0:16, k:k + 1].broadcast_to([16, P]),
                              arow[0:16].rearrange("p d s -> p (d s)"), start=True, stop=True)\
                        .then_inc(bc_ok.sem, 1)
                elif kind == "y":
                    pe.wait_ge(att_ok.sem, att_ok.at(lay, k + 1))
                    j = k // 2
                    if k % 2 == 0 and j >= 2:
                        pe.wait_ge(y_cp.sem, y_cp.at(lay, j - 1))
                    r = k % 2 * 64
                    for i in range(T):
                        mm = pe.matmul(A[2 + j % 2][r:r + 64, 0:S], xtok[:, i, k * 64:(k + 1) * 64],
                                       arena[:, SW[k % 2] + i, :], start=(i == 0), stop=(i == T - 1))
                    mm.then_inc(y_ok.sem, 1)
                elif kind == "ssd_norm":
                    pe.wait_ge(ysq.sem, ysq.at(lay, 1))
                    for g in range(2):
                        for c in range(4):
                            mm = pe.matmul(A[0][:, g * S:(g + 1) * S], ones, arena[:, XBC + 4 * g + c, :],
                                           start=(c == 0), stop=(c == 3))
                    mm.then_inc(yss.sem, 1)
                elif kind == "hvt":
                    pe.wait_ge(yrs.sem, yrs.at(lay, 1))
                    pe.wait_ge(y_cp.sem, y_cp.at(lay, 8))
                    pe.wait_ge(*evac(lay, last("hi")))
                    turn(chunks(HV, KC), hvT, lay, None)
                elif kind == "hgB":
                    b, l = divmod(k, 9)
                    pe.wait_ge(hqk.sem, hqk.at(lay, k + 1))
                    if k >= 2:
                        pe.wait_ge(hcp.sem, hcp.at(lay, k - 1))
                    else:
                        pe.wait_ge(hvT_cp.sem, hvT_cp.at(lay, 4))
                    e = HE[k % 2]
                    for i in range(T):
                        j = 1 - i if l == 8 else i
                        for hd in range(4):
                            q = arena[:, HQ + 4 * b + hd if l == 0 else e + hd, j * P:(j + 1) * P]
                            mm = pe.matmul(A[k % 2 * 2 + i][:, hd * P:(hd + 1) * P],
                                           arena[:, e + 4 + hd, i * P:(i + 1) * P], q, start=True, stop=True)
                    mm.then_inc(hprod.sem, 1)
                elif kind == "ho":
                    pe.wait_ge(hcp.sem, hcp.at(lay, 9 * (k + 1)))
                    for pair in range(2):
                        n = 2 * k + pair
                        if n:
                            pe.wait_ge(ho_cp.sem, ho_cp.at(lay, n))
                        for a in range(2):
                            hd = 2 * pair + a
                            for i in range(T):
                                mm = pe.matmul(A[4][:, a * S:(a + 1) * S], hvtok[:, i, (4 * k + hd) * P:(4 * k + hd + 1) * P],
                                               hatt[:, i, hd, :], start=(i == 0), stop=(i == T - 1))
                        mm.then_inc(ho_ok.sem, 1)
                elif kind == "hnorm":
                    pe.wait_ge(hsq.sem, hsq.at(lay, 1))
                    for c in range(KC):
                        mm = pe.matmul(A[c // 2][:, c % 2 * S:c % 2 * S + S], ones, arena[:, HE[0] + c, :],
                                       start=True, stop=True)
                    mm.then_inc(hss.sem, 1)
                elif kind == "mvt":
                    pe.wait_ge(hrs.sem, hrs.at(lay, 1))
                    turn(chunks(MV, KC), mvT, lay, None)
                elif kind == "mlA":
                    if k < 2:
                        pe.wait_ge(mvT_cp.sem, mvT_cp.at(lay, 5))
                    else:
                        pe.wait_ge(marg.sem, marg.at(lay, k - 1))
                    pe.matmul(A[k % 2][:, :], ident[0:8, k:k + 1].broadcast_to([8, P]),
                              mrow[0:8, 3].rearrange("p d s -> p (d s)"), start=True, stop=True)\
                        .then_inc(mbc.sem, 1)
                elif kind == "mlB":
                    if k:
                        pe.wait_ge(matt.sem, matt.at(lay, k))
                    for i in range(T):
                        mm = pe.matmul(A[2][:, i * S:(i + 1) * S], arena[:, MK + k, i * P:(i + 1) * P],
                                       arena[:, MQ + k, :], start=True, stop=True)
                    mm.then_inc(mqk.sem, 1)
                elif kind == "mlC":
                    pe.wait_ge(matt.sem, matt.at(lay, k + 1))
                    if k:
                        pe.wait_ge(mh_cp.sem, mh_cp.at(lay, k))
                    w = flat(MA[k % 2], 3)
                    for t, d, parts in ((0, 0, ((0, 0),)), (0, 1, ((256, 0), (512, 1))),
                                        (1, 0, ((128, 0), (384, 1))), (1, 1, ((640, 1),))):
                        for n, (at, i) in enumerate(parts):
                            mm = pe.matmul(A[3 + t][:, d * 129:(d + 1) * 129], w[:, at:at + P], mvtok[:, i, k, :],
                                           start=(n == 0), stop=(n == len(parts) - 1))
                    mm.then_inc(mnum.sem, 1)
                elif kind == "mlturn":
                    pe.wait_ge(mhn.sem, mhn.at(lay, 1))
                    for q in range(4):
                        for a in range(2):
                            for i in range(T):
                                mm = pe.transpose(A[q][:, a * S + i * P:a * S + (i + 1) * P], hsum[:, i, 2 * q + a, :], ident)
                        mm.then_inc(mhT.sem, 1)

            def norm2(n):
                pe.wait_ge(sq_ready.sem, sq_ready.at(DEPTH, n))
                for c in range(KC):
                    mm = pe.matmul(A[4][:, 0:S], ones, arena[:, SQ + c, :], start=(c == 0), stop=(c == KC - 1))
                mm.then_inc(ss_ready.sem, 1)

            def gemm2(m, x):
                b, before = use2(m)
                pe.wait_ge(*landed2(m))
                pe.wait_ge(freed[b].sem, before)
                w = ring[:, m % RING, :].rearrange("p (k m) -> p k m", k=KC)
                for c in range(2):
                    for k in range(KC):
                        mm = pe.matmul(G[b][:, c * S:(c + 1) * S], w[:, k, c * P:(c + 1) * P], x[:, k, :],
                                       start=(k == 0), stop=(k == KC - 1))
                mm.then_inc(unit_done.sem, 1)

            pe.wait_ge(con_in, 16)
            for lay in range(n_layers):
                for kind, k in sched:
                    item(kind, k, lay)
            if not second:
                return
            norm2(1)
            pe.wait_ge(cs_ok, 1)
            for m in range(ADA_UNITS):
                pe.wait_ge(*landed2(m))
                w = ring[:, m % RING, :].rearrange("p (k m) -> p k m", k=KC)
                for c in range(2):
                    for k in range(KC):
                        mm = pe.matmul(A[2][:, 2 * m + c:2 * m + c + 1], w[:, k, c * P:(c + 1) * P],
                                       mod[:, 64 + k:65 + k], start=(k == 0), stop=(k == KC - 1))
                mm.then_inc(unit_done.sem, 1)
            pe.wait_ge(lam_in, 1)
            pe.matmul(A[3][:, 0:2], con[0:64, CON["ones"]:CON["ones"] + P], small[0:64, 0:2], start=True, stop=True)\
                .then_inc(lam_mm, 1)
            norm2(2)
            if upto == "ada":
                return
            pe.wait_ge(u_ready.sem, u_ready.at(DEPTH, 2))
            for m in range(WIN2, WOUT2):
                gemm2(m, u)
            for q in range(4):
                b, before = use2(WIN2 + q)
                pe.wait_ge(freed[b].sem, before + 1)
                for c in range(2):
                    mm = pe.matmul(A[q][:, c * S:(c + 1) * S], c2("rot", 0, P), arena[:, Q2 + 2 * q + c, :],
                                   start=True, stop=True)
                mm.then_inc(rope_mm, 1)
            for q in range(2):
                b, before = use2(WIN2 + 4 + q)
                pe.wait_ge(freed[b].sem, before + 1)
            pe.wait_ge(rope_ok, 2)
            for i in range(T):
                for c in range(4):
                    mm = pe.transpose(A[i][:, c * P:(c + 1) * P], arena[:, V2 + c, i * P:(i + 1) * P], ident)
                mm.then_inc(v2T, 1)

            def scores(hd):
                if hd < 2:
                    pe.wait_ge(rope_ok, 4)
                    pe.wait_ge(v2T_cp, 2)
                else:
                    pe.wait_ge(sc_exp, 4 * (hd - 1))
                for i in range(T):
                    for c in range(2):
                        r = slice(64 * c, 64 * c + 64)
                        mm = pe.matmul(A[hd % 2 * 2 + c][:, i * S:(i + 1) * S], arena[r, Q2 + hd, i * P:(i + 1) * P],
                                       arena[r, K2 + hd, :], start=True, stop=True)
                mm.then_inc(sc_ok, 1)

            def values(hd):
                pe.wait_ge(w2_ok, hd + 1)
                if hd:
                    pe.wait_ge(w2T_cp, hd)
                for j in range(T):
                    for i in range(T):
                        mm = pe.transpose(A[4][:, j * S + i * P:j * S + (i + 1) * P],
                                          arena[:, WA[hd % 2] + i, j * P:(j + 1) * P], ident)
                mm.then_inc(w2T, 1)
                pe.wait_ge(w2T_cp, hd + 1)
                for j in range(T):
                    mm = pe.matmul(G[hd // 2][:, hd % 2 * S:hd % 2 * S + S], v2tok[:, j, hd * P:(hd + 1) * P],
                                   arena[:, WAT[hd % 2] + j, :], start=(j == 0), stop=(j == T - 1))
                mm.then_inc(o2_ok, 1)

            scores(0)
            scores(1)
            pe.wait_ge(pool_d, 1)
            b, before = use2(WOUT2 - 1)
            pe.wait_ge(freed[2].sem, DEPTH * USES_PER_BANK + 2)
            for g in range(4):
                if g == 2:
                    pe.wait_ge(pool_fin, 1)
                mm = pe.matmul(G[2][:, g % 2 * S:g % 2 * S + S], p2("w_pool", g * P, P), arena[:, RD + g, :],
                               start=True, stop=True)
                if g % 2:
                    mm.then_inc(pool_mm, 1)
            for hd in range(HEADS2):
                values(hd)
                if hd + 2 < HEADS2:
                    scores(hd + 2)
            pe.wait_ge(o2_sq, 1)
            for hd in range(HEADS2):
                mm = pe.matmul(A[hd // 2][:, hd % 2 * S:hd % 2 * S + S], ones, arena[:, SQ + hd, :], start=True, stop=True)
            mm.then_inc(o2_ss, 1)
            pe.wait_ge(o2_fin, 1)
            pe.wait_ge(pool_fin, 2)
            for m in range(WOUT2, ROUTER):
                gemm2(m, chunks(O2, KC))
            norm2(3)
            if upto == "attn":
                return
            pe.wait_ge(u_ready.sem, u_ready.at(DEPTH, 3))
            pe.wait_ge(*landed2(ROUTER))
            w = ring[:, ROUTER % RING, :].rearrange("p (k m) -> p k m", k=KC)
            for i in range(T):
                o = A[0][:, i * 64:i * 64 + 36]
                for k in range(KC):
                    pe.matmul(o, u[:, k, i * P:(i + 1) * P], w[:, k, 0:36], start=(k == 0), stop=False)
                mm = pe.matmul(o, con[0:1, CON["ones"]:CON["ones"] + P], p2("b_route", 0, 36)[0:1], start=False, stop=True)
            mm.then_inc(unit_done.sem, 1)

            def moe_units(first, e_gate, e_down, start):
                six, rest = first
                n = 0
                for j in range(4) if e_gate is not None else ():
                    at = B2 + MOE + rest + n
                    pe.wait_ge(landed[at % RING], (six * 2 + (at // RING + 1)) * 16)
                    if j < 3:
                        pe.wait_ge(freed[j].sem, e_gate + G2)
                    elif not isinstance(e_gate, int) or e_gate:
                        pe.wait_ge(e4_freed, e_gate)
                    w = ring[:, at % RING, :].rearrange("p (k m) -> p k m", k=KC)
                    for c in range(2):
                        for k in range(KC):
                            mm = pe.matmul(E4[j][:, c * S:(c + 1) * S], w[:, k, c * P:(c + 1) * P], u[:, k, :],
                                           start=(k == 0), stop=(k == KC - 1))
                    mm.then_inc(unit_done.sem, 1)
                    n += 1
                if e_down is None:
                    return
                e, par_e = e_down
                pe.wait_ge(hide_ok, (e + 1) * 4)
                for j in range(2):
                    at = B2 + MOE + rest + n
                    pe.wait_ge(landed[at % RING], (six * 2 + (at // RING + 1)) * 16)
                    w = ring[:, at % RING, :].rearrange("p (k m) -> p k m", k=4)
                    for c in range(4):
                        ch = 4 * j + c
                        for k in range(4):
                            mm = pe.matmul(A[ch // 2][:, ch % 2 * S:ch % 2 * S + S], w[:, k, c * P:(c + 1) * P],
                                           arena[:, HIDE[par_e] + k, :], start=(start and ch % 2 == 0 and k == 0),
                                           stop=False, skip_group_check=True)
                    mm.then_inc(unit_done.sem, 1)
                    n += 1

            moe_units((0, 0), 0, None, False)
            pe.wait_ge(r_w, 1)
            for i in range(T):
                mm = pe.transpose(A[1][0:32, i * P:(i + 1) * P], small[:, 128 + 32 * i:160 + 32 * i], ident)
            mm.then_inc(r_T, 1)
            pe.wait_ge(r_wT, 1)
            for q in range(EXPERTS // 2):
                if q >= 4:
                    pe.wait_ge(wb_cp, q - 3)
                for a in range(2):
                    e = 2 * q + a
                    mm = pe.matmul(A[q % 4][:, a * S:(a + 1) * S], ident[0:32, e:e + 1].broadcast_to([32, P]),
                                   rowt[:, :], start=True, stop=True)
                mm.then_inc(wb_mm, 1)
            pe.wait_ge(wb_cp, EXPERTS // 2)
            moe_units((0, 4), 1, (0, 0), True)
            with pe.Fori(0, (EXPERTS - 2) // 2) as i:
                for a in range(2):
                    moe_units((i * 2 + a, 10), i * 2 + (a + 2), (i * 2 + (a + 1), (a + 1) % 2), False)
            moe_units((0, UNITS2 - MOE - 2), None, (EXPERTS - 1, 1), False)
            pe.transpose(G[0][0:32, 0:P], small[:, 128:160], ident).then_inc(y2_ok, 1)
            norm2(4)

        @block.scalar
        def _(act):
            st = Steps(act, act_step)

            def unit(lay, n):
                kind, j = KINDS[n], n - OF[KINDS[n]]
                j = j // 2 if kind in ("gs", "bs") else j
                if kind in ("bs", "bh", "bm", "out", "down"):
                    return
                act.wait_ge(unit_done.sem, unit_done.at(lay, n + 1))
                if kind == "ple":
                    for q in range(4):
                        a = act.activation(flat(PLE + 2 * q, 2), A[q][:, :], ACT.Copy)
                    a.then_inc(ple_cp.sem, 1)
                    return
                bank, f = G[USE[n] % GBANKS], freed[USE[n] % GBANKS]
                if kind == "rows":
                    act.activation(rows[:, :], bank[0:96, 0:S], ACT.Identity, bias=pc("row_b")[0:96]).then_inc(f.sem, 1)
                elif kind in ("xbc", "up"):
                    conv = kind == "xbc"
                    if not conv and j >= 2:
                        act.wait_ge(hid_ok.sem, hid_ok.at(lay, j - 1))
                    for c in range(2):
                        if conv:
                            ch, width, wn, bn, dst = 2 * j + c, SSD_CONV, "conv_w", "conv_b", XBC + 2 * j + c
                        else:
                            ch, width, wn, bn, dst = j + FC * c, FFN_CONV, "fconv_w", "fconv_b", FT[j % 2] + c
                        a = act.activation(arena[:, dst, :], bank[:, c * S:(c + 1) * S], ACT.Identity,
                                           scale=pc(wn, ch * width + width // 2), bias=pc(bn, ch))
                    a.then_inc(center.sem, 1)
                else:
                    dst = {"z": Z, "hf": HF, "hq": HQ, "hi": HV, "hg": HG, "mq": MQ, "mk": MK, "mv": MV, "mo": MO,
                           "gs": GS, "gh": GH, "gm": GM, "pleg": PLG}[kind]
                    func = {"z": ACT.Silu, "gs": ACT.Sigmoid, "gh": ACT.Sigmoid, "gm": ACT.Sigmoid,
                            "pleg": ACT.Sigmoid}.get(kind, ACT.Copy)
                    if kind == "gs":
                        if j:
                            act.wait_ge(*evac(lay, n - 1))
                        at = GS
                    else:
                        at = dst + 2 * j
                    if kind == "mo" and j == 0:
                        act.wait_ge(ys_fin.sem, ys_fin.at(lay, 1))
                    act.activation(flat(at, 2), bank[:, :], func).then_inc(f.sem, 1)

            def rstd_of(src, log, outp, n, ready):
                st.done(act.activation(log, src, ACT.Ln, scale=1.0 / n, bias=eps[:, 0:1]))
                st.wait()
                act.activation(outp, log, ACT.Exp, scale=-0.5).then_inc(ready.sem, 1)

            def item(kind, k, lay):
                if kind == "unit":
                    unit(lay, k)
                elif kind == "norm":
                    if k == 0:
                        if lay:
                            act.wait_ge(h_fin.sem, h_fin.at(lay, 0))
                        else:
                            act.wait_ge(x_in, 16)
                    else:
                        act.wait_ge(*evac(lay, last("out")))
                    act.activation(flat(SQ, KC), h[:].rearrange("p c s -> p (c s)"), ACT.Square).then_inc(sq_ready.sem, 1)
                    act.wait_ge(ss_ready.sem, ss_ready.at(lay, k + 1))
                    rstd_of(A[4][:, 0:S], rstd[:, 0, 0, :], rstd[:, 1, 0, :], D, rs_ready)
                elif kind == "lb":
                    act.wait_ge(par_in, 16 * (lay + 1))
                    act.activation(nega[:, 0:1], pc("a_log")[0:32], ACT.Exp).then_inc(nega_exp.sem, 1)
                    act.wait_ge(lb_in.sem, lb_in.at(lay, 1))
                    act.activation(small[:, 48:80], small[:, 16:48], ACT.Exp).then_inc(lb_exp.sem, 1)
                elif kind == "rows":
                    act.wait_ge(sp_abs.sem, sp_abs.at(lay, 1))
                    st.done(act.activation(rtmp[:, 1, :], rtmp[:, 0, :], ACT.Exp, scale=-1.0))
                    st.wait()
                    act.activation(rtmp[:, 0, :], rtmp[:, 1, :], ACT.Ln, bias=1.0).then_inc(sp_ln.sem, 1)
                elif kind == "rows2":
                    act.wait_ge(m_ok.sem, m_ok.at(lay, 1))
                    act.activation(mrow[0:8, 0], mrow[0:8, 1], ACT.Exp, scale=-1.0).then_inc(em_ok.sem, 1)
                elif kind == "silu_x":
                    act.wait_ge(*evac(lay, last("xbc")))
                    act.activation(flat(XBC, 12), flat(XBC, 12), ACT.Silu).then_inc(xs_ok.sem, 1)
                elif kind == "bc":
                    act.wait_ge(arg_ok.sem, arg_ok.at(lay, k + 1))
                    act.activation(flat(SE[k % 2], 3), flat(SE[k % 2], 3), ACT.Exp).then_inc(exp_ok.sem, 1)
                elif kind == "hprep":
                    act.wait_ge(*evac(lay, last("hg")))
                    st.done(act.activation(flat(HK, 16), flat(HF, 16), ACT.Sigmoid, scale=-1.0))
                    st.wait()
                    act.activation(flat(HF, 16), flat(HF, 16), ACT.Sigmoid).then_inc(hsig.sem, 1)
                    act.activation(flat(HQ, KC), flat(HQ, KC), ACT.Silu)
                    act.activation(flat(HG, KC), flat(HG, KC), ACT.Silu).then_inc(hsilu.sem, 1)
                elif kind == "ssd_norm":
                    act.wait_ge(yz_ok.sem, yz_ok.at(lay, 1))
                    act.activation(flat(XBC, KC), flat(Z, KC), ACT.Square).then_inc(ysq.sem, 1)
                    act.wait_ge(yss.sem, yss.at(lay, 1))
                    rstd_of(A[0][:, :], rstd[:, 0].rearrange("p a s -> p (a s)"),
                            rstd[:, 1].rearrange("p a s -> p (a s)"), D // 2, yrs)
                elif kind == "hlog":
                    act.wait_ge(hclamp.sem, hclamp.at(lay, 1))
                    act.activation(flat(HF, 16), flat(HF, 16), ACT.Ln)
                    act.activation(flat(HE[0], 16), flat(HE[0], 16), ACT.Ln, scale=1.0 / LN_FLOOR).then_inc(hln.sem, 1)
                elif kind == "hgA":
                    b, l = divmod(k, 9)
                    if l == 0:
                        return
                    act.wait_ge(hargs.sem, hargs.at(lay, 8 * b + l))
                    m = 1 << (l - 1)
                    e = HE[k % 2]
                    act.activation(half(flat(e, 4), m, 1), half(flat(HF + 4 * b, 4), m, 1), ACT.Exp)
                    act.activation(half(flat(e, 4), m, 0), half(flat(HF + 8 + 4 * b, 4), m, 0), ACT.Exp)
                    act.activation(flat(e + 4, 4), flat(e + 4, 4), ACT.Exp).then_inc(hexp.sem, 1)
                elif kind == "ho":
                    for n in (2 * k, 2 * k + 1):
                        act.wait_ge(ho_ok.sem, ho_ok.at(lay, n + 1))
                        act.activation(flat(HQ + 2 * n, 2), A[4][:, :], ACT.Copy).then_inc(ho_cp.sem, 1)
                elif kind == "hnorm":
                    act.wait_ge(ho_cp.sem, ho_cp.at(lay, 4))
                    act.activation(flat(HE[0], KC), flat(HQ, KC), ACT.Square).then_inc(hsq.sem, 1)
                    act.wait_ge(hss.sem, hss.at(lay, 1))
                    for q in range(4):
                        a = act.activation(flat(HE[1] + 2 * q, 2), A[q][:, :], ACT.Ln, scale=1.0 / P, bias=eps[:, 0:1])
                    st.done(a)
                    st.wait()
                    act.activation(flat(HE[1], KC), flat(HE[1], KC), ACT.Exp, scale=-0.5).then_inc(hrs.sem, 1)
                elif kind == "mvt":
                    act.wait_ge(*evac(lay, last("mo")))
                    act.activation(flat(MO, KC), flat(MO, KC), ACT.Sigmoid).then_inc(msig.sem, 1)
                elif kind == "mlA":
                    act.wait_ge(marg.sem, marg.at(lay, k + 1))
                    act.activation(flat(ME[k % 2], 3), flat(ME[k % 2], 3), ACT.Exp).then_inc(mexp.sem, 1)
                elif kind == "mlnorm":
                    act.wait_ge(mcen.sem, mcen.at(lay, 1))
                    act.activation(flat(SQ, KC), flat(HSUM, KC), ACT.Square).then_inc(msq.sem, 1)
                    act.wait_ge(mvar.sem, mvar.at(lay, 1))
                    rstd_of(small[:, 16:32], small[:, 32:48], small[:, 48:64], P, mrs)
                elif kind == "hid":
                    act.wait_ge(*evac(lay, OF["up"] + k))
                    act.activation(arena[:, FT[k % 2], :], arena[:, FT[k % 2], :], ACT.Silu).then_inc(silu_ok.sem, 1)

            def norm2(n):
                act.activation(flat(SQ, KC), h[:].rearrange("p c s -> p (c s)"), ACT.Square).then_inc(sq_ready.sem, 1)
                act.wait_ge(ss_ready.sem, ss_ready.at(DEPTH, n))
                rstd_of(A[4][:, 0:S], rstd[:, 0, 0, :], rstd[:, 1, 0, :], D, rs_ready)

            act.wait_ge(eps_set, 1)
            for lay in range(n_layers):
                for kind, k in sched:
                    item(kind, k, lay)
            if not second:
                return
            act.wait_ge(h_fin.sem, h_fin.at(DEPTH, 0))
            norm2(1)
            act.wait_ge(par2_in, 32)
            act.activation(mod[:, 64:72], p2("c", 0, 8), ACT.Silu).then_inc(cs_ok, 1)
            act.wait_ge(lam_mm, 1)
            act.activation(small[:, 2:4], A[3][:, 0:2], ACT.Exp).then_inc(lam_exp, 1)
            act.wait_ge(u_ready.sem, u_ready.at(DEPTH, 1))
            norm2(2)
            if upto == "ada":
                return
            for m in range(WIN2, WOUT2):
                act.wait_ge(*done2(m))
                b, before = use2(m)
                act.activation(flat(Q2 + 2 * (m - WIN2), 2), G[b][:, :], ACT.Copy).then_inc(freed[b].sem, 1)

            def exps(hd):
                act.wait_ge(sc_max, hd + 1)
                for i in range(T):
                    for c in range(2):
                        n = 4 * (hd % 2) + 2 * c + i
                        act.activation(arena[:, EA[hd % 2] + 2 * c + i, :], A[hd % 2 * 2 + c][:, i * S:(i + 1) * S], ACT.Exp,
                                       scale=HD2 ** -0.5, bias=small[:, 8 + n:9 + n],
                                       accum_out=small[:, 16 + n:17 + n]).then_inc(sc_exp, 1)

            for hd in range(HEADS2):
                if hd >= 2:
                    act.wait_ge(w2_ok, hd - 1)
                exps(hd)
            for n in range(2):
                act.wait_ge(o2_ok, 2 * n + 2)
                st.done(act.activation(flat(O2 + 2 * n, 2), G[n][:, :], ACT.Copy))
            st.wait()
            act.activation(flat(SQ, 4), flat(O2, 4), ACT.Square).then_inc(o2_sq, 1)
            act.wait_ge(o2_ss, 1)
            for n in range(2):
                a = act.activation(flat(RD + 2 * n, 2), A[n][:, :], ACT.Ln, scale=1.0 / P, bias=eps[:, 0:1])
            st.done(a)
            st.wait()
            act.activation(flat(RD, 4), flat(RD, 4), ACT.Exp, scale=-0.5).then_inc(o2_rs, 1)
            act.wait_ge(freed[2].sem, DEPTH * USES_PER_BANK + 4)
            norm2(3)
            if upto == "attn":
                return
            act.wait_ge(r_sh, 1)
            act.activation(small[:, 8:16], small[:, 0:8], ACT.Exp).then_inc(r_exp, 1)
            act.wait_ge(r_sh, 2)
            act.activation(small[:, 18:20], small[:, 16:18], ACT.Exp).then_inc(r_exp, 1)

            for j in range(4):
                act.wait_ge(*done2(MOE + j))
                act.activation(arena[:, SG2 + j, :], E4[j][:, 0:S], ACT.Silu).then_inc(gate_ok, 1)
            with act.Fori(0, EXPERTS - 1) as e:
                for j in range(4):
                    act.wait_ge(unit_done.sem, e * 6 + (B2 + MOE + 4 + j + 1))
                    act.wait_ge(hide_ok, e * 4 + (j + 1))
                    act.activation(arena[:, SG2 + j, :], E4[j][:, 0:S], ACT.Silu).then_inc(gate_ok, 1)
            act.wait_ge(y2_fin, 1)
            norm2(4)

        @block.vector
        def _(dve):
            st = Steps(dve, dve_step)
            V = nc.vector
            stt, tt, ts = V.scalar_tensor_tensor, V.tensor_tensor, V.tensor_scalar

            def taps(lay, n, width, wn, chans, dsts):
                bank, f = G[USE[n] % GBANKS], freed[USE[n] % GBANKS]
                offs = [j for j in range(width) if j != width // 2]
                for a, j in enumerate(offs):
                    d = j - width // 2
                    lo, hi = max(0, -d), S - max(0, d)
                    for c in range(2):
                        if a:
                            st.wait(back=1)
                        o = arena[:, dsts[c], lo:hi]
                        ins = stt(o, bank[:, c * S + lo + d:c * S + hi + d], pc(wn, chans[c] * width + j), o,
                                  ALU.mult, ALU.add)
                        if j == offs[-1] and c == 1:
                            st.wait()
                            ins.then_inc(f.sem, 1)
                        else:
                            st.done(ins)

            def unit(lay, n):
                kind, j = KINDS[n], n - OF[KINDS[n]]
                j = j // 2 if kind in ("gs", "bs") else j
                if kind not in ("bs", "bh", "bm", "out", "down", "xbc", "up"):
                    return
                if kind == "down" and j % 3 != 2:
                    return
                if kind == "xbc":
                    dve.wait_ge(center.sem, center.at(lay, j + 1))
                    taps(lay, n, SSD_CONV, "conv_w", (2 * j, 2 * j + 1), (XBC + 2 * j, XBC + 2 * j + 1))
                    return
                if kind == "up":
                    dve.wait_ge(center.sem, center.at(lay, 6 + j + 1))
                    taps(lay, n, FFN_CONV, "fconv_w", (j, j + FC), (FT[j % 2], FT[j % 2] + 1))
                    return
                dve.wait_ge(unit_done.sem, unit_done.at(lay, n + 1))
                bank, f = G[USE[n] % GBANKS], freed[USE[n] % GBANKS]
                if kind in ("out", "down"):
                    j = j // 3 if kind == "down" else j
                    o = h[:, 2 * j:2 * j + 2, :].rearrange("p c s -> p (c s)")
                    tt(o, bank[:, :], o, ALU.add).then_inc(f.sem, 1)
                elif kind == "bs":
                    dve.wait_ge(*evac(lay, n - 1))
                    tt(flat(MERGED + 2 * j, 2), bank[:, :], flat(GS, 2), ALU.mult).then_inc(f.sem, 1)
                else:
                    g = {"bh": GH, "bm": GM}[kind] + 2 * j
                    if j == 0:
                        dve.wait_ge(*evac(lay, last("gm")))
                    tt(flat(g, 2), bank[:, :], flat(g, 2), ALU.mult).then_inc(f.sem, 1)
                    dve.wait_ge(*evac(lay, n))
                    m = flat(MERGED + 2 * j, 2)
                    ins = tt(m, m, flat(g, 2), ALU.add)
                    if kind == "bm" and j == 3:
                        st.wait()
                        ins.then_inc(merge_ok.sem, 1)
                    else:
                        st.done(ins)

            def decay_args(k, lay, e, bank, col, ready):
                w = flat(e, 3)
                for i, d, lo, hi, at, mask in ((0, 0, 0, 256, 0, cn("mf", 0, 256)), (0, 1, 0, 128, 256, cn("mb", 128, 256)),
                                               (1, 0, 128, 256, 384, cn("mf", 0, 128)), (1, 1, 0, 256, 512, cn("mb", 0, 256))):
                    ins = stt(w[:, at:at + hi - lo], bank[:, d * S + lo:d * S + hi], ntok[:, i, col(d):col(d) + 1], mask,
                              ALU.add, ALU.min)
                ins.then_inc(ready.sem, 1)

            def item(kind, k, lay):
                if kind == "unit":
                    unit(lay, k)
                elif kind == "norm":
                    dve.wait_ge(rs_ready.sem, rs_ready.at(lay, k + 1))
                    if k == 0:
                        dve.wait_ge(par_in, 16 * (lay + 1))
                    for c in range(KC):
                        ins = stt(u[:, c, :], h[:, c, :], pc(("mix_g", "ffn_g")[k], c), rstd[:, 1, 0, :], ALU.mult, ALU.mult)
                    ins.then_inc(u_ready.sem, 1)
                elif kind == "lb":
                    raw = [par[:, PAR["lb_raw"] + 16 * i:PAR["lb_raw"] + 16 * i + 16] for i in range(DEPTH)]
                    st.done(tt(small[:, 0:16], raw[0], raw[1], ALU.max))
                    st.wait()
                    st.done(tt(small[:, 16:32], raw[0], small[:, 0:16], ALU.subtract))
                    st.wait()
                    tt(small[:, 32:48], raw[1], small[:, 0:16], ALU.subtract).then_inc(lb_in.sem, 1)
                    dve.wait_ge(lb_exp.sem, lb_exp.at(lay, 1))
                    st.done(tt(small[:, 80:96], small[:, 48:64], small[:, 64:80], ALU.add))
                    st.wait()
                    st.done(V.reciprocal(small[:, 96:112], small[:, 80:96]))
                    st.wait()
                    st.done(tt(small[:, 112:128], small[:, 48:64], small[:, 96:112], ALU.mult))
                    st.done(tt(small[:, 128:144], small[:, 64:80], small[:, 96:112], ALU.mult))
                    st.wait()
                    st.done(stt(lb[:, 2, :], small[:, 112:128], pc("lb_mask", 0), small[:, 112:128], ALU.mult, ALU.subtract))
                    st.wait()
                    st.done(stt(lb[:, 0, :], small[:, 128:144], pc("lb_mask", 1), lb[:, 2, :], ALU.mult, ALU.add))
                    st.wait()
                    st.done(ts(lb[:, 1, :], lb[:, 0, :], -1.0, 1.0, ALU.mult, ALU.add))
                    dve.wait_ge(nega_exp.sem, nega_exp.at(lay, 1))
                    st.done(ts(nega[:, 1:2], nega[:, 0:1], -1.0, None, ALU.mult))
                elif kind == "rows":
                    dve.wait_ge(*evac(lay, 0))
                    stt(rtmp[:, 0, :], rows[:, :], -1.0, rows[:, :], ALU.mult, ALU.max).then_inc(sp_abs.sem, 1)
                    dve.wait_ge(sp_ln.sem, sp_ln.at(lay, 1))
                    st.done(stt(dtr[:, :], rows[0:32, :], 0.0, rtmp[0:32, 0, :], ALU.max, ALU.add))
                    st.wait()
                    st.done(ts(rows[0:32, :], dtr[:, :], nega[:, 1:2], None, ALU.mult))
                    st.wait()
                    stt(rows[64:80, :], rows[64:80, :], 0.0, rtmp[64:80, 0, :], ALU.min, ALU.subtract)\
                        .then_inc(rows_ok.sem, 1)
                elif kind == "rows1":
                    dve.wait_ge(rowsT.sem, rowsT.at(lay, 1))
                    V.tensor_copy(tok[:].rearrange("p i n -> p (i n)"), A[3][:, 0:2 * P]).then_inc(tok_ok.sem, 1)
                elif kind == "rows2":
                    dve.wait_ge(tok_ok.sem, tok_ok.at(lay, 1))
                    dve.wait_ge(cum_ok.sem, cum_ok.at(lay, 1))
                    sums = A[2][:, 0:96].rearrange("p (i n) -> p i n", i=T)
                    st.done(ts(ntok[:, :, 0:32], sums[:, :, 0:32], -1.0, None, ALU.mult))
                    st.done(tt(ntok[:, :, 32:48], tok[:, :, 32:48], sums[:, :, 32:48], ALU.subtract))
                    dve.wait_ge(cum_ok.sem, cum_ok.at(lay, 2))
                    st.done(V.tensor_copy(arow[:].rearrange("p d s -> p (d s)"), A[1][0:16, :]))
                    dve.wait_ge(cum_ok.sem, cum_ok.at(lay, 3))
                    r = [mrow[0:8, i].rearrange("p d s -> p (d s)") for i in range(4)]
                    st.done(V.tensor_copy(r[0], A[0][0:8, :]))
                    st.wait()
                    st.done(tt(r[1], A[4][0:8, :], r[0], ALU.subtract))
                    st.wait()
                    f, b, o, ob = mrow[0:8, 1, 0, :], mrow[0:8, 1, 1, ::-1], mrow[0:8, 2, 0, :], mrow[0:8, 2, 1, ::-1]
                    st.done(V.tensor_tensor_scan(o, f, f, NEG, ALU.max, ALU.bypass))
                    st.done(V.tensor_tensor_scan(ob, b, b, NEG, ALU.max, ALU.bypass))
                    st.wait()
                    st.done(ts(r[3], r[2], -1.0, None, ALU.mult))
                    tt(r[1], r[0], r[2], ALU.add).then_inc(m_ok.sem, 1)
                elif kind == "rows3":
                    dve.wait_ge(emT.sem, emT.at(lay, 1))
                    st.wait()
                    V.tensor_copy(etok[:].rearrange("p i d n -> p (i d n)"), A[3][:, 0:32]).then_inc(rows_fin.sem, 1)
                elif kind == "xs_turn":
                    for q in range(4):
                        dve.wait_ge(xT.sem, xT.at(lay, q + 1))
                        V.tensor_copy(xtok[:, q // 2, q % 2 * 512:q % 2 * 512 + 512], A[q][:, :]).then_inc(xT_cp.sem, 1)
                elif kind == "cb":
                    for g in range(2):
                        dve.wait_ge(cb_ok.sem, cb_ok.at(lay, g + 1))
                        V.tensor_copy(flat(CB + 2 * g, 2), A[g][:, :]).then_inc(cb_cp.sem, 1)
                elif kind == "bc":
                    if k == 0:
                        st.wait()
                        dve.wait_ge(rows_fin.sem, rows_fin.at(lay, 1))
                    if k >= 2:
                        dve.wait_ge(att_ok.sem, att_ok.at(lay, k - 1))
                    dve.wait_ge(bc_ok.sem, bc_ok.at(lay, k + 1))
                    decay_args(k, lay, SE[k % 2], A[k % 2], lambda d: 16 * d + k, arg_ok)
                elif kind == "seg":
                    dve.wait_ge(exp_ok.sem, exp_ok.at(lay, k + 1))
                    if k == 0:
                        dve.wait_ge(cb_cp.sem, cb_cp.at(lay, 2))
                    if k >= 2:
                        dve.wait_ge(y_ok.sem, y_ok.at(lay, k - 1))
                    g = k // 8
                    e, w = flat(SE[k % 2], 3), SW[k % 2]
                    dt = [[tok[:, i, 96 + 16 * d + k:97 + 16 * d + k] for d in range(2)] for i in range(T)]
                    c0, c1 = arena[:, CB + 2 * g, :], arena[:, CB + 2 * g + 1, :]
                    w0, w1 = arena[:, w, :], arena[:, w + 1, :]
                    stt(w0, e[:, 0:256], dt[0][0], c0, ALU.mult, ALU.mult)
                    stt(w1, e[:, 512:768], dt[1][1], c1, ALU.mult, ALU.mult)
                    stt(e[:, 256:384], e[:, 256:384], dt[0][1], c0[:, 0:P], ALU.mult, ALU.mult)
                    st.done(stt(e[:, 384:512], e[:, 384:512], dt[1][0], c1[:, P:S], ALU.mult, ALU.mult))
                    st.wait()
                    tt(w0[:, 0:P], w0[:, 0:P], e[:, 256:384], ALU.add)
                    tt(w1[:, P:S], w1[:, P:S], e[:, 384:512], ALU.add).then_inc(att_ok.sem, 1)
                elif kind == "y":
                    if k % 2 == 0:
                        return
                    j = k // 2
                    dve.wait_ge(y_ok.sem, y_ok.at(lay, k + 1))
                    stt(arena[:, XBC + j, :], arena[:, XBC + j, :], pc("ssd_d", j), A[2 + j % 2][:, 0:S],
                        ALU.mult, ALU.add).then_inc(y_cp.sem, 1)
                    dve.wait_ge(y_cp.sem, y_cp.at(lay, j + 1))
                    ins = tt(arena[:, Z + j, :], arena[:, Z + j, :], arena[:, XBC + j, :], ALU.mult)
                    if k == SSD_H - 1:
                        ins.then_inc(yz_ok.sem, 1)
                elif kind == "ssd_norm":
                    dve.wait_ge(yrs.sem, yrs.at(lay, 1))
                    for c in range(KC):
                        ins = stt(arena[:, Z + c, :], arena[:, Z + c, :], pc("ssd_g", c), rstd[:, 1, c // 4, :],
                                  ALU.mult, ALU.mult)
                    ins.then_inc(ys_fin.sem, 1)
                elif kind == "hclamp":
                    dve.wait_ge(hsig.sem, hsig.at(lay, 1))
                    for c in range(16):
                        ts(arena[:, HK + c, :], arena[:, HK + c, :], lb[:, 1, c:c + 1], None, ALU.mult)
                        ins = ts(arena[:, HF + c, :], arena[:, HF + c, :], lb[:, 1, c:c + 1], lb[:, 0, c:c + 1],
                                 ALU.mult, ALU.add)
                    st.done(ins)
                    st.wait()
                    st.done(ts(flat(HE[0], 16), flat(HF, 16), TINY, LN_FLOOR, ALU.max, ALU.min))
                    st.wait()
                    ts(flat(HF, 16), flat(HF, 16), LN_FLOOR, None, ALU.max).then_inc(hclamp.sem, 1)
                elif kind == "hvt":
                    for q in range(4):
                        dve.wait_ge(hvT.sem, hvT.at(lay, q + 1))
                        V.tensor_copy(hvtok[:, q // 2, q % 2 * 512:q % 2 * 512 + 512], A[q][:, :]).then_inc(hvT_cp.sem, 1)
                elif kind == "hlog":
                    dve.wait_ge(hln.sem, hln.at(lay, 1))
                    st.done(tt(flat(HF, 16), flat(HF, 16), flat(HE[0], 16), ALU.add))
                    st.wait()
                elif kind == "hgA":
                    b, l = divmod(k, 9)
                    e = HE[k % 2]
                    pf, sbw = flat(HF + 4 * b, 4), flat(HF + 8 + 4 * b, 4)
                    if k >= 2:
                        dve.wait_ge(hprod.sem, hprod.at(lay, k - 1))
                    if l == 0:
                        return
                    m = 1 << (l - 1)
                    n = 4 * S // (2 * m)
                    if l >= 2:
                        dve.wait_ge(hexp.sem, hexp.at(lay, 8 * b + l - 1))
                        q = m // 2
                        st.done(tt(half(pf, q, 1), half(pf, q, 1), half(pf, q, 0)[:, :, q - 1:q].broadcast_to([P, 2 * n, q]), ALU.add))
                        st.done(tt(half(sbw, q, 0), half(sbw, q, 0), half(sbw, q, 1)[:, :, 0:1].broadcast_to([P, 2 * n, q]), ALU.add))
                        st.wait()
                    ek = flat(e + 4, 4)
                    tt(half(ek, m, 0), half(pf, m, 0)[:, :, m - 1:m].broadcast_to([P, n, m]), half(pf, m, 0), ALU.subtract)
                    tt(half(ek, m, 1), half(sbw, m, 1)[:, :, 0:1].broadcast_to([P, n, m]), half(sbw, m, 1), ALU.subtract)\
                        .then_inc(hargs.sem, 1)
                elif kind == "hgB":
                    b, l = divmod(k, 9)
                    e = HE[k % 2]
                    if l == 0:
                        if k == 0:
                            dve.wait_ge(hsilu.sem, hsilu.at(lay, 1))
                        else:
                            dve.wait_ge(hprod.sem, hprod.at(lay, k - 1))
                        tt(flat(e + 4, 4), flat(HK + 4 * b, 4), flat(HK + 8 + 4 * b, 4), ALU.add)\
                            .then_inc(hqk.sem, 1)
                        return
                    m = 1 << (l - 1)
                    dve.wait_ge(hexp.sem, hexp.at(lay, 8 * b + l))
                    tt(flat(e, 4), flat(e, 4), flat(HQ + 4 * b, 4), ALU.mult)
                    ek = flat(e + 4, 4)
                    tt(half(ek, m, 0), half(ek, m, 0), half(flat(HK + 4 * b, 4), m, 0), ALU.mult)
                    tt(half(ek, m, 1), half(ek, m, 1), half(flat(HK + 8 + 4 * b, 4), m, 1), ALU.mult).then_inc(hqk.sem, 1)
                elif kind == "hgC":
                    b, l = divmod(k, 9)
                    dve.wait_ge(hprod.sem, hprod.at(lay, k + 1))
                    if k == 9:
                        dve.wait_ge(ho_ok.sem, ho_ok.at(lay, 2))
                    if k:
                        dve.wait_ge(hcp.sem, hcp.at(lay, k))
                    for i in range(T):
                        j = 1 - i if l == 8 else i
                        o = hatt[:, i, :, j * P:(j + 1) * P]
                        src = A[k % 2 * 2 + i][:, :].rearrange("p (a s) -> p a s", a=4)
                        if l in (0, 8):
                            ins = V.tensor_copy(o, src)
                        else:
                            mask = cn("lev", (l - 1) * P, l * P).bitcast(U32).rearrange("p (a s) -> p a s", a=1)
                            ins = V.copy_predicated(o, mask.broadcast_to([P, 4, P]), src)
                    ins.then_inc(hcp.sem, 1)
                elif kind == "hnorm":
                    dve.wait_ge(hrs.sem, hrs.at(lay, 1))
                    for c in range(KC):
                        ins = stt(arena[:, HQ + c, :], arena[:, HQ + c, :], pc("hg_g", c), arena[:, HE[1] + c, :],
                                  ALU.mult, ALU.mult)
                    st.done(ins)
                    st.wait()
                    tt(flat(HQ, KC), flat(HQ, KC), flat(HG, KC), ALU.mult).then_inc(yh_fin.sem, 1)
                elif kind == "mvt":
                    V.memset(mvtok[:, :, :, P:P + 1], 1.0).then_inc(mvT_cp.sem, 1)
                    for q in range(4):
                        dve.wait_ge(mvT.sem, mvT.at(lay, q + 1))
                        V.tensor_copy(mvtok[:, q // 2, q % 2 * 4:q % 2 * 4 + 4, 0:P],
                                      A[q][:, :].rearrange("p (a s) -> p a s", a=4)).then_inc(mvT_cp.sem, 1)
                elif kind == "mlA":
                    if k >= 2:
                        dve.wait_ge(matt.sem, matt.at(lay, k - 1))
                    dve.wait_ge(mbc.sem, mbc.at(lay, k + 1))
                    decay_args(k, lay, ME[k % 2], A[k % 2], lambda d: 32 + 8 * d + k, marg)
                elif kind == "mlB":
                    dve.wait_ge(mexp.sem, mexp.at(lay, k + 1))
                    dve.wait_ge(mqk.sem, mqk.at(lay, k + 1))
                    if k >= 2:
                        dve.wait_ge(mnum.sem, mnum.at(lay, k - 1))
                    e, w = flat(ME[k % 2], 3), flat(MA[k % 2], 3)
                    for at, src, n in ((0, 0, 256), (256, 0, 128), (384, S + 128, 128), (512, S, 256)):
                        ins = stt(w[:, at:at + n], e[:, at:at + n], float(P) ** -0.5, A[2][:, src:src + n], ALU.mult, ALU.mult)
                    ins.then_inc(matt.sem, 1)
                elif kind == "mlC":
                    dve.wait_ge(mnum.sem, mnum.at(lay, k + 1))
                    den = small[:, 0:4].rearrange("p (i d) -> p i d", i=T)
                    for i in range(T):
                        ins = V.tensor_copy(den[:, i, :], A[3 + i][:, 0:258].rearrange("p (d e) -> p d e", d=2)[:, :, P])
                    st.done(ins)
                    st.wait()
                    st.done(stt(small[:, 4:8], small[:, 0:4], -1.0, small[:, 0:4], ALU.mult, ALU.max))
                    st.wait()
                    st.done(tt(small[:, 8:12].rearrange("p (i d) -> p i d", i=T), small[:, 4:8].rearrange("p (i d) -> p i d", i=T),
                               etok[:, :, :, k], ALU.max))
                    st.wait()
                    st.done(V.reciprocal(small[:, 12:16], small[:, 8:12]))
                    st.wait()
                    for i in range(T):
                        ins = ts(hsum[:, i, k, :], A[3 + i][:, 0:P], small[:, 12 + 2 * i:13 + 2 * i], None, ALU.mult)
                    st.done(ins)
                    st.wait()
                    for i in range(T):
                        ins = stt(hsum[:, i, k, :], A[3 + i][:, 129:129 + P], small[:, 13 + 2 * i:14 + 2 * i],
                                  hsum[:, i, k, :], ALU.mult, ALU.add)
                    ins.then_inc(mh_cp.sem, 1)
                elif kind == "mlnorm":
                    dve.wait_ge(mh_cp.sem, mh_cp.at(lay, 8))
                    x = flat(HSUM, KC).rearrange("p (n e) -> p n e", n=16)
                    st.done(V.tensor_reduce(small[:, 0:16], x, AX_X, ALU.add))
                    st.wait()
                    st.done(ts(small[:, 0:16], small[:, 0:16], 1.0 / P, None, ALU.mult))
                    st.wait()
                    tt(x, x, small[:, 0:16].rearrange("p (n e) -> p n e", e=1).broadcast_to([P, 16, P]), ALU.subtract)\
                        .then_inc(mcen.sem, 1)
                    dve.wait_ge(msq.sem, msq.at(lay, 1))
                    V.tensor_reduce(small[:, 16:32], flat(SQ, KC).rearrange("p (n e) -> p n e", n=16), AX_X, ALU.add)\
                        .then_inc(mvar.sem, 1)
                    dve.wait_ge(mrs.sem, mrs.at(lay, 1))
                    tt(x, x, small[:, 48:64].rearrange("p (n e) -> p n e", e=1).broadcast_to([P, 16, P]), ALU.mult)\
                        .then_inc(mhn.sem, 1)
                elif kind == "mlturn":
                    dve.wait_ge(msig.sem, msig.at(lay, 1))
                    for q in range(4):
                        dve.wait_ge(mhT.sem, mhT.at(lay, q + 1))
                        for a in range(2):
                            c = 2 * q + a
                            ins = stt(arena[:, MO + c, :], A[q][:, a * S:(a + 1) * S], pc("ml_g", c), arena[:, MO + c, :],
                                      ALU.mult, ALU.mult)
                    ins.then_inc(ym_fin.sem, 1)
                elif kind == "hid":
                    dve.wait_ge(silu_ok.sem, silu_ok.at(lay, k + 1))
                    f = FT[k % 2]
                    tt(arena[:, HID + k, :], arena[:, f, :], arena[:, f + 1, :], ALU.mult).then_inc(hid_ok.sem, 1)
                elif kind == "ple_add":
                    dve.wait_ge(*evac(lay, last("pleg")))
                    dve.wait_ge(ple_cp.sem, ple_cp.at(lay, 1))
                    st.done(tt(flat(PLG, KC), flat(PLG, KC), flat(PLE, KC), ALU.mult))
                    st.wait()
                    hf = h[:].rearrange("p c s -> p (c s)")
                    tt(hf, hf, flat(PLG, KC), ALU.add).then_inc(h_fin.sem, 1)

            hflat = h[:].rearrange("p c s -> p (c s)")

            def norm2(n, scale, shift):
                dve.wait_ge(rs_ready.sem, rs_ready.at(DEPTH, n))
                if shift is None:
                    for c in range(KC):
                        ins = stt(h[:, c, :] if n == 1 else arena[:, c, :], h[:, c, :], p2(scale, c), rstd[:, 1, 0, :],
                                  ALU.mult, ALU.mult)
                    ins.then_inc(*((u_ready.sem, 1) if n == 1 else (y2_fin, 1)))
                    return
                st.done(tt(u[:], h[:], rstd[:, 1, 0:1, :].broadcast_to([P, KC, S]), ALU.mult))
                st.wait()
                for c in range(KC):
                    ins = ts(u[:, c, :], u[:, c, :], mod[:, scale + c:scale + c + 1], mod[:, shift + c:shift + c + 1],
                             ALU.mult, ALU.add)
                ins.then_inc(u_ready.sem, 1)

            V.memset(eps[:], EPS).then_inc(eps_set, 1)
            dve.wait_ge(con_in, 16)
            for lay in range(n_layers):
                for kind, k in sched:
                    item(kind, k, lay)
            if not second:
                return
            dve.wait_ge(par2_in, 32)
            norm2(1, "fin1_g", None)
            st.wait()
            lam = p2("lam", 0, 4)
            st.done(tt(small[0:64, 0:1], lam[0:64, 0:1], lam[0:64, 1:2], ALU.mult))
            tt(small[0:64, 1:2], lam[0:64, 2:3], lam[0:64, 3:4], ALU.mult).then_inc(lam_in, 1)
            dve.wait_ge(*done2(ADA_UNITS - 1))
            st.done(tt(mod[:, 0:48], A[2][:, 0:48], p2("b_ada", 0, 48), ALU.add))
            st.wait()
            st.done(stt(mod[:, 48:56], mod[:, 8:16], 1.0, p2("n1_g", 0, 8), ALU.add, ALU.mult))
            st.done(stt(mod[:, 56:64], mod[:, 32:40], 1.0, p2("n2_g", 0, 8), ALU.add, ALU.mult))
            st.done(ts(mod[:, 73:74], p2("sub_g"), 1.0 - LAMBDA_INIT, None, ALU.mult))
            dve.wait_ge(lam_exp, 1)
            st.done(tt(small[:, 4:5], small[:, 3:4], small[:, 2:3], ALU.subtract))
            st.wait()
            st.done(ts(mod[:, 72:73], small[:, 4:5], -LAMBDA_INIT, None, ALU.add))
            st.wait()
            norm2(2, 48, 0)
            if upto == "ada":
                return
            for q in range(4):
                dve.wait_ge(rope_mm, q + 1)
                x = chunks(Q2 + 2 * q, 2)
                t = chunks(PADA + 2 * q, 2)
                sin, cos = (c2(n, 0, S).rearrange("p (c s) -> p c s", c=1).broadcast_to([P, 2, S]) for n in ("sin", "cos"))
                st.done(tt(t, A[q][:, :].rearrange("p (c s) -> p c s", c=2), sin, ALU.mult))
                st.done(tt(x, x, cos, ALU.mult))
                st.wait()
                tt(x, x, t, ALU.add).then_inc(rope_ok, 1)
            for i in range(T):
                dve.wait_ge(v2T, i + 1)
                V.tensor_copy(v2tok[:, i, :], A[i][:, :]).then_inc(v2T_cp, 1)

            def maxima(hd):
                dve.wait_ge(sc_ok, hd + 1)
                if hd >= 2:
                    dve.wait_ge(w2_ok, hd - 1)
                n = 4 * (hd % 2)
                for c in range(2):
                    ins = V.tensor_reduce(small[:, 24 + n + 2 * c:26 + n + 2 * c],
                                          A[hd % 2 * 2 + c][:, :].rearrange("p (c s) -> p c s", c=2), AX_X, ALU.max)
                st.done(ins)
                st.wait()
                ts(small[:, 8 + n:12 + n], small[:, 24 + n:28 + n], -(HD2 ** -0.5), None, ALU.mult).then_inc(sc_max, 1)

            def weights(hd):
                n = 4 * (hd % 2)
                dve.wait_ge(sc_exp, 4 * (hd + 1))
                if hd >= 2:
                    dve.wait_ge(w2T, hd - 1)
                r = small[:, 32 + n:36 + n]
                st.done(V.reciprocal(small[:, 32 + n:36 + n], small[:, 16 + n:20 + n]))
                st.wait()
                st.done(ts(r[:, 2:4], r[:, 2:4], mod[:, 72:73], None, ALU.mult))
                st.wait()
                for i in range(T):
                    ins = ts(arena[:, WA[hd % 2] + i, :], arena[:, EA[hd % 2] + i, :], r[:, i:i + 1], None, ALU.mult)
                st.done(ins)
                st.wait()
                for i in range(T):
                    ins = stt(arena[:, WA[hd % 2] + i, :], arena[:, EA[hd % 2] + 2 + i, :], r[:, 2 + i:3 + i],
                              arena[:, WA[hd % 2] + i, :], ALU.mult, ALU.add)
                ins.then_inc(w2_ok, 1)

            def turned(hd):
                dve.wait_ge(w2T, hd + 1)
                if hd >= 2:
                    dve.wait_ge(o2_ok, hd - 1)
                V.tensor_copy(flat(WAT[hd % 2], 2), A[4][:, :]).then_inc(w2T_cp, 1)

            maxima(0)
            maxima(1)
            b, before = use2(WOUT2 - 1)
            dve.wait_ge(freed[b].sem, before + 1)
            b, before = use2(WOUT2 - 2)
            dve.wait_ge(freed[b].sem, before + 1)
            W = S + 16
            pa = flat(PADA, 5)[:, 0:4 * W].rearrange("p (g w) -> p g w", g=4)
            pb = flat(PADB, 5)[:, 0:4 * W].rearrange("p (g w) -> p g w", g=4)
            st.done(V.memset(pa[:, :, 0:8], 0.0))
            st.done(V.memset(pa[:, :, W - 8:W], 0.0))
            st.done(V.tensor_copy(pa[:, :, 8:8 + S], chunks(U2, 4)))
            st.wait()
            st.done(tt(pb[:, :, 1:W], pa[:, :, 0:W - 1], pa[:, :, 1:W], ALU.add))
            st.wait()
            src, dst, lo = pb, pa, 1
            for g in range(4):
                st.done(tt(arena[:, RD + g, :], src[:, g, 8:8 + S], c2("cnt", g * S, (g + 1) * S), ALU.mult))
                st.wait()
                ins = tt(arena[:, RD + g, :], arena[:, RD + g, :], arena[:, U2 + g, :], ALU.subtract)
                if g == 3:
                    ins.then_inc(pool_d, 1)
                    break
                st.done(ins)
                k = 1 << g
                hi = W - lo if g else W
                st.done(tt(dst[:, g + 1:4, lo + k:hi - k], src[:, g + 1:4, lo:hi - 2 * k], src[:, g + 1:4, lo + 2 * k:hi], ALU.add))
                st.wait()
                src, dst, lo = dst, src, lo + k
            for n in range(2):
                dve.wait_ge(pool_mm, n + 1)
                for g in (2 * n, 2 * n + 1):
                    ins = ts(arena[:, P2 + g, :], G[2][:, g % 2 * S:g % 2 * S + S], p2("pool_s", g), None, ALU.mult)
                ins.then_inc(pool_fin, 1)
            for hd in range(HEADS2):
                weights(hd)
                turned(hd)
                if hd + 2 < HEADS2:
                    maxima(hd + 2)
            dve.wait_ge(o2_rs, 1)
            for hd in range(HEADS2):
                ins = stt(arena[:, O2 + hd, :], arena[:, O2 + hd, :], mod[:, 73:74], arena[:, RD + hd, :], ALU.mult, ALU.mult)
            ins.then_inc(o2_fin, 1)
            for m in range(WOUT2, ROUTER):
                b, before = use2(m)
                dve.wait_ge(*done2(m))
                for c in range(2):
                    n = 2 * (m - WOUT2) + c
                    ins = stt(h[:, n, :], G[b][:, c * S:(c + 1) * S], mod[:, 16 + n:17 + n], h[:, n, :], ALU.mult, ALU.add)
                ins.then_inc(freed[b].sem, 1)
            norm2(3, 56, 24)
            if upto == "attn":
                return
            dve.wait_ge(*done2(ROUTER))
            lg = flat(RD, 1)[:, 0:T * 36].rearrange("p (i n) -> p i n", i=T)
            st.done(V.tensor_copy(lg, A[0][:, 0:128].rearrange("p (i n) -> p i n", i=T)[:, :, 0:36]))
            st.wait()
            scr = flat(RD + 1, 2)

            def view(at, *dims):
                n = int(np.prod(dims))
                v = scr[:, at:at + T * n]
                if len(dims) == 1:
                    return v.rearrange("p (i a) -> p i a", i=T)
                return v.rearrange("p (i a b) -> p i a b", i=T, a=dims[0])

            def op(ins):
                st.done(ins)
                st.wait()

            def first_max(x, n, at):
                mx, t, mn, oh = view(at, 1), view(at + 2, n), view(at + 2 + 2 * n, 1), view(at + 4 + 2 * n, n)
                io = c2("iota", 0, n).rearrange("p (i n) -> p i n", i=1).broadcast_to([P, T, n])
                op(V.tensor_reduce(mx, x, AX_X, ALU.max))
                op(tt(t, x, mx.broadcast_to([P, T, n]), ALU.is_equal))
                op(stt(t, t, -100.0, io, ALU.mult, ALU.add))
                op(V.tensor_reduce(mn, t, AX_X, ALU.min))
                op(ts(mn, mn, 100.0, None, ALU.add))
                op(tt(oh, io, mn.broadcast_to([P, T, n]), ALU.is_equal))
                return mx, oh

            gl = lg[:, :, 0:4]
            gmx, goh = first_max(gl, 4, 0)
            tt(small[:, 0:8].rearrange("p (i n) -> p i n", i=T), gl, gmx.broadcast_to([P, T, 4]), ALU.subtract).then_inc(r_sh, 1)
            el = lg[:, :, 4:36].rearrange("p i (g j) -> p i g j", g=4)
            pr = view(40, 4, 8)
            op(tt(pr, el, goh.rearrange("p i (g o) -> p i g o", o=1).broadcast_to([P, T, 4, 8]), ALU.mult))
            ein = view(110, 8)
            op(V.tensor_reduce(ein, pr.rearrange("p i g j -> p i j g"), AX_X, ALU.add))
            m1, oh1 = first_max(ein, 8, 130)
            rest = view(180, 8)
            op(stt(rest, oh1, NEG, ein, ALU.mult, ALU.add))
            m2, oh2 = first_max(rest, 8, 200)
            tt(small[:, 16:18].rearrange("p (i n) -> p i n", i=T), m2, m1, ALU.subtract).then_inc(r_sh, 1)
            dve.wait_ge(r_exp, 2)
            op(V.tensor_reduce(small[:, 20:22], small[:, 8:16].rearrange("p (i n) -> p i n", i=T), AX_X, ALU.add))
            op(ts(small[:, 22:24], small[:, 18:20], 1.0, None, ALU.add))
            op(V.reciprocal(small[:, 24:28], small[:, 20:24]))
            op(tt(small[:, 28:30], small[:, 24:26], small[:, 26:28], ALU.mult))
            op(tt(small[:, 30:32], small[:, 28:30], small[:, 18:20], ALU.mult))

            def col(at):
                return small[:, at:at + 2].rearrange("p (i n) -> p i n", i=T).broadcast_to([P, T, 8])

            w8 = view(250, 8)
            op(tt(oh1, oh1, col(28), ALU.mult))
            op(tt(oh2, oh2, col(30), ALU.mult))
            op(tt(w8, oh1, oh2, ALU.add))
            wrow = small[:, 128:192].rearrange("p (i g j) -> p i g j", i=T, g=4)
            for i in range(T):
                ins = tt(wrow[:, i], goh[:, i].rearrange("p (g o) -> p g o", o=1).broadcast_to([P, 4, 8]),
                         w8[:, i:i + 1, :].broadcast_to([P, 4, 8]), ALU.mult)
                if i:
                    ins.then_inc(r_w, 1)
                else:
                    st.done(ins)
            dve.wait_ge(r_T, 1)
            V.tensor_copy(rowt[:, :], A[1][0:32, 0:S]).then_inc(r_wT, 1)
            for q in range(EXPERTS // 2):
                dve.wait_ge(wb_mm, q + 1)
                V.tensor_copy(flat(WB + 2 * q, 2), A[q % 4][:, :]).then_inc(wb_cp, 1)
            dve.wait_ge(wb_cp, EXPERTS // 2)

            def hidden(e, parity):
                for j in range(4):
                    dve.wait_ge(gate_ok, e * 4 + (j + 1))
                    o = arena[:, HIDE[parity] + j, :]
                    if j < 3:
                        tt(o, arena[:, SG2 + j, :], E4[j][:, S:2 * S], ALU.mult).then_inc(freed[j].sem, 1)
                        dve.wait_ge(freed[j].sem, e + (G2 + 1))
                    else:
                        tt(o, arena[:, SG2 + j, :], E4[j][:, S:2 * S], ALU.mult).then_inc(e4_freed, 1)
                        dve.wait_ge(e4_freed, e + 1)
                    tt(o, o, wb[:, e, :], ALU.mult).then_inc(hide_ok, 1)

            wb = chunks(WB, EXPERTS)
            hidden(0, 0)
            hidden(1, 1)
            with dve.Fori(0, (EXPERTS - 2) // 2) as i:
                for a in range(2):
                    dve.wait_ge(unit_done.sem, (i * 2 + a) * 6 + (B2 + MOE + 10))
                    hidden(i * 2 + (a + 2), a)
            dve.wait_ge(y2_ok, 1)
            for c in range(KC):
                ins = stt(h[:, c, :], A[c // 2][:, c % 2 * S:c % 2 * S + S], mod[:, 40 + c:41 + c], h[:, c, :], ALU.mult, ALU.add)
            ins.then_inc(y2_fin, 1)
            norm2(4, "fin2_g", None)




def units(w):
    n = w.shape[1]
    return w.reshape(KC, P, n // UC, UC).transpose(2, 1, 0, 3).reshape(n // UC, P, UNIT)


def by_channel(v):
    return v.reshape(-1, P).T


def layer_units(i, lay):
    sizes = (("z", D), ("xbc", 1536), ("dt", 32), ("hq", D), ("hf", 2 * D), ("hi", D), ("hg", D), ("mq", D), ("mk", D),
             ("mv", D), ("mi", 16), ("mf", 16), ("mo", D), ("gates", 3 * D))
    seg, at = {}, 0
    for name, n in sizes:
        seg[name] = i["w_in"][lay][:, at:at + n]
        at += n
    rows = np.zeros((D, UC), np.float32)
    rows[:, 0:32], rows[:, 32:48], rows[:, 64:80] = seg["dt"], seg["mi"], seg["mf"]
    g = seg["gates"]
    parts = [units(rows)] + [units(seg[k]) for k in ("z", "xbc", "hf", "hq", "hi", "hg", "mq", "mk", "mv", "mo")]
    parts.append(np.stack([units(g[:, :D]), units(i["w_br_ssd"][lay])], 1).reshape(8, P, UNIT))
    parts += [units(w) for w in (g[:, D:2 * D], g[:, 2 * D:], i["w_br_hg"][lay], i["w_br_ml"][lay], i["w_out"][lay])]
    parts.append(units(i["w_up"][lay].reshape(D, 2, FC, P).transpose(0, 2, 1, 3).reshape(D, FC * UC)))
    down = np.zeros((3 * D, D), np.float32)
    down[:FF] = i["w_down"][lay]
    parts.append(down.reshape(3, KC, P, 4, UC).transpose(3, 0, 2, 1, 4).reshape(12, P, UNIT))
    parts.append(i["w_ple"][lay].reshape(2, P, D).transpose(1, 0, 2).reshape(1, P, UNIT))
    parts.append(units(i["w_ple_gate"][lay]))
    return np.concatenate(parts)


def layer_parameters(i, lay):
    par = np.zeros((P, NPAR), np.float32)

    def put(name, a):
        par[:a.shape[0], PAR[name]:PAR[name] + a.shape[1]] = a

    put("mix_g", by_channel(i["norm_mix_g"][lay]))
    put("conv_w", i["ssd_conv_w"][lay].reshape(SSD_CONV, 12, P).transpose(2, 1, 0).reshape(P, 60))
    put("conv_b", by_channel(i["ssd_conv_b"][lay]))
    put("ssd_d", by_channel(np.repeat(i["ssd_d"][lay], 64)))
    put("ssd_g", by_channel(i["ssd_norm_g"][lay]))
    put("hg_g", by_channel(i["hg_norm_g"][lay]))
    put("ml_g", by_channel(i["ml_norm_g"][lay]))
    put("ffn_g", by_channel(i["norm_ffn_g"][lay]))
    put("fconv_w", i["ffn_conv_w"][lay].reshape(FFN_CONV, 2 * FC, P).transpose(2, 1, 0).reshape(P, 132))
    put("fconv_b", by_channel(i["ffn_conv_b"][lay]))
    row_b = np.zeros((P, 1), np.float32)
    row_b[:32, 0] = i["ssd_dt_bias"][lay].ravel()
    row_b[32:48, 0] = i["ml_i_bias"][lay].ravel()
    row_b[64:80, 0] = i["ml_f_bias"][lay].ravel()
    put("row_b", row_b)
    put("a_log", i["ssd_a_log"][lay].reshape(32, 1))
    put("lb_raw", np.concatenate([by_channel(i["hg_lb_raw"][j].ravel()) for j in range(DEPTH)], 1))
    put("lb_mask", np.tile(np.array([[1.0, float(lay >= 1)]], np.float32), (P, 1)))
    put("p", i["p"][lay, 0].T.reshape(2, P, S).transpose(1, 0, 2).reshape(P, 2 * S))
    return par


def second_units(i):
    router = np.zeros((D, UC), np.float32)
    router[:, 0:GROUPS] = i["w_router_group_2"][0]
    router[:, GROUPS:GROUPS + EXPERTS] = i["w_router_expert_2"][0]
    gate, up = (i[k][0].reshape(EXPERTS, KC, P, 4, P) for k in ("w_gate_2", "w_up_2"))
    gate_up = np.stack([gate, up], 4).transpose(0, 3, 2, 1, 4, 5).reshape(EXPERTS, 4, P, UNIT)
    down = i["w_down_2"][0].reshape(EXPERTS, 4, P, 2, 512).transpose(0, 3, 2, 1, 4).reshape(EXPERTS, 2, P, UNIT)
    experts = np.concatenate([gate_up, down], 1)
    order = moe_order()
    return np.concatenate([units(i["w_ada_2"][0]), units(i["w_in_2"][0]), units(i["w_out_2"][0]), units(router),
                           experts[[e for e, _ in order], [j for _, j in order]]])


def second_parameters(i):
    par = np.zeros((P, NPAR2), np.float32)

    def put(name, a):
        par[:a.shape[0], PAR2[name]:PAR2[name] + a.shape[1]] = a

    for name, key in (("c", "c_2"), ("b_ada", "b_ada_2"), ("n1_g", "norm1_g_2"), ("n2_g", "norm2_g_2"),
                      ("sub_g", "subln_g_2")):
        put(name, by_channel(i[key][0]))
    put("fin1_g", by_channel(i["final_norm_g"]))
    put("fin2_g", by_channel(i["final_g_2"]))
    put("pool_s", i["pool_scale_2"][0].T)
    put("lam", np.stack([i[f"lambda_{k}_2"][0] for k in ("q1", "k1", "q2", "k2")], 1))
    put("w_pool", i["w_pool_2"][0].transpose(1, 0, 2).reshape(P, 4 * P))
    put("b_route", np.concatenate([i["b_router_group_2"][0], i["b_router_expert_2"][0]])[None])
    return par


def kernel(**inputs):
    import concourse.bacc as _bacc
    from concourse.bass_utils import run_bass_kernel_spmd as _run

    i = {k: np.asarray(v) for k, v in inputs.items()}
    x = i["x"][0].T.reshape(KC, P, S).transpose(1, 0, 2).reshape(P, KC * S)
    arrays = {
        "stream": np.concatenate([layer_units(i, 0), layer_units(i, 1), second_units(i)]),
        "par_d": np.stack([layer_parameters(i, lay) for lay in range(DEPTH)]),
        "con_d": constants(),
        "x_d": np.ascontiguousarray(x),
        "par2_d": second_parameters(i),
        "con2_d": constants2(),
    }
    nc = _bacc.Bacc("TRN2", target_bir_lowering=False, num_devices=1)
    args = [nc.dram_tensor(name, a.shape, F32, kind="ExternalInput").ap() for name, a in arrays.items()]
    out = nc.dram_tensor("out", (P, KC * S), F32, kind="ExternalOutput").ap()
    program(nc, *args, out)
    r = _run(nc, [arrays], core_ids=[0])
    return r.results[0]["out"].reshape(P, KC, S).transpose(2, 1, 0).reshape(1, S, D)
```

```python
from contextlib import ExitStack

import numpy as np

import concourse.bass as bass
from concourse import mybir

F32 = mybir.dt.float32
U32 = mybir.dt.uint32
F32R = mybir.dt.float32r
I32 = mybir.dt.int32
ONE_BITS = 0x3F800000
ALU = mybir.AluOpType
ACT = mybir.ActivationFunctionType
AX_X = mybir.AxisListType.X

P = 128
D = 1024
S = 256
KC = D // P
T = S // P
DEPTH = 2
EPS = 1e-6
NEG = -1e30
TINY = 1e-30
LN_FLOOR = 2.0 ** -60
SSD_H, ML_H = 16, 8
SSD_CONV, FFN_CONV = 5, 3
FF = 2816
HG_DELAY = 4
FC = FF // P
UC = 2 * P
UNIT = KC * UC
RING = 3
ERING = 6
GBANKS = 3

KINDS = (["rows"] + ["z"] * 4 + ["xbc"] * 6 + ["hf"] * 8 + ["hq"] * 4 + ["hi"] * 4 + ["hg"] * 4
         + ["mq"] * 4 + ["mk"] * 4 + ["mv"] * 4 + ["mo"] * 4
         + ["gs", "bs"] * 4 + ["gh"] * 4 + ["gm"] * 4 + ["bh"] * 4 + ["bm"] * 4
         + ["out"] * 4 + ["up"] * 22 + ["down"] * 12 + ["ple"] + ["pleg"] * 4)
UNITS = len(KINDS)
OF = {k: KINDS.index(k) for k in dict.fromkeys(KINDS)}


def bank_uses():
    use, out = 0, []
    for n, kind in enumerate(KINDS):
        if kind == "ple":
            out.append(None)
        elif kind == "down":
            out.append(use)
            if (n - OF["down"]) % 3 == 2:
                use += 1
        else:
            out.append(use)
            use += 1
    return out, use


USE, USES = bank_uses()
SPLITS = KINDS.count("up") + KINDS.count("down")
assert UNITS % RING == 0 and USES % GBANKS == 0
USES_PER_BANK = USES // GBANKS

PAR = {}
_at = 0
for _name, _n in (("mix_g", 8), ("conv_w", 60), ("conv_b", 12), ("ssd_d", 8), ("ssd_g", 8), ("hg_g", 8),
                  ("ml_g", 8), ("ffn_g", 8), ("fconv_w", 132), ("fconv_b", 44), ("row_b", 1), ("a_log", 1),
                  ("lb_raw", 32), ("lb_mask", 2), ("p", 512)):
    PAR[_name] = _at
    _at += _n
NPAR = _at

CON = {}
_at = 0
for _name, _n in (("ident", 128), ("ones", 128), ("fw", 512), ("bw", 512), ("mf", 256), ("mb", 256),
                  ("lev", 896)):
    CON[_name] = _at
    _at += _n
NCON = _at


HEADS2, HD2 = 4, 64
GROUPS, PER_GROUP = 4, 8
EXPERTS = GROUPS * PER_GROUP
LAMBDA_INIT = 0.8 - 0.6
ADA_UNITS = 6 * D // UC
WIN2, WOUT2, ROUTER = ADA_UNITS, ADA_UNITS + 8, ADA_UNITS + 12
MOE = ROUTER + 1
UNITS2 = MOE + EXPERTS * 6
ALL_UNITS = DEPTH * UNITS + UNITS2

PAR2 = {}
_at = 0
for _name, _n in (("c", 8), ("b_ada", 48), ("fin1_g", 8), ("n1_g", 8), ("n2_g", 8), ("fin2_g", 8), ("sub_g", 1),
                  ("pool_s", 4), ("lam", 4), ("w_pool", 512), ("b_route", 36)):
    PAR2[_name] = _at
    _at += _n
NPAR2 = _at

SLOTS = 64

CON2 = {}
_at = 0
for _name, _n in (("cos", 256), ("sin", 256), ("rot", 128), ("cnt", 1024), ("iota", SLOTS), ("quarters", 1)):
    CON2[_name] = _at
    _at += _n
NCON2 = _at


WIN_ORDER = (6, 7, 0, 1, 2, 3, 4, 5)


def moe_order():
    out = [(0, j) for j in range(4)]
    for e in range(1, EXPERTS):
        out += [(e, j) for j in range(4)] + [(e - 1, 4), (e - 1, 5)]
    return out + [(EXPERTS - 1, 4), (EXPERTS - 1, 5)]


def constants2():
    c = np.zeros((P, NCON2), np.float32)
    rot_dim = HD2 // 4
    hf = rot_dim // 2
    pos = np.arange(S, dtype=np.float32)
    inv = np.power(np.float32(500000.0), -np.arange(0, rot_dim, 2, dtype=np.float32) / np.float32(rot_dim)).astype(np.float32)
    ang = (pos[:, None] * inv[None, :]).astype(np.float32)
    cos, sin = np.cos(ang).astype(np.float32), np.sin(ang).astype(np.float32)
    ct, sn, rot = np.ones((P, S), np.float32), np.zeros((P, S), np.float32), np.zeros((P, P), np.float32)
    for base in (0, HD2):
        for i in range(hf):
            ct[base + i], ct[base + i + hf] = cos[:, i], cos[:, i]
            sn[base + i], sn[base + i + hf] = -sin[:, i], sin[:, i]
            rot[base + i + hf, base + i] = 1.0
            rot[base + i, base + i + hf] = 1.0
    c[:, 0:256], c[:, 256:512], c[:, 512:640] = ct, sn, rot
    t = np.arange(S)
    for g in range(4):
        w = 2 << g
        left, right = w // 2, w - 1 - w // 2
        cnt = (np.clip(t + right + 1, 0, S) - np.clip(t - left, 0, S)).astype(np.float32)
        c[:, 640 + g * S:640 + (g + 1) * S] = np.float32(1.0) / cnt
    c[:, CON2["iota"]:CON2["iota"] + SLOTS] = np.arange(SLOTS, dtype=np.float32)
    c[::32, CON2["quarters"]] = 1.0
    return c


def constants():
    c = np.zeros((P, NCON), np.float32)
    i = np.arange(P)
    s, t = i[:, None], i[None, :]

    def put(name, a):
        c[:, CON[name]:CON[name] + a.shape[1]] = a

    one, zero = np.ones((P, P), np.float32), np.zeros((P, P), np.float32)
    le, ge = (s <= t).astype(np.float32), (s >= t).astype(np.float32)
    put("ident", np.eye(P, dtype=np.float32))
    put("ones", one)
    put("fw", np.concatenate([le, one, zero, le], 1))
    put("bw", np.concatenate([ge, zero, one, ge], 1))
    put("mf", np.concatenate([np.where(s <= t, 0, NEG).astype(np.float32), zero], 1))
    put("mb", np.concatenate([zero, np.where(s >= t, 0, NEG).astype(np.float32)], 1))
    lev = [((s // (2 * m) == t // (2 * m)) & (s // m != t // m)).astype(np.float32)
           for m in (1, 2, 4, 8, 16, 32, 64)]
    put("lev", np.concatenate(lev, 1))
    return c


class Signal:

    def __init__(self, sem, per_layer, credit=0):
        self.sem, self.per, self.credit = sem, per_layer, credit

    def at(self, lay, n):
        return lay * self.per + (self.credit + n)


class Steps:

    def __init__(self, eng, sem):
        self.eng, self.sem, self.n = eng, sem, 0

    def done(self, ins):
        ins.then_inc(self.sem, 1)
        self.n += 1

    def wait(self, back=0):
        self.eng.wait_ge(self.sem, self.n - back)


def program(nc, stream, par_d, con_d, x_d, par2_d, con2_d, out):
    ctx = ExitStack()
    with ctx:
        def sb(name, shape, dt=F32):
            return ctx.enter_context(nc.sbuf_tensor(name, shape, dt))

        def sem(name):
            return ctx.enter_context(nc.semaphore(name))

        with nc.sbuf_tensor("ring", [P, RING, UNIT], F32) as ring, nc.sbuf_tensor("arena", [P, 130, S], F32) as arena:
            pass
        ring_r = sb("ring_r", [P, RING, UNIT], F32R)
        as_r, at = {}, 0
        for name, first, n in (("hidden_low", 8, 22), ("weights_and_u_high", 58, 32), ("hidden_high", 102, 22)):
            sb(f"before_{name}", [P, first - at, S])
            as_r[first] = sb(name, [P, n, S], F32R)
            at = first + n
        sb("arena_end", [P, 130 - at, S])
        h = sb("h", [P, KC, S])
        with nc.sbuf_tensor("u", [P, KC, S], F32) as u:
            pass
        u_r = sb("u_r", [P, KC, S], F32R)
        par = sb("par", [P, NPAR])
        con = sb("con", [P, NCON])
        rows = sb("rows", [96, S])
        rtmp = sb("rtmp", [96, 2, S])
        dtr = sb("dtr", [32, S])
        tok = sb("tok", [P, T, P])
        ctok = sb("ctok", [P, T, 48])
        ntok = sb("ntok", [P, T, 48])
        arow = sb("arow", [16, 2, S])
        mrow = sb("mrow", [8, 4, 2, S])
        etok = sb("etok", [P, T, 2, 8])
        rstd = sb("rstd", [P, 2, 2, S])
        small = sb("small", [P, 256])
        rowt = sb("rowt", [EXPERTS, S])
        mod = sb("mod", [P, 80])
        eps = sb("eps", [P, 1])
        path = sb("path", [P, 1])
        nega = sb("nega", [32, 2])
        lb = sb("lb", [P, 3, 16])

        def chunks(at, n):
            return arena[:, at:at + n, :]

        def chunks_r(at, n):
            first = max(a for a in as_r if a <= at)
            return as_r[first][:, at - first:at - first + n, :]

        def flat_r(at, n):
            return chunks_r(at, n).rearrange("p c s -> p (c s)")

        def flat(at, n):
            return arena[:, at:at + n, :].rearrange("p c s -> p (c s)")

        Z, XBC, XTOK, CB = 0, 8, 20, 28
        SE = (32, 35)
        SW = (38, 40)
        HF, HQ, HV, HG, HK, HVT = 42, 58, 66, 74, 82, 98
        HE = (8, 16)
        HATT = 24
        MQ, MK, MV, MO, MERGED = 106, 114, 66, 32, 122
        MVT, ME, MA, HSUM, GH, GM = 42, (51, 54), (82, 85), 98, 88, 8
        HID, FT, PLE, PLG = 8, (98, 100), 42, 50
        WHI, UHI, HIDHI = (58, 66, 74), 82, 102
        SQ = 106

        Q2, K2, V2, U2, V2T, O2, P2 = 0, 4, 8, 12, 16, 20, 24
        PADA, PADB, EA, WA, WAT, RD = 28, 33, (38, 42), (46, 48), (50, 52), 54
        HIDE, SG2, WB = (8, 12), 16, 20
        MEMBER, ADA = RD + 3, (60, 62)
        UTOK, PICK, WS, PICKW, XE, SGE, HSE, HTE, YE, WNOW = 0, 8, 24, 58, 98, 106, 108, 110, 112, (56, 57)
        MORE_SLOTS = 74
        CON2_AT, PAR2_AT = 114, 121

        banks = [ctx.enter_context(nc.psum_tensor(f"bank{i}", [P, 512], F32)) for i in range(8)]
        G, A = banks[:GBANKS], banks[GBANKS:]
        E4 = G + [A[4]]
        ident = con[:, CON["ident"]:CON["ident"] + P]
        ones = con[:, CON["ones"]:CON["ones"] + P]

        v2tok = flat(V2T, 4).rearrange("p (i n) -> p i n", i=T)
        xtok = flat(XTOK, 8).rearrange("p (i n) -> p i n", i=T)
        hvtok = flat(HVT, 8).rearrange("p (i n) -> p i n", i=T)
        hatt = flat(HATT, 8).rearrange("p (i a s) -> p i a s", i=T, a=4)
        mvtok = flat(MVT, 9)[:, 0:T * 8 * 129].rearrange("p (i a e) -> p i a e", i=T, a=8)
        hsum = flat(HSUM, 8).rearrange("p (i a e) -> p i a e", i=T, a=8)

        def half(x, m, which):
            return x.rearrange("p (n two m) -> p n two m", two=2, m=m)[:, :, which, :]

        def cn(name, a, b):
            return con[:, CON[name] + a:CON[name] + b]

        def pc(name, i=0):
            return par[:, PAR[name] + i:PAR[name] + i + 1]

        def c2(name, a, b):
            at = CON2[name]
            return flat(CON2_AT, 7)[:, at + a:at + b]

        def p2(name, i=0, n=1):
            at = PAR2[name]
            return flat(PAR2_AT, 3)[:, at + i:at + i + n]

        def signal(name, per_layer, credit=0):
            return Signal(sem(name), per_layer, credit)

        landed = [sem(f"weights_landed{i}") for i in range(RING)]
        e_landed = [sem(f"expert_weights_landed{i}") for i in range(ERING)]
        par_in, con_in, x_in, stored = sem("par_landed"), sem("constants_landed"), sem("x_landed"), sem("stored")
        dve_step, act_step, eps_set = sem("dve_step"), sem("act_step"), sem("eps_set")
        unit_done = signal("unit_done", UNITS)
        freed = [signal(f"bank{i}_read", USES_PER_BANK) for i in range(GBANKS)]
        center = signal("center_taps_done", 6 + 22)
        sq_ready = signal("squares_ready", 8)
        ss_ready = signal("square_sums_ready", 2)
        rs_ready = signal("rstd_ready", 2)
        u_ready = signal("u_ready", 16)
        lb_in = signal("lb_shifted", 1)
        lb_exp = signal("lb_exponentials", 1)
        nega_exp = signal("a_exponential", 1)
        sp_abs = signal("softplus_abs", 1)
        sp_ln = signal("softplus_log", 1)
        rows_ok = signal("rows_ready", 1)
        rowsT = signal("rows_transposed", 1)
        tok_ok = signal("rows_by_token_copied", 1)
        cum_ok = signal("cumulative_sums_ready", 3)
        m_ok = signal("m_rows_ready", 1)
        em_ok = signal("exp_minus_m_ready", 1)
        emT = signal("exp_minus_m_transposed", 1)
        rows_fin = signal("row_scalars_ready", 1)
        xs_ok = signal("xs_ready", 1)
        xT = signal("xs_transposed", 4)
        xT_cp = signal("xs_by_token_copied", 4)
        cb_ok = signal("cb_ready", 2)
        cb_cp = signal("cb_copied", 2)
        bc_ok = signal("decay_row_spread", SSD_H)
        arg_ok = signal("decay_arguments_ready", SSD_H)
        exp_ok = signal("decays_ready", SSD_H)
        att_ok = signal("ssd_weights_ready", SSD_H)
        y_ok = signal("ssd_sums_ready", SSD_H)
        y_cp = signal("ssd_sums_read", SSD_H // 2)
        yz_ok = signal("ssd_gated", 1)
        ysq = signal("ssd_squares_ready", 1)
        yss = signal("ssd_square_sums_ready", 1)
        yrs = signal("ssd_rstd_ready", 1)
        ys_fin = signal("ssd_branch_ready", 1)
        hsig = signal("hg_sigmoids_ready", 1)
        hsilu = signal("hg_silus_ready", 1)
        hclamp = signal("hg_forget_clamped", 1)
        hln = signal("hg_forget_logs_ready", 1)
        hvT = signal("hg_v_transposed", 4)
        hvT_cp = signal("hg_v_by_token_copied", 4)
        HSTEPS = 18
        hargs = signal("hg_arguments_ready", 16)
        hexp = signal("hg_decays_ready", 16)
        hqk = signal("hg_operands_ready", HSTEPS)
        hprod = signal("hg_products_ready", HSTEPS)
        hcp = signal("hg_weights_copied", HSTEPS)
        ho_ok = signal("hg_sums_ready", 4)
        ho_cp = signal("hg_sums_copied", 4)
        hsq = signal("hg_squares_ready", 1)
        hss = signal("hg_square_sums_ready", 1)
        hrs = signal("hg_rstd_ready", 1)
        yh_fin = signal("hg_branch_ready", 1)
        mvT = signal("ml_v_transposed", 4)
        mvT_cp = signal("ml_v_by_token_copied", 5)
        msig = signal("ml_output_gate_ready", 1)
        mbc = signal("ml_row_spread", ML_H)
        mqk = signal("ml_qk_ready", ML_H)
        marg = signal("ml_arguments_ready", ML_H)
        mexp = signal("ml_decays_ready", ML_H)
        matt = signal("ml_weights_ready", ML_H)
        mnum = signal("ml_sums_ready", ML_H)
        mh_cp = signal("ml_sums_read", ML_H)
        mcen = signal("ml_centred", 1)
        msq = signal("ml_squares_ready", 1)
        mvar = signal("ml_variance_ready", 1)
        mrs = signal("ml_rstd_ready", 1)
        mhn = signal("ml_normalised", 1)
        mhT = signal("ml_transposed", 4)
        ym_fin = signal("ml_branch_ready", 1)
        merge_ok = signal("merged_ready", 1)
        silu_ok = signal("ffn_silu_ready", 22)
        whi_ok = signal("weights_high_ready", SPLITS)
        wlo_ok = signal("weights_low_ready", SPLITS)
        uhi_ok = signal("u_high_ready", 4)
        ulo_ok = signal("u_low_ready", 1)
        hhi_ok = signal("ffn_hidden_high_ready", 22)
        hlo_ok = signal("ffn_hidden_low_ready", 22)
        hid_ok = signal("ffn_hidden_ready", 22)
        ple_cp = signal("ple_copied", 1)
        h_new = signal("h_sums_ready", 4)
        h_fin = signal("h_ready", 1)

        par2_in = sem("par2_landed")
        cs_ok = sem("silu_c_ready")
        ada_cp, ada_mm = sem("modulation_rows_copied"), sem("modulation_columns_ready")
        lam_in, lam_mm, lam_exp = sem("lambda_products"), sem("lambda_sums"), sem("lambda_exponentials")
        rope_mm, rope_ok = sem("rope_turned"), sem("rope_done")
        v2T, v2T_cp = sem("v2_transposed"), sem("v2_copied")
        sc_ok, sc_max, sc_exp, w2_ok = sem("scores_ready"), sem("score_maxima"), sem("score_exps"), sem("diff_weights_ready")
        w2T, w2T_cp, o2_ok = sem("diff_weights_transposed"), sem("diff_weights_copied"), sem("diff_sums")
        o2_sq, o2_ss, o2_rs, o2_fin = sem("diff_squares"), sem("diff_square_sums"), sem("diff_rstd"), sem("diff_out")
        pool_d, pool_mm, pool_fin = sem("pool_means"), sem("pool_products"), sem("pool_out")
        r_sh, r_exp, r_w, r_T, r_wT = (sem(f"route_{n}") for n in ("shifted", "exps", "weights", "transposed", "rows"))
        wb_mm, wb_cp = sem("expert_row_spread"), sem("expert_row_copied")
        e4_freed = sem("expert_bank3_read")
        gate_ok, hide_ok, y2_fin = sem("expert_gate"), sem("expert_hidden"), sem("x_final")
        utT, utT_cp = sem("u_transposed"), sem("u_by_token_copied")
        r_mem, r_cum, path_ok = sem("route_members"), sem("route_counts"), sem("path_chosen")
        pick_ok, pickw_ok, ws_mm, ws_cp = sem("picks_ready"), sem("weighted_picks_ready"), sem("picks_transposed"), sem("picks_copied")
        x_mm, x_cp = sem("expert_tokens_picked"), sem("expert_tokens_copied")
        sg_ok, hs_ok = sem("slot_silu_ready"), sem("slot_hidden_ready")
        ht_mm, ht_cp = sem("slot_hidden_transposed"), sem("slot_hidden_copied")
        ye_cp, wn_cp, s_sum = sem("slot_outputs_copied"), sem("slot_weights_copied"), sem("slots_summed")

        B2 = DEPTH * UNITS

        def done2(m):
            return unit_done.sem, B2 + m + 1

        def landed2(m):
            return landed[m % RING], 16 * ((B2 + m) // RING + 1)

        def e_slot(m):
            n = m % ERING
            if n < ERING - RING:
                return flat(MORE_SLOTS + 8 * n, 8)
            return ring[:, (B2 + MOE + n) % RING, :]

        def use2(m):
            k = m - WIN2
            return k % GBANKS, DEPTH * USES_PER_BANK + k // GBANKS

        def q_unit(j):
            return WIN2 + WIN_ORDER.index(j)

        G2 = DEPTH * USES_PER_BANK + 12 // GBANKS

        def evac(lay, unit):
            k = USE[unit]
            s = freed[k % GBANKS]
            return s.sem, s.at(lay, k // GBANKS + 1)

        def last(kind):
            return OF[kind] + KINDS.count(kind) - 1

        sched = [("norm", 0), ("unit", 0), ("lb", 0), ("rows", 0)]
        for n in range(1, OF["hf"]):
            sched.append(("unit", n))
            if n in (3, 6, 9):
                sched.append((f"rows{n // 3}", 0))
        sched.append(("silu_x", 0))
        for i in range(22):
            if i < 20:
                sched.append(("unit", OF["hf"] + i))
            if i == 1:
                sched.append(("xs_turn", 0))
            if i == 2:
                sched.append(("cb", 0))
            k = i - 3
            if 0 <= k < SSD_H:
                sched.append(("bc", k))
            if 0 <= k - 1 < SSD_H:
                sched.append(("seg", k - 1))
            if 0 <= k - 2 < SSD_H:
                sched.append(("y", k - 2))
        mq = OF["mq"]
        sched += [("hprep", 0), ("products", mq), ("products", mq + 1), ("products", mq + 2), ("ssd_norm", 0),
                  ("read", mq), ("hclamp", 0), ("hvt", 0), ("products", mq + 3), ("read", mq + 1), ("read", mq + 2),
                  ("hlog", 0), ("read", mq + 3)]
        for i in range(24):
            if i >= 4:
                sched.append(("products", mq + i))
            k = i - HG_DELAY
            if 0 <= k < HSTEPS:
                sched.append(("hgA", k))
            if 0 <= k - 1 < HSTEPS:
                sched.append(("hgB", k - 1))
            if 0 <= k - 2 < HSTEPS:
                sched.append(("hgC", k - 2))
            if i >= 4:
                sched.append(("read", mq + i))
            if k - 2 == 8:
                sched.append(("ho", 0))
        gh = OF["gh"]
        sched += [("ho", 1), ("products", gh), ("hnorm", 0), ("products", gh + 1), ("mvt", 0),
                  ("read", gh), ("read", gh + 1)]
        for i in range(10):
            if i < 8:
                if i >= 2:
                    sched.append(("unit", gh + i))
                sched.append(("mlA", i))
            if 0 <= i - 1 < 8:
                sched.append(("mlB", i - 1))
            if 0 <= i - 2 < 8:
                sched.append(("mlC", i - 2))
        bh = OF["bh"]
        sched += [("products", bh), ("products", bh + 1), ("products", bh + 2), ("mlnorm", 0), ("read", bh),
                  ("mlturn", 0), ("products", bh + 3), ("read", bh + 1), ("read", bh + 2), ("read", bh + 3)]
        sched += [("unit", OF["bm"] + i) for i in range(4)]
        up = OF["up"]
        sched += [("unit", OF["out"] + i) for i in range(3)]
        sched += [("split", up), ("unit", OF["out"] + 3), ("split", up + 1), ("norm", 1)]
        for i in range(24):
            if i < 22:
                sched += [("split", up + i + 2), ("unit", up + i)]
            if 1 <= i < 23:
                sched.append(("hid", i - 1))
            if i >= 2:
                sched.append(("hsplit", i - 2))
        for n in range(OF["down"], OF["pleg"]):
            if n + 2 < up + SPLITS:
                sched.append(("split", n + 2))
            sched.append(("unit", n))
        for j in range(4):
            sched += [("unit", OF["pleg"] + j), ("ple_add", j)]
        assert [n for k, n in sched if k in ("unit", "products")] == list(range(UNITS))

        utok = flat(UTOK, 8).rearrange("p (i n) -> p i n", i=T)
        pick = flat(PICK, 16).rearrange("p (i e s) -> p i e s", i=T, e=EXPERTS)
        pickw = flat(PICKW, 16).rearrange("p (i e s) -> p i e s", i=T, e=EXPERTS)
        pick2 = flat(PICK, 16).rearrange("p (i q n) -> p i q n", i=T, q=EXPERTS // 2)
        ws = chunks(WS, EXPERTS)
        xe = flat(XE, 4).rearrange("p (c n) -> p c n", c=KC)
        hte = flat(HTE, 1).rearrange("p (k s) -> p k s", k=4)
        PAIRS = EXPERTS // 2

        block = ctx.enter_context(nc.Block())

        assert 6 == ERING

        @block.sync
        def _(sp):
            total = B2 + MOE
            sp.dma_start(con[:], con_d).then_inc(con_in, 16)
            for n in range(RING):
                sp.dma_start(ring[:, n, :], stream[n]).then_inc(landed[n], 16)
            with sp.Fori(1, total // RING) as i:
                for r in range(RING):
                    sp.wait_ge(unit_done.sem, i * RING + (r - RING + 1))
                    sp.dma_start(ring[:, r, :], stream[i * RING + r]).then_inc(landed[r], 16)
            for n in range(total // RING * RING, total):
                sp.wait_ge(unit_done.sem, n - RING + 1)
                sp.dma_start(ring[:, n % RING, :], stream[n]).then_inc(landed[n % RING], 16)
            sp.wait_ge(h_new.sem, h_new.at(DEPTH, 0))
            for n in range(ERING):
                if n >= ERING - RING:
                    sp.wait_ge(unit_done.sem, B2 + MOE + n - ERING + 1)
                sp.dma_start(e_slot(n), stream[B2 + MOE + n]).then_inc(e_landed[n], 16)
            with sp.Fori(1, EXPERTS) as i:
                for r in range(ERING):
                    sp.wait_ge(unit_done.sem, i * ERING + (B2 + MOE + r - ERING + 1))
                    sp.dma_start(e_slot(r), stream[i * ERING + (B2 + MOE + r)]).then_inc(e_landed[r], 16)
            sp.wait_ge(y2_fin, 2)
            sp.dma_start(out, flat(0, KC)).then_inc(stored, 16)
            sp.wait_ge(stored, 16)

        @block.gpsimd
        def _(pool):
            for lay in range(DEPTH):
                if lay:
                    pool.wait_ge(h_new.sem, h_new.at(lay, 0))
                pool.dma_start(par[:], par_d[lay]).then_inc(par_in, 16)
            pool.wait_ge(unit_done.sem, unit_done.at(DEPTH - 1, last("down") + 1))
            pool.dma_start(flat(CON2_AT, 7)[:, 0:NCON2], con2_d).then_inc(par2_in, 16)
            pool.dma_start(flat(PAR2_AT, 3)[:, 0:NPAR2], par2_d).then_inc(par2_in, 16)

        @block.tensor
        def _(pe):
            RHS = {"bs": Z, "bh": HQ, "bm": MO, "out": MERGED}
            NEED = {"bs": (ys_fin, 1), "bh": (yh_fin, 1),
                    "bm": (ym_fin, 1), "out": (merge_ok, 1), "down": (hlo_ok, 22)}

            def unit(lay, n):
                kind = KINDS[n]
                sub = (n - OF["down"]) % 3 if kind == "down" else 0
                if kind in ("up", "down"):
                    pe.wait_ge(wlo_ok.sem, wlo_ok.at(lay, n - OF["up"] + 1))
                else:
                    pe.wait_ge(landed[n % RING], 16 * (lay * (UNITS // RING) + n // RING + 1))
                if n == OF[kind] and kind in NEED:
                    need, count = NEED[kind]
                    pe.wait_ge(need.sem, need.at(lay, count))
                slot = ring[:, n % RING, :]
                if kind == "ple":
                    pe.wait_ge(ym_fin.sem, ym_fin.at(lay, 1))
                    w = slot.rearrange("p (k m) -> p k m", k=2)
                    pin = par[:, PAR["p"]:PAR["p"] + 512].rearrange("p (k s) -> p k s", k=2)
                    for c in range(KC):
                        for k in range(2):
                            mm = pe.matmul(A[c // 2][:, c % 2 * S:c % 2 * S + S], w[:, k, c * P:(c + 1) * P],
                                           pin[:, k, :], start=(k == 0), stop=(k == 1))
                    mm.then_inc(unit_done.sem, 1)
                    return
                use = USE[n]
                bank = G[use % GBANKS]
                if sub == 0 and (lay or use >= GBANKS):
                    f = freed[use % GBANKS]
                    pe.wait_ge(f.sem, f.at(lay, use // GBANKS))
                if n == OF["pleg"]:
                    pe.wait_ge(*evac(lay, last("down")))
                w = slot.rearrange("p (k m) -> p k m", k=KC)
                x = u if kind not in RHS else chunks(RHS[kind], KC)
                x = h if kind == "pleg" else x
                if kind == "rows":
                    for k in range(KC):
                        pe.wait_ge(u_ready.sem, u_ready.at(lay, k + 1))
                        mm = pe.matmul(bank[0:96, 0:S], w[:, k, 0:96], u[:, k, :], start=(k == 0), stop=(k == KC - 1))
                elif kind in ("up", "down"):
                    ks = KC if kind == "up" else min(KC, FC - KC * sub)
                    whi = flat_r(WHI[(n - OF["up"]) % 3], KC).rearrange("p (k m) -> p k m", k=KC)
                    w = ring_r[:, n % RING, :].rearrange("p (k m) -> p k m", k=KC)
                    if kind == "up":
                        xhi, x = chunks_r(UHI, KC), u_r
                    else:
                        xhi, x = (chunks_r(at + KC * sub, ks) for at in (HIDHI, HID))
                    for c in range(2):
                        for part, (wx, xx) in enumerate(((whi, xhi), (w, xhi), (whi, x))):
                            for k in range(ks):
                                if n == OF["up"] and c == 0:
                                    if part == 0 and k % 2 == 0:
                                        pe.wait_ge(uhi_ok.sem, uhi_ok.at(lay, k // 2 + 1))
                                    elif part == 2 and k == 0:
                                        pe.wait_ge(ulo_ok.sem, ulo_ok.at(lay, 1))
                                mm = pe.matmul(bank[:, c * S:(c + 1) * S], wx[:, k, c * P:(c + 1) * P], xx[:, k, :],
                                               start=(sub == 0 and c == part == k == 0),
                                               stop=(part == 2 and k == ks - 1 and (kind == "up" or sub == 2)),
                                               skip_group_check=True)
                else:
                    for c in range(2):
                        for k in range(KC):
                            mm = pe.matmul(bank[:, c * S:(c + 1) * S], w[:, k, c * P:(c + 1) * P], x[:, k, :],
                                           start=(k == 0), stop=(k == KC - 1))
                mm.then_inc(unit_done.sem, 1)

            def turn(src, done):
                for q in range(4):
                    for c in range(4):
                        mm = pe.transpose(A[q][:, c * P:(c + 1) * P],
                                          src[:, q % 2 * 4 + c, q // 2 * P:(q // 2 + 1) * P], ident)
                    mm.then_inc(done.sem, 1)

            def item(kind, k, lay):
                if kind in ("unit", "products"):
                    unit(lay, k)
                elif kind == "norm":
                    for c in range(KC):
                        if c % 2 == 0:
                            pe.wait_ge(sq_ready.sem, sq_ready.at(lay, 4 * k + c // 2 + 1))
                        mm = pe.matmul(A[4][:, 0:S], ones, arena[:, SQ + c, :], start=(c == 0), stop=(c == KC - 1))
                    mm.then_inc(ss_ready.sem, 1)
                elif kind == "rows1":
                    pe.wait_ge(rows_ok.sem, rows_ok.at(lay, 1))
                    for i in range(T):
                        pe.transpose(A[3][:, i * P:i * P + 96], rows[0:96, i * P:(i + 1) * P], ident[0:96, 0:96])
                        mm = pe.transpose(A[3][:, i * P + 96:(i + 1) * P], dtr[0:32, i * P:(i + 1) * P], ident[0:32, 0:32])
                    mm.then_inc(rowsT.sem, 1)
                elif kind == "rows2":
                    pe.wait_ge(tok_ok.sem, tok_ok.at(lay, 1))
                    tri = ("fw", "bw")
                    for i in range(T):
                        for d, src, dst in ((0, 0, 0), (1, 16, 16), (0, 64, 32), (1, 72, 40)):
                            n = 16 if src < 64 else 8
                            for j in range(T):
                                mm = pe.matmul(A[2][:, i * 48 + dst:i * 48 + dst + n],
                                               cn(tri[d], j * S + i * P, j * S + (i + 1) * P),
                                               tok[:, j, src:src + n], start=(j == 0), stop=(j == T - 1))
                    mm.then_inc(cum_ok.sem, 1)
                    for d in range(2):
                        for j in range(T):
                            mm = pe.matmul(A[1][0:16, d * S:(d + 1) * S], tok[:, j, 16 * d:16 * d + 16],
                                           cn(tri[d], j * S, (j + 1) * S), start=(j == 0), stop=(j == T - 1))
                    mm.then_inc(cum_ok.sem, 1)
                    for d in range(2):
                        for j in range(T):
                            pe.matmul(A[0][0:8, d * S:(d + 1) * S], tok[:, j, 64 + 8 * d:72 + 8 * d],
                                      cn(tri[d], j * S, (j + 1) * S), start=(j == 0), stop=(j == T - 1))
                        for j in range(T):
                            mm = pe.matmul(A[4][0:8, d * S + j * P:d * S + (j + 1) * P],
                                           tok[:, j, 32 + 8 * d:40 + 8 * d], ident, start=True, stop=True)
                    mm.then_inc(cum_ok.sem, 1)
                elif kind == "rows3":
                    pe.wait_ge(em_ok.sem, em_ok.at(lay, 1))
                    for i in range(T):
                        for d in range(2):
                            mm = pe.transpose(A[3][:, (2 * i + d) * 8:(2 * i + d) * 8 + 8],
                                              mrow[0:8, 0, d, i * P:(i + 1) * P], ident[0:8, 0:8])
                    mm.then_inc(emT.sem, 1)
                elif kind == "xs_turn":
                    pe.wait_ge(xs_ok.sem, xs_ok.at(lay, 1))
                    pe.wait_ge(rows_fin.sem, rows_fin.at(lay, 1))
                    turn(chunks(XBC, KC), xT)
                elif kind == "cb":
                    pe.wait_ge(xT_cp.sem, xT_cp.at(lay, 4))
                    for g in range(2):
                        for i in range(T):
                            mm = pe.matmul(A[g][:, i * S:(i + 1) * S], arena[:, XBC + 8 + g, i * P:(i + 1) * P],
                                           arena[:, XBC + 10 + g, :], start=True, stop=True)
                        mm.then_inc(cb_ok.sem, 1)
                elif kind == "bc":
                    if k < 2:
                        pe.wait_ge(cb_cp.sem, cb_cp.at(lay, k + 1))
                    else:
                        pe.wait_ge(arg_ok.sem, arg_ok.at(lay, k - 1))
                    pe.matmul(A[k % 2][:, :], ident[0:16, k:k + 1].broadcast_to([16, P]),
                              arow[0:16].rearrange("p d s -> p (d s)"), start=True, stop=True)\
                        .then_inc(bc_ok.sem, 1)
                elif kind == "y":
                    pe.wait_ge(att_ok.sem, att_ok.at(lay, k + 1))
                    j = k // 2
                    if k % 2 == 0 and j >= 2:
                        pe.wait_ge(y_cp.sem, y_cp.at(lay, j - 1))
                    r = k % 2 * 64
                    for i in range(T):
                        mm = pe.matmul(A[2 + j % 2][r:r + 64, 0:S], xtok[:, i, k * 64:(k + 1) * 64],
                                       arena[:, SW[k % 2] + i, :], start=(i == 0), stop=(i == T - 1))
                    mm.then_inc(y_ok.sem, 1)
                elif kind == "ssd_norm":
                    pe.wait_ge(ysq.sem, ysq.at(lay, 1))
                    for g in range(2):
                        for c in range(4):
                            mm = pe.matmul(A[0][:, g * S:(g + 1) * S], ones, arena[:, XBC + 4 * g + c, :],
                                           start=(c == 0), stop=(c == 3))
                    mm.then_inc(yss.sem, 1)
                elif kind == "hvt":
                    pe.wait_ge(yrs.sem, yrs.at(lay, 1))
                    pe.wait_ge(y_cp.sem, y_cp.at(lay, 8))
                    pe.wait_ge(*evac(lay, last("hi")))
                    turn(chunks(HV, KC), hvT)
                elif kind == "hgB":
                    b, l = divmod(k, 9)
                    pe.wait_ge(hqk.sem, hqk.at(lay, k + 1))
                    if k >= 2:
                        pe.wait_ge(hcp.sem, hcp.at(lay, k - 1))
                    else:
                        pe.wait_ge(hvT_cp.sem, hvT_cp.at(lay, 4))
                    e = HE[k % 2]
                    for i in range(T):
                        j = 1 - i if l == 8 else i
                        for hd in range(4):
                            q = arena[:, HQ + 4 * b + hd if l == 0 else e + hd, j * P:(j + 1) * P]
                            mm = pe.matmul(A[k % 2 * 2 + i][:, hd * P:(hd + 1) * P],
                                           arena[:, e + 4 + hd, i * P:(i + 1) * P], q, start=True, stop=True)
                    mm.then_inc(hprod.sem, 1)
                elif kind == "ho":
                    pe.wait_ge(hcp.sem, hcp.at(lay, 9 * (k + 1)))
                    for pair in range(2):
                        n = 2 * k + pair
                        if n:
                            pe.wait_ge(ho_cp.sem, ho_cp.at(lay, n))
                        for a in range(2):
                            hd = 2 * pair + a
                            for i in range(T):
                                mm = pe.matmul(A[4][:, a * S:(a + 1) * S], hvtok[:, i, (4 * k + hd) * P:(4 * k + hd + 1) * P],
                                               hatt[:, i, hd, :], start=(i == 0), stop=(i == T - 1))
                        mm.then_inc(ho_ok.sem, 1)
                elif kind == "hnorm":
                    pe.wait_ge(hsq.sem, hsq.at(lay, 1))
                    for c in range(KC):
                        mm = pe.matmul(A[c // 2][:, c % 2 * S:c % 2 * S + S], ones, arena[:, HE[0] + c, :],
                                       start=True, stop=True)
                    mm.then_inc(hss.sem, 1)
                elif kind == "mvt":
                    pe.wait_ge(hrs.sem, hrs.at(lay, 1))
                    turn(chunks(MV, KC), mvT)
                elif kind == "mlA":
                    if k < 2:
                        pe.wait_ge(mvT_cp.sem, mvT_cp.at(lay, 5))
                    else:
                        pe.wait_ge(marg.sem, marg.at(lay, k - 1))
                    pe.matmul(A[k % 2][:, :], ident[0:8, k:k + 1].broadcast_to([8, P]),
                              mrow[0:8, 3].rearrange("p d s -> p (d s)"), start=True, stop=True)\
                        .then_inc(mbc.sem, 1)
                elif kind == "mlB":
                    if k:
                        pe.wait_ge(matt.sem, matt.at(lay, k))
                    for i in range(T):
                        mm = pe.matmul(A[2][:, i * S:(i + 1) * S], arena[:, MK + k, i * P:(i + 1) * P],
                                       arena[:, MQ + k, :], start=True, stop=True)
                    mm.then_inc(mqk.sem, 1)
                elif kind == "mlC":
                    pe.wait_ge(matt.sem, matt.at(lay, k + 1))
                    if k:
                        pe.wait_ge(mh_cp.sem, mh_cp.at(lay, k))
                    w = flat(MA[k % 2], 3)
                    for t, d, parts in ((0, 0, ((0, 0),)), (0, 1, ((256, 0), (512, 1))),
                                        (1, 0, ((128, 0), (384, 1))), (1, 1, ((640, 1),))):
                        for n, (at, i) in enumerate(parts):
                            mm = pe.matmul(A[3 + t][:, d * 129:(d + 1) * 129], w[:, at:at + P], mvtok[:, i, k, :],
                                           start=(n == 0), stop=(n == len(parts) - 1))
                    mm.then_inc(mnum.sem, 1)
                elif kind == "mlturn":
                    pe.wait_ge(mhn.sem, mhn.at(lay, 1))
                    for q in range(4):
                        for a in range(2):
                            for i in range(T):
                                mm = pe.transpose(A[q][:, a * S + i * P:a * S + (i + 1) * P], hsum[:, i, 2 * q + a, :], ident)
                        mm.then_inc(mhT.sem, 1)

            def norm2(n):
                for c in range(KC):
                    if c % 2 == 0:
                        pe.wait_ge(sq_ready.sem, sq_ready.at(DEPTH, 4 * (n - 1) + c // 2 + 1))
                    mm = pe.matmul(A[4][:, 0:S], ones, arena[:, SQ + c, :], start=(c == 0), stop=(c == KC - 1))
                mm.then_inc(ss_ready.sem, 1)

            def gemm2(m, x):
                b, before = use2(m)
                pe.wait_ge(*landed2(m))
                pe.wait_ge(freed[b].sem, before)
                w = ring[:, m % RING, :].rearrange("p (k m) -> p k m", k=KC)
                for c in range(2):
                    for k in range(KC):
                        mm = pe.matmul(G[b][:, c * S:(c + 1) * S], w[:, k, c * P:(c + 1) * P], x[:, k, :],
                                       start=(k == 0), stop=(k == KC - 1))
                mm.then_inc(unit_done.sem, 1)

            pe.wait_ge(con_in, 16)
            for lay in range(DEPTH):
                for kind, k in sched:
                    item(kind, k, lay)
            norm2(1)
            def modulation_columns(n):
                pe.wait_ge(ada_cp, n + 1)
                for c in range(4):
                    mm = pe.matmul(A[2][:, 4 * n + c:4 * n + c + 1], flat(ADA[n % 2], 2)[:, c * P:(c + 1) * P],
                                   c2("quarters", 0, 1), start=True, stop=True)
                return mm

            pe.wait_ge(cs_ok, 1)
            for m in range(ADA_UNITS):
                if m == 4:
                    norm2(2)
                if m % 2 == 0 and m >= 4:
                    modulation_columns(m // 2 - 2).then_inc(ada_mm, 1)
                pe.wait_ge(*landed2(m))
                w = ring[:, m % RING, :].rearrange("p (k m) -> p k m", k=KC)
                for k in range(2):
                    for g in range(4):
                        mm = pe.matmul(G[m // 2 % 2][32 * g:32 * g + 32, m % 2 * UC:(m % 2 + 1) * UC],
                                       mod[:, 64 + 2 * g + k:65 + 2 * g + k].broadcast_to([P, 32]), w[:, 2 * g + k, :],
                                       start=(k == 0), stop=(k == 1))
                mm.then_inc(unit_done.sem, 1)
            for n in (ADA_UNITS // 2 - 2, ADA_UNITS // 2 - 1):
                modulation_columns(n).then_inc(ada_mm, 1)
            pe.wait_ge(lam_in, 1)
            pe.matmul(A[3][:, 0:2], con[0:64, CON["ones"]:CON["ones"] + P], small[0:64, 0:2], start=True, stop=True)\
                .then_inc(lam_mm, 1)
            pe.wait_ge(u_ready.sem, u_ready.at(DEPTH, 2))
            for m in range(WIN2, WOUT2):
                gemm2(m, u)
                if m in (WIN2 + 5, WIN2 + 6):
                    n = m - WIN2 - 5
                    pe.wait_ge(pool_d, 1)
                    if n:
                        pe.wait_ge(pool_fin, 1)
                    for g in (2 * n, 2 * n + 1):
                        mm = pe.matmul(A[4][:, g % 2 * S:g % 2 * S + S], p2("w_pool", g * P, P), arena[:, RD + g, :],
                                       start=True, stop=True)
                    mm.then_inc(pool_mm, 1)
            for q in range(4):
                b, before = use2(q_unit(q))
                pe.wait_ge(freed[b].sem, before + 1)
                for c in range(2):
                    mm = pe.matmul(A[q][:, c * S:(c + 1) * S], c2("rot", 0, P), arena[:, Q2 + 2 * q + c, :],
                                   start=True, stop=True)
                mm.then_inc(rope_mm, 1)
            for q in range(2):
                b, before = use2(q_unit(4 + q))
                pe.wait_ge(freed[b].sem, before + 1)
            pe.wait_ge(rope_ok, 2)
            for i in range(T):
                for c in range(4):
                    mm = pe.transpose(A[i][:, c * P:(c + 1) * P], arena[:, V2 + c, i * P:(i + 1) * P], ident)
                mm.then_inc(v2T, 1)

            def scores(hd):
                if hd < 2:
                    pe.wait_ge(rope_ok, 4)
                    pe.wait_ge(v2T_cp, 2)
                else:
                    pe.wait_ge(sc_exp, 4 * (hd - 1))
                for i in range(T):
                    for c in range(2):
                        r = slice(64 * c, 64 * c + 64)
                        mm = pe.matmul(A[hd % 2 * 2 + c][:, i * S:(i + 1) * S], arena[r, Q2 + hd, i * P:(i + 1) * P],
                                       arena[r, K2 + hd, :], start=True, stop=True)
                mm.then_inc(sc_ok, 1)

            def values(hd):
                pe.wait_ge(w2_ok, hd + 1)
                if hd:
                    pe.wait_ge(w2T_cp, hd)
                for j in range(T):
                    for i in range(T):
                        mm = pe.transpose(A[4][:, j * S + i * P:j * S + (i + 1) * P],
                                          arena[:, WA[hd % 2] + i, j * P:(j + 1) * P], ident)
                mm.then_inc(w2T, 1)
                pe.wait_ge(w2T_cp, hd + 1)
                for j in range(T):
                    mm = pe.matmul(G[hd // 2][:, hd % 2 * S:hd % 2 * S + S], v2tok[:, j, hd * P:(hd + 1) * P],
                                   arena[:, WAT[hd % 2] + j, :], start=(j == 0), stop=(j == T - 1))
                mm.then_inc(o2_ok, 1)

            scores(0)
            scores(1)
            for hd in range(HEADS2):
                if hd == 0:
                    pe.wait_ge(pool_fin, 2)
                values(hd)
                if hd + 2 < HEADS2:
                    scores(hd + 2)
            pe.wait_ge(o2_sq, 1)
            for hd in range(HEADS2):
                mm = pe.matmul(A[hd // 2][:, hd % 2 * S:hd % 2 * S + S], ones, arena[:, SQ + hd, :], start=True, stop=True)
            mm.then_inc(o2_ss, 1)
            pe.wait_ge(o2_fin, 1)
            pe.wait_ge(pool_fin, 2)
            for m in range(WOUT2, ROUTER):
                gemm2(m, chunks(O2, KC))
            norm2(3)
            pe.wait_ge(u_ready.sem, u_ready.at(DEPTH, 3))
            pe.wait_ge(*landed2(ROUTER))
            w = ring[:, ROUTER % RING, :].rearrange("p (k m) -> p k m", k=KC)
            for i in range(T):
                o = A[0][:, i * 64:i * 64 + 36]
                for k in range(KC):
                    pe.matmul(o, u[:, k, i * P:(i + 1) * P], w[:, k, 0:36], start=(k == 0), stop=False)
                mm = pe.matmul(o, con[0:1, CON["ones"]:CON["ones"] + P], p2("b_route", 0, 36)[0:1], start=False, stop=True)
            mm.then_inc(unit_done.sem, 1)

            for q in range(4):
                for c in range(4):
                    mm = pe.transpose(A[1 + q][:, c * P:(c + 1) * P], u[:, q % 2 * 4 + c, q // 2 * P:(q // 2 + 1) * P], ident)
                mm.then_inc(utT, 1)
            pe.wait_ge(r_mem, 1)
            member = flat(MEMBER, 1)[:, 0:64].rearrange("p (i n) -> p i n", i=T)
            for i in range(T):
                for j in range(T):
                    pe.matmul(A[0][:, 256 + 32 * i:288 + 32 * i], cn("fw", j * S + i * P, j * S + (i + 1) * P), member[:, j],
                              start=(j == 0), stop=(j == T - 1))
            for j in range(T):
                mm = pe.matmul(A[0][:, 320:352], ones, member[:, j], start=(j == 0), stop=(j == T - 1))
            mm.then_inc(r_cum, 1)

            def dense():
                moe_units((0, 0), 0, None, False)
                pe.wait_ge(r_w, 1)
                pe.wait_ge(utT_cp, 4)
                for i in range(T):
                    mm = pe.transpose(A[1][0:32, i * P:(i + 1) * P], small[:, 128 + 32 * i:160 + 32 * i], ident)
                mm.then_inc(r_T, 1)
                pe.wait_ge(r_wT, 1)
                for q in range(EXPERTS // 2):
                    if q >= 4:
                        pe.wait_ge(wb_cp, q - 3)
                    for a in range(2):
                        e = 2 * q + a
                        mm = pe.matmul(A[q % 4][:, a * S:(a + 1) * S], ident[0:32, e:e + 1].broadcast_to([32, P]),
                                       rowt[:, :], start=True, stop=True)
                    mm.then_inc(wb_mm, 1)
                pe.wait_ge(wb_cp, EXPERTS // 2)
                moe_units((0, 4), 1, (0, 0), True)
                with pe.Fori(0, (EXPERTS - 2) // 2) as i:
                    for a in range(2):
                        moe_units((i * 2 + a, 10), i * 2 + (a + 2), (i * 2 + (a + 1), (a + 1) % 2), False)
                moe_units((0, UNITS2 - MOE - 2), None, (EXPERTS - 1, 1), False)

            def pick_tokens(q, n):
                if n or not isinstance(q, int) or q:
                    pe.wait_ge(x_cp, q * 2 + n)
                for c in range(4):
                    for i in range(T):
                        mm = pe.matmul(G[1][:, c * P:(c + 1) * P], utok[:, i, (4 * n + c) * P:(4 * n + c + 1) * P],
                                       pick2[:, i, q, :], start=(i == 0), stop=(i == T - 1))
                mm.then_inc(x_mm, 1)

            def slot_gate_up(r, c):
                at = 6 * c - 2 if c or not isinstance(r, int) else 0
                a = c % 2
                pe.wait_ge(x_cp, r + (c - a + 2))
                if c or not isinstance(r, int):
                    pe.wait_ge(hs_ok, r + c)
                for j in range(4):
                    m = at + j
                    pe.wait_ge(e_landed[m % ERING], (r + (m // ERING + 1)) * 16)
                    w = e_slot(m).rearrange("p (k m) -> p k m", k=2)
                    for k in range(2):
                        for g in range(2):
                            mm = pe.matmul(G[0][g * 64:(g + 1) * 64, :], xe[:, 2 * j + k, a * SLOTS:(a + 1) * SLOTS],
                                           w[:, k, g * 512:(g + 1) * 512], start=(j == k == 0), stop=(j == 3 and k == 1),
                                           skip_group_check=True)
                    mm.then_inc(unit_done.sem, 1)

            def slot_turn(r, c):
                pe.wait_ge(hs_ok, r + (c + 1))
                if c or not isinstance(r, int):
                    pe.wait_ge(ht_cp, r + c)
                for k in range(4):
                    mm = pe.matmul(A[4][:, k * SLOTS:(k + 1) * SLOTS], flat(HSE, 2)[0:SLOTS, k * P:(k + 1) * P],
                                   ident[0:SLOTS, 0:SLOTS], start=True, stop=True)
                mm.then_inc(ht_mm, 1)

            def slot_down(r, c):
                pe.wait_ge(ht_cp, r + (c + 1))
                if c or not isinstance(r, int):
                    pe.wait_ge(ye_cp, r + c)
                for j in range(2):
                    m = (6 * c + 8 if c < EXPERTS - 1 else 6 * c + 4) + j
                    pe.wait_ge(e_landed[m % ERING], (r + (m // ERING + 1)) * 16)
                    w = e_slot(m).rearrange("p (k m) -> p k m", k=2)
                    for k in range(2):
                        for g in range(2):
                            mm = pe.matmul(G[2][g * 64:(g + 1) * 64, :], hte[:, 2 * j + k, :],
                                           w[:, k, g * 512:(g + 1) * 512], start=(j == k == 0), stop=(j == 1 and k == 1),
                                           skip_group_check=True)
                    mm.then_inc(unit_done.sem, 1)

            def slot_sum(r, c):
                pe.wait_ge(ye_cp, r + (c + 1))
                pe.wait_ge(wn_cp, r + (c + 1))
                start = isinstance(r, int) and c == 0
                for n in range(4):
                    for g in range(2):
                        ch = 4 * g + n
                        row = slice(64 * g, 64 * g + 64)
                        mm = pe.matmul(A[ch // 2][:, ch % 2 * S:ch % 2 * S + S], flat(YE, 2)[row, n * P:(n + 1) * P],
                                       arena[row, WNOW[c % 2], :], start=(start and n % 2 == 0), stop=False, skip_group_check=True)
                mm.then_inc(s_sum, 1)

            def compact():
                pe.wait_ge(pick_ok, 1)
                pe.wait_ge(utT_cp, 4)
                pick_tokens(0, 0)
                pick_tokens(0, 1)
                slot_gate_up(0, 0)
                slot_gate_up(0, 1)
                pe.wait_ge(pickw_ok, 1)
                for q in range(PAIRS):
                    if q >= 4:
                        pe.wait_ge(ws_cp, q - 3)
                    for a in range(2):
                        for i in range(T):
                            for g in range(2):
                                mm = pe.matmul(A[q % 4][g * 64:(g + 1) * 64, a * S + i * P:a * S + (i + 1) * P],
                                               pickw[:, i, 2 * q + a, :], ident, start=True, stop=True)
                    mm.then_inc(ws_mm, 1)
                slot_turn(0, 0)
                pick_tokens(1, 0)
                pick_tokens(1, 1)
                slot_down(0, 0)
                slot_gate_up(0, 2)
                slot_turn(0, 1)
                pe.wait_ge(ws_cp, PAIRS)
                slot_sum(0, 0)
                slot_down(0, 1)
                with pe.Fori(0, PAIRS - 2) as i:
                    slot_gate_up(i * 2, 3)
                    pick_tokens(i + 2, 0)
                    slot_turn(i * 2, 2)
                    pick_tokens(i + 2, 1)
                    slot_sum(i * 2, 1)
                    slot_down(i * 2, 2)
                    slot_gate_up(i * 2, 4)
                    slot_turn(i * 2, 3)
                    slot_sum(i * 2, 2)
                    slot_down(i * 2, 3)
                slot_gate_up(0, EXPERTS - 1)
                slot_turn(0, EXPERTS - 2)
                slot_sum(0, EXPERTS - 3)
                slot_down(0, EXPERTS - 2)
                slot_turn(0, EXPERTS - 1)
                slot_sum(0, EXPERTS - 2)
                slot_down(0, EXPERTS - 1)
                slot_sum(0, EXPERTS - 1)

            def moe_units(first, e_gate, e_down, start):
                six, rest = first
                n = 0
                if e_gate is not None:
                    for j in range(3):
                        pe.wait_ge(freed[j].sem, e_gate + G2)
                    if not isinstance(e_gate, int) or e_gate:
                        pe.wait_ge(e4_freed, e_gate)
                for j in range(4) if e_gate is not None else ():
                    at = rest + n
                    pe.wait_ge(e_landed[at % ERING], (six + (at // ERING + 1)) * 16)
                    w = e_slot(at).rearrange("p (k m) -> p k m", k=2)
                    for b in range(4):
                        for c in range(2):
                            for k in range(2):
                                mm = pe.matmul(E4[b][:, c * S:(c + 1) * S], w[:, k, c * 512 + b * P:c * 512 + (b + 1) * P],
                                               u[:, 2 * j + k, :], start=(j == c == k == 0), stop=(j == 3 and k == 1),
                                               skip_group_check=True)
                    mm.then_inc(unit_done.sem, 1)
                    n += 1
                if e_down is None:
                    return
                e, par_e = e_down
                pe.wait_ge(hide_ok, (e + 1) * 4)
                for j in range(2):
                    at = rest + n
                    pe.wait_ge(e_landed[at % ERING], (six + (at // ERING + 1)) * 16)
                    w = e_slot(at).rearrange("p (k m) -> p k m", k=2)
                    for ch in range(KC):
                        for k in range(2):
                            mm = pe.matmul(A[ch // 2][:, ch % 2 * S:ch % 2 * S + S], w[:, k, ch * P:(ch + 1) * P],
                                           arena[:, HIDE[par_e] + 2 * j + k, :],
                                           start=(start and ch % 2 == 0 and j == k == 0),
                                           stop=False, skip_group_check=True)
                    mm.then_inc(unit_done.sem, 1)
                    n += 1

            pe.wait_ge(path_ok, 1)
            some_over = pe.value_load(path[0:1, 0:1].bitcast(I32), min_val=0, max_val=ONE_BITS)
            with pe.If(some_over != 0):
                dense()
            with pe.Else():
                compact()
            norm2(4)

        @block.scalar
        def _(act):
            st = Steps(act, act_step)

            def unit(lay, n):
                kind, j = KINDS[n], n - OF[KINDS[n]]
                j = j // 2 if kind in ("gs", "bs") else j
                if kind in ("bs", "bh", "bm", "out", "down"):
                    return
                act.wait_ge(unit_done.sem, unit_done.at(lay, n + 1))
                if kind == "ple":
                    for q in range(4):
                        a = act.activation(flat(PLE + 2 * q, 2), A[q][:, :], ACT.Copy)
                    a.then_inc(ple_cp.sem, 1)
                    return
                bank, f = G[USE[n] % GBANKS], freed[USE[n] % GBANKS]
                if kind == "rows":
                    act.activation(rows[:, :], bank[0:96, 0:S], ACT.Identity, bias=pc("row_b")[0:96]).then_inc(f.sem, 1)
                elif kind in ("xbc", "up"):
                    conv = kind == "xbc"
                    if not conv and j >= 2:
                        act.wait_ge(hid_ok.sem, hid_ok.at(lay, j - 1))
                    for c in range(2):
                        if conv:
                            ch, width, wn, bn, dst = 2 * j + c, SSD_CONV, "conv_w", "conv_b", XBC + 2 * j + c
                        else:
                            ch, width, wn, bn, dst = j + FC * c, FFN_CONV, "fconv_w", "fconv_b", FT[j % 2] + c
                        a = act.activation(arena[:, dst, :], bank[:, c * S:(c + 1) * S], ACT.Identity,
                                           scale=pc(wn, ch * width + width // 2), bias=pc(bn, ch))
                    a.then_inc(center.sem, 1)
                else:
                    dst = {"z": Z, "hf": HF, "hq": HQ, "hi": HV, "hg": HG, "mq": MQ, "mk": MK, "mv": MV, "mo": MO,
                           "gs": MERGED, "gh": GH, "gm": GM, "pleg": PLG}[kind]
                    func = {"z": ACT.Silu, "gs": ACT.Sigmoid, "gh": ACT.Sigmoid, "gm": ACT.Sigmoid,
                            "pleg": ACT.Sigmoid}.get(kind, ACT.Copy)
                    at = dst + 2 * j
                    if kind == "mo" and j == 0:
                        act.wait_ge(ys_fin.sem, ys_fin.at(lay, 1))
                    act.activation(flat(at, 2), bank[:, :], func).then_inc(f.sem, 1)

            def rstd_of(src, log, outp, n, ready):
                st.done(act.activation(log, src, ACT.Ln, scale=1.0 / n, bias=eps[:, 0:1]))
                st.wait()
                act.activation(outp, log, ACT.Exp, scale=-0.5).then_inc(ready.sem, 1)

            def keep_h():
                act.activation(h[:].rearrange("p c s -> p (c s)"), flat(PLG, KC), ACT.Copy).then_inc(h_fin.sem, 1)

            def item(kind, k, lay):
                if kind in ("unit", "read"):
                    unit(lay, k)
                elif kind == "norm":
                    for j in range(4):
                        x = h[:, 2 * j:2 * j + 2, :].rearrange("p c s -> p (c s)")
                        if k == 1:
                            act.wait_ge(*evac(lay, OF["out"] + j))
                        elif lay:
                            act.wait_ge(h_new.sem, h_new.at(lay - 1, j + 1))
                            x = flat(PLG + 2 * j, 2)
                        else:
                            act.wait_ge(x_in, 16)
                        act.activation(flat(SQ + 2 * j, 2), x, ACT.Square).then_inc(sq_ready.sem, 1)
                    act.wait_ge(ss_ready.sem, ss_ready.at(lay, k + 1))
                    rstd_of(A[4][:, 0:S], rstd[:, 0, 0, :], rstd[:, 1, 0, :], D, rs_ready)
                    if lay and k == 0:
                        keep_h()
                    for j in range(4 * k):
                        act.wait_ge(u_ready.sem, u_ready.at(lay, KC + 2 * j + 2))
                        act.activation(flat_r(UHI + 2 * j, 2), u[:, 2 * j:2 * j + 2, :].rearrange("p c s -> p (c s)"),
                                       ACT.Copy).then_inc(uhi_ok.sem, 1)
                elif kind == "lb":
                    act.wait_ge(par_in, 16 * (lay + 1))
                    act.activation(nega[:, 0:1], pc("a_log")[0:32], ACT.Exp).then_inc(nega_exp.sem, 1)
                    act.wait_ge(lb_in.sem, lb_in.at(lay, 1))
                    act.activation(small[:, 48:80], small[:, 16:48], ACT.Exp).then_inc(lb_exp.sem, 1)
                elif kind == "rows":
                    act.wait_ge(sp_abs.sem, sp_abs.at(lay, 1))
                    st.done(act.activation(rtmp[:, 1, :], rtmp[:, 0, :], ACT.Exp, scale=-1.0))
                    st.wait()
                    act.activation(rtmp[:, 0, :], rtmp[:, 1, :], ACT.Ln, bias=1.0).then_inc(sp_ln.sem, 1)
                elif kind == "rows2":
                    act.wait_ge(m_ok.sem, m_ok.at(lay, 1))
                    act.activation(mrow[0:8, 0], mrow[0:8, 1], ACT.Exp, scale=-1.0).then_inc(em_ok.sem, 1)
                elif kind == "silu_x":
                    act.wait_ge(*evac(lay, last("xbc")))
                    act.activation(flat(XBC, 12), flat(XBC, 12), ACT.Silu).then_inc(xs_ok.sem, 1)
                elif kind == "bc":
                    act.wait_ge(arg_ok.sem, arg_ok.at(lay, k + 1))
                    act.activation(flat(SE[k % 2], 3), flat(SE[k % 2], 3), ACT.Exp).then_inc(exp_ok.sem, 1)
                elif kind == "hprep":
                    act.wait_ge(*evac(lay, last("hg")))
                    st.done(act.activation(flat(HK, 16), flat(HF, 16), ACT.Sigmoid, scale=-1.0))
                    st.wait()
                    act.activation(flat(HF, 16), flat(HF, 16), ACT.Sigmoid).then_inc(hsig.sem, 1)
                    act.activation(flat(HQ, KC), flat(HQ, KC), ACT.Silu)
                    act.activation(flat(HG, KC), flat(HG, KC), ACT.Silu).then_inc(hsilu.sem, 1)
                elif kind == "ssd_norm":
                    act.wait_ge(yz_ok.sem, yz_ok.at(lay, 1))
                    act.activation(flat(XBC, KC), flat(Z, KC), ACT.Square).then_inc(ysq.sem, 1)
                    act.wait_ge(yss.sem, yss.at(lay, 1))
                    rstd_of(A[0][:, :], rstd[:, 0].rearrange("p a s -> p (a s)"),
                            rstd[:, 1].rearrange("p a s -> p (a s)"), D // 2, yrs)
                elif kind == "hlog":
                    act.wait_ge(hclamp.sem, hclamp.at(lay, 1))
                    act.activation(flat(HF, 16), flat(HF, 16), ACT.Ln)
                    act.activation(flat(HE[0], 16), flat(HE[0], 16), ACT.Ln, scale=1.0 / LN_FLOOR).then_inc(hln.sem, 1)
                elif kind == "hgA":
                    b, l = divmod(k, 9)
                    if l == 0:
                        return
                    act.wait_ge(hargs.sem, hargs.at(lay, 8 * b + l))
                    m = 1 << (l - 1)
                    e = HE[k % 2]
                    act.activation(half(flat(e, 4), m, 1), half(flat(HF + 4 * b, 4), m, 1), ACT.Exp)
                    act.activation(half(flat(e, 4), m, 0), half(flat(HF + 8 + 4 * b, 4), m, 0), ACT.Exp)
                    act.activation(flat(e + 4, 4), flat(e + 4, 4), ACT.Exp).then_inc(hexp.sem, 1)
                elif kind == "ho":
                    for n in (2 * k, 2 * k + 1):
                        act.wait_ge(ho_ok.sem, ho_ok.at(lay, n + 1))
                        act.activation(flat(HQ + 2 * n, 2), A[4][:, :], ACT.Copy).then_inc(ho_cp.sem, 1)
                elif kind == "hnorm":
                    act.wait_ge(ho_cp.sem, ho_cp.at(lay, 4))
                    act.activation(flat(HE[0], KC), flat(HQ, KC), ACT.Square).then_inc(hsq.sem, 1)
                    act.wait_ge(hss.sem, hss.at(lay, 1))
                    for q in range(4):
                        a = act.activation(flat(HE[1] + 2 * q, 2), A[q][:, :], ACT.Ln, scale=1.0 / P, bias=eps[:, 0:1])
                    st.done(a)
                    st.wait()
                    act.activation(flat(HE[1], KC), flat(HE[1], KC), ACT.Exp, scale=-0.5).then_inc(hrs.sem, 1)
                elif kind == "mvt":
                    act.wait_ge(*evac(lay, last("mo")))
                    act.activation(flat(MO, KC), flat(MO, KC), ACT.Sigmoid).then_inc(msig.sem, 1)
                elif kind == "mlA":
                    act.wait_ge(marg.sem, marg.at(lay, k + 1))
                    act.activation(flat(ME[k % 2], 3), flat(ME[k % 2], 3), ACT.Exp).then_inc(mexp.sem, 1)
                elif kind == "mlnorm":
                    act.wait_ge(mcen.sem, mcen.at(lay, 1))
                    act.activation(flat(SQ, KC), flat(HSUM, KC), ACT.Square).then_inc(msq.sem, 1)
                    act.wait_ge(mvar.sem, mvar.at(lay, 1))
                    rstd_of(small[:, 16:32], small[:, 32:48], small[:, 48:64], P, mrs)
                elif kind == "split":
                    i = k - OF["up"]
                    act.wait_ge(landed[k % RING], 16 * (lay * (UNITS // RING) + k // RING + 1))
                    if i >= 3:
                        act.wait_ge(unit_done.sem, unit_done.at(lay, k - 2))
                    act.activation(flat_r(WHI[i % 3], KC), ring[:, k % RING, :], ACT.Copy).then_inc(whi_ok.sem, 1)
                elif kind == "hsplit":
                    act.wait_ge(hid_ok.sem, hid_ok.at(lay, k + 1))
                    act.activation(flat_r(HIDHI + k, 1), arena[:, HID + k, :], ACT.Copy)\
                        .then_inc(hhi_ok.sem, 1)
                elif kind == "hid":
                    act.wait_ge(*evac(lay, OF["up"] + k))
                    act.activation(arena[:, FT[k % 2], :], arena[:, FT[k % 2], :], ACT.Silu).then_inc(silu_ok.sem, 1)

            def norm2(n):
                x = h[:].rearrange("p c s -> p (c s)")
                for j in range(4):
                    if n == 1:
                        act.wait_ge(h_new.sem, h_new.at(DEPTH - 1, j + 1))
                        x = flat(PLG, KC)
                    elif n == 3:
                        act.wait_ge(freed[(WOUT2 - WIN2 + j) % GBANKS].sem, use2(WOUT2 + j)[1] + 1)
                    act.activation(flat(SQ + 2 * j, 2), x[:, j * 512:(j + 1) * 512], ACT.Square).then_inc(sq_ready.sem, 1)
                act.wait_ge(ss_ready.sem, ss_ready.at(DEPTH, n))
                rstd_of(A[4][:, 0:S], rstd[:, 0, 0, :], rstd[:, 1, 0, :], D, rs_ready)

            act.dma_start(h[:].rearrange("p c s -> p (c s)"), x_d).then_inc(x_in, 16)
            act.wait_ge(eps_set, 1)
            for lay in range(DEPTH):
                for kind, k in sched:
                    item(kind, k, lay)
            norm2(1)
            act.wait_ge(par2_in, 32)
            act.activation(mod[:, 64:72], p2("c", 0, 8), ACT.Silu).then_inc(cs_ok, 1)
            for n in range(ADA_UNITS // 2):
                if n == 1:
                    act.wait_ge(u_ready.sem, u_ready.at(DEPTH, 1))
                    norm2(2)
                act.wait_ge(*done2(2 * n + 1))
                if n >= 2:
                    act.wait_ge(ada_mm, n - 1)
                act.activation(flat(ADA[n % 2], 2), G[n % 2][:, :], ACT.Copy).then_inc(ada_cp, 1)
            act.wait_ge(lam_mm, 1)
            act.activation(small[:, 2:4], A[3][:, 0:2], ACT.Exp).then_inc(lam_exp, 1)
            for m in range(WIN2, WOUT2):
                act.wait_ge(*done2(m))
                b, before = use2(m)
                act.activation(flat(Q2 + 2 * WIN_ORDER[m - WIN2], 2), G[b][:, :], ACT.Copy).then_inc(freed[b].sem, 1)

            def exps(hd):
                act.wait_ge(sc_max, hd + 1)
                for i in range(T):
                    for c in range(2):
                        n = 4 * (hd % 2) + 2 * c + i
                        act.activation(arena[:, EA[hd % 2] + 2 * c + i, :], A[hd % 2 * 2 + c][:, i * S:(i + 1) * S], ACT.Exp,
                                       scale=HD2 ** -0.5, bias=small[:, 8 + n:9 + n],
                                       accum_out=small[:, 16 + n:17 + n]).then_inc(sc_exp, 1)

            for hd in range(HEADS2):
                if hd >= 2:
                    act.wait_ge(w2_ok, hd - 1)
                exps(hd)
            for n in range(2):
                act.wait_ge(o2_ok, 2 * n + 2)
                st.done(act.activation(flat(O2 + 2 * n, 2), G[n][:, :], ACT.Copy))
            st.wait()
            act.activation(flat(SQ, 4), flat(O2, 4), ACT.Square).then_inc(o2_sq, 1)
            act.wait_ge(o2_ss, 1)
            for n in range(2):
                a = act.activation(flat(RD + 2 * n, 2), A[n][:, :], ACT.Ln, scale=1.0 / P, bias=eps[:, 0:1])
            st.done(a)
            st.wait()
            act.activation(flat(RD, 4), flat(RD, 4), ACT.Exp, scale=-0.5).then_inc(o2_rs, 1)
            norm2(3)
            act.wait_ge(r_sh, 1)
            act.activation(small[:, 8:16], small[:, 0:8], ACT.Exp).then_inc(r_exp, 1)
            act.wait_ge(r_sh, 2)
            act.activation(small[:, 18:20], small[:, 16:18], ACT.Exp).then_inc(r_exp, 1)

            def dense():
                act.wait_ge(*done2(MOE + 3))
                for j in range(4):
                    act.activation(arena[:, SG2 + j, :], E4[j][:, 0:S], ACT.Silu).then_inc(gate_ok, 1)
                with act.Fori(0, EXPERTS - 1) as e:
                    act.wait_ge(unit_done.sem, e * 6 + (B2 + MOE + 8))
                    for j in range(4):
                        act.wait_ge(hide_ok, e * 4 + (j + 1))
                        act.activation(arena[:, SG2 + j, :], E4[j][:, 0:S], ACT.Silu).then_inc(gate_ok, 1)

            def slots_in(q, n):
                act.wait_ge(x_mm, q * 2 + (n + 1))
                act.activation(flat(XE + 2 * n, 2), G[1][:, :], ACT.Copy).then_inc(x_cp, 1)

            def gate(r, c):
                act.wait_ge(unit_done.sem, r * 6 + (B2 + MOE + (6 * c + 2 if c or not isinstance(r, int) else 4)))
                if c or not isinstance(r, int):
                    act.wait_ge(hs_ok, r + c)
                act.activation(flat(SGE, 2)[0:SLOTS], G[0][0:SLOTS, :], ACT.Silu).then_inc(sg_ok, 1)

            def outputs(r, c):
                act.wait_ge(unit_done.sem, r * 6 + (B2 + MOE + (6 * c + 10 if c < EXPERTS - 1 else 6 * EXPERTS)))
                if c or not isinstance(r, int):
                    act.wait_ge(ye_cp, r + c)
                act.activation(flat(YE, 2), G[2][:, :], ACT.Copy).then_inc(ye_cp, 1)

            def compact():
                slots_in(0, 0)
                slots_in(0, 1)
                gate(0, 0)
                for q in range(PAIRS):
                    act.wait_ge(ws_mm, q + 1)
                    act.activation(flat(WS + 2 * q, 2), A[q % 4][:, :], ACT.Copy).then_inc(ws_cp, 1)
                gate(0, 1)
                slots_in(1, 0)
                slots_in(1, 1)
                outputs(0, 0)
                gate(0, 2)
                outputs(0, 1)
                with act.Fori(0, PAIRS - 2) as i:
                    gate(i * 2, 3)
                    slots_in(i + 2, 0)
                    slots_in(i + 2, 1)
                    outputs(i * 2, 2)
                    gate(i * 2, 4)
                    outputs(i * 2, 3)
                gate(0, EXPERTS - 1)
                outputs(0, EXPERTS - 2)
                outputs(0, EXPERTS - 1)

            act.wait_ge(path_ok, 1)
            some_over = act.value_load(path[0:1, 0:1].bitcast(I32), min_val=0, max_val=ONE_BITS)
            with act.If(some_over != 0):
                dense()
            with act.Else():
                compact()
            act.wait_ge(y2_fin, 1)
            norm2(4)

        @block.vector
        def _(dve):
            st = Steps(dve, dve_step)
            V = nc.vector
            stt, tt, ts = V.scalar_tensor_tensor, V.tensor_tensor, V.tensor_scalar

            def taps(lay, n, width, wn, chans, dsts):
                bank, f = G[USE[n] % GBANKS], freed[USE[n] % GBANKS]
                offs = [j for j in range(width) if j != width // 2]
                for a, j in enumerate(offs):
                    d = j - width // 2
                    lo, hi = max(0, -d), S - max(0, d)
                    for c in range(2):
                        if a:
                            st.wait(back=1)
                        o = arena[:, dsts[c], lo:hi]
                        ins = stt(o, bank[:, c * S + lo + d:c * S + hi + d], pc(wn, chans[c] * width + j), o,
                                  ALU.mult, ALU.add)
                        if j == offs[-1] and c == 1:
                            st.wait()
                            ins.then_inc(f.sem, 1)
                        else:
                            st.done(ins)

            def unit(lay, n):
                kind, j = KINDS[n], n - OF[KINDS[n]]
                j = j // 2 if kind in ("gs", "bs") else j
                if kind not in ("bs", "bh", "bm", "out", "down", "xbc", "up"):
                    return
                if kind == "down" and j % 3 != 2:
                    return
                if kind == "xbc":
                    dve.wait_ge(center.sem, center.at(lay, j + 1))
                    taps(lay, n, SSD_CONV, "conv_w", (2 * j, 2 * j + 1), (XBC + 2 * j, XBC + 2 * j + 1))
                    return
                if kind == "up":
                    dve.wait_ge(center.sem, center.at(lay, 6 + j + 1))
                    taps(lay, n, FFN_CONV, "fconv_w", (j, j + FC), (FT[j % 2], FT[j % 2] + 1))
                    return
                dve.wait_ge(unit_done.sem, unit_done.at(lay, n + 1))
                bank, f = G[USE[n] % GBANKS], freed[USE[n] % GBANKS]
                if kind in ("out", "down"):
                    j = j // 3 if kind == "down" else j
                    o = h[:, 2 * j:2 * j + 2, :].rearrange("p c s -> p (c s)")
                    tt(o, bank[:, :], o, ALU.add).then_inc(f.sem, 1)
                elif kind == "bs":
                    dve.wait_ge(*evac(lay, n - 1))
                    tt(flat(MERGED + 2 * j, 2), bank[:, :], flat(MERGED + 2 * j, 2), ALU.mult).then_inc(f.sem, 1)
                else:
                    g = {"bh": GH, "bm": GM}[kind] + 2 * j
                    if j == 0:
                        dve.wait_ge(*evac(lay, last("gm")))
                    tt(flat(g, 2), bank[:, :], flat(g, 2), ALU.mult).then_inc(f.sem, 1)
                    dve.wait_ge(*evac(lay, n))
                    m = flat(MERGED + 2 * j, 2)
                    ins = tt(m, m, flat(g, 2), ALU.add)
                    if kind == "bm" and j == 3:
                        st.wait()
                        ins.then_inc(merge_ok.sem, 1)
                    else:
                        st.done(ins)

            def decay_args(e, bank, col, ready):
                w = flat(e, 3)
                for i, d, lo, hi, at, mask in ((0, 0, 0, 256, 0, cn("mf", 0, 256)), (0, 1, 0, 128, 256, cn("mb", 128, 256)),
                                               (1, 0, 128, 256, 384, cn("mf", 0, 128)), (1, 1, 0, 256, 512, cn("mb", 0, 256))):
                    ins = stt(w[:, at:at + hi - lo], bank[:, d * S + lo:d * S + hi], ntok[:, i, col(d):col(d) + 1], mask,
                              ALU.add, ALU.min)
                ins.then_inc(ready.sem, 1)

            def item(kind, k, lay):
                if kind in ("unit", "read"):
                    unit(lay, k)
                elif kind == "norm":
                    dve.wait_ge(rs_ready.sem, rs_ready.at(lay, k + 1))
                    if k == 0:
                        dve.wait_ge(par_in, 16 * (lay + 1))
                    x = chunks(PLG, KC) if lay and k == 0 else h
                    for c in range(KC):
                        stt(u[:, c, :], x[:, c, :], pc(("mix_g", "ffn_g")[k], c), rstd[:, 1, 0, :], ALU.mult, ALU.mult)\
                            .then_inc(u_ready.sem, 1)
                    for j in range(4 * k):
                        dve.wait_ge(uhi_ok.sem, uhi_ok.at(lay, j + 1))
                        x = u[:, 2 * j:2 * j + 2, :].rearrange("p c s -> p (c s)")
                        ins = tt(u_r[:, 2 * j:2 * j + 2, :].rearrange("p c s -> p (c s)"), x,
                                 flat_r(UHI + 2 * j, 2).bitcast(F32), ALU.subtract)
                    if k:
                        ins.then_inc(ulo_ok.sem, 1)
                elif kind == "lb":
                    raw = [par[:, PAR["lb_raw"] + 16 * i:PAR["lb_raw"] + 16 * i + 16] for i in range(DEPTH)]
                    st.done(tt(small[:, 0:16], raw[0], raw[1], ALU.max))
                    st.wait()
                    st.done(tt(small[:, 16:32], raw[0], small[:, 0:16], ALU.subtract))
                    st.wait()
                    tt(small[:, 32:48], raw[1], small[:, 0:16], ALU.subtract).then_inc(lb_in.sem, 1)
                    dve.wait_ge(lb_exp.sem, lb_exp.at(lay, 1))
                    st.done(tt(small[:, 80:96], small[:, 48:64], small[:, 64:80], ALU.add))
                    st.wait()
                    st.done(V.reciprocal(small[:, 96:112], small[:, 80:96]))
                    st.wait()
                    st.done(tt(small[:, 112:128], small[:, 48:64], small[:, 96:112], ALU.mult))
                    st.done(tt(small[:, 128:144], small[:, 64:80], small[:, 96:112], ALU.mult))
                    st.wait()
                    st.done(stt(lb[:, 2, :], small[:, 112:128], pc("lb_mask", 0), small[:, 112:128], ALU.mult, ALU.subtract))
                    st.wait()
                    st.done(stt(lb[:, 0, :], small[:, 128:144], pc("lb_mask", 1), lb[:, 2, :], ALU.mult, ALU.add))
                    st.wait()
                    st.done(ts(lb[:, 1, :], lb[:, 0, :], -1.0, 1.0, ALU.mult, ALU.add))
                    dve.wait_ge(nega_exp.sem, nega_exp.at(lay, 1))
                    st.done(ts(nega[:, 1:2], nega[:, 0:1], -1.0, None, ALU.mult))
                elif kind == "rows":
                    dve.wait_ge(*evac(lay, 0))
                    stt(rtmp[:, 0, :], rows[:, :], -1.0, rows[:, :], ALU.mult, ALU.max).then_inc(sp_abs.sem, 1)
                    dve.wait_ge(sp_ln.sem, sp_ln.at(lay, 1))
                    st.done(stt(dtr[:, :], rows[0:32, :], 0.0, rtmp[0:32, 0, :], ALU.max, ALU.add))
                    st.wait()
                    st.done(ts(rows[0:32, :], dtr[:, :], nega[:, 1:2], None, ALU.mult))
                    st.wait()
                    stt(rows[64:80, :], rows[64:80, :], 0.0, rtmp[64:80, 0, :], ALU.min, ALU.subtract)\
                        .then_inc(rows_ok.sem, 1)
                elif kind == "rows1":
                    dve.wait_ge(rowsT.sem, rowsT.at(lay, 1))
                    V.tensor_copy(tok[:].rearrange("p i n -> p (i n)"), A[3][:, 0:2 * P]).then_inc(tok_ok.sem, 1)
                elif kind == "rows2":
                    dve.wait_ge(tok_ok.sem, tok_ok.at(lay, 1))
                    dve.wait_ge(cum_ok.sem, cum_ok.at(lay, 1))
                    sums = A[2][:, 0:96].rearrange("p (i n) -> p i n", i=T)
                    st.done(ts(ntok[:, :, 0:32], sums[:, :, 0:32], -1.0, None, ALU.mult))
                    st.done(tt(ntok[:, :, 32:48], tok[:, :, 32:48], sums[:, :, 32:48], ALU.subtract))
                    dve.wait_ge(cum_ok.sem, cum_ok.at(lay, 2))
                    st.done(V.tensor_copy(arow[:].rearrange("p d s -> p (d s)"), A[1][0:16, :]))
                    dve.wait_ge(cum_ok.sem, cum_ok.at(lay, 3))
                    r = [mrow[0:8, i].rearrange("p d s -> p (d s)") for i in range(4)]
                    st.done(V.tensor_copy(r[0], A[0][0:8, :]))
                    st.wait()
                    st.done(tt(r[1], A[4][0:8, :], r[0], ALU.subtract))
                    st.wait()
                    f, b, o, ob = mrow[0:8, 1, 0, :], mrow[0:8, 1, 1, ::-1], mrow[0:8, 2, 0, :], mrow[0:8, 2, 1, ::-1]
                    st.done(V.tensor_tensor_scan(o, f, f, NEG, ALU.max, ALU.bypass))
                    st.done(V.tensor_tensor_scan(ob, b, b, NEG, ALU.max, ALU.bypass))
                    st.wait()
                    st.done(ts(r[3], r[2], -1.0, None, ALU.mult))
                    tt(r[1], r[0], r[2], ALU.add).then_inc(m_ok.sem, 1)
                elif kind == "rows3":
                    dve.wait_ge(emT.sem, emT.at(lay, 1))
                    st.wait()
                    V.tensor_copy(etok[:].rearrange("p i d n -> p (i d n)"), A[3][:, 0:32]).then_inc(rows_fin.sem, 1)
                elif kind == "xs_turn":
                    for q in range(4):
                        dve.wait_ge(xT.sem, xT.at(lay, q + 1))
                        V.tensor_copy(xtok[:, q // 2, q % 2 * 512:q % 2 * 512 + 512], A[q][:, :]).then_inc(xT_cp.sem, 1)
                elif kind == "cb":
                    for g in range(2):
                        dve.wait_ge(cb_ok.sem, cb_ok.at(lay, g + 1))
                        V.tensor_copy(flat(CB + 2 * g, 2), A[g][:, :]).then_inc(cb_cp.sem, 1)
                elif kind == "bc":
                    if k == 0:
                        st.wait()
                        dve.wait_ge(rows_fin.sem, rows_fin.at(lay, 1))
                    if k >= 2:
                        dve.wait_ge(att_ok.sem, att_ok.at(lay, k - 1))
                    dve.wait_ge(bc_ok.sem, bc_ok.at(lay, k + 1))
                    decay_args(SE[k % 2], A[k % 2], lambda d: 16 * d + k, arg_ok)
                elif kind == "seg":
                    dve.wait_ge(exp_ok.sem, exp_ok.at(lay, k + 1))
                    if k == 0:
                        dve.wait_ge(cb_cp.sem, cb_cp.at(lay, 2))
                    if k >= 2:
                        dve.wait_ge(y_ok.sem, y_ok.at(lay, k - 1))
                    g = k // 8
                    e, w = flat(SE[k % 2], 3), SW[k % 2]
                    dt = [[tok[:, i, 96 + 16 * d + k:97 + 16 * d + k] for d in range(2)] for i in range(T)]
                    c0, c1 = arena[:, CB + 2 * g, :], arena[:, CB + 2 * g + 1, :]
                    w0, w1 = arena[:, w, :], arena[:, w + 1, :]
                    stt(w0, e[:, 0:256], dt[0][0], c0, ALU.mult, ALU.mult)
                    stt(w1, e[:, 512:768], dt[1][1], c1, ALU.mult, ALU.mult)
                    stt(e[:, 256:384], e[:, 256:384], dt[0][1], c0[:, 0:P], ALU.mult, ALU.mult)
                    st.done(stt(e[:, 384:512], e[:, 384:512], dt[1][0], c1[:, P:S], ALU.mult, ALU.mult))
                    st.wait()
                    tt(w0[:, 0:P], w0[:, 0:P], e[:, 256:384], ALU.add)
                    tt(w1[:, P:S], w1[:, P:S], e[:, 384:512], ALU.add).then_inc(att_ok.sem, 1)
                elif kind == "y":
                    if k % 2 == 0:
                        return
                    j = k // 2
                    dve.wait_ge(y_ok.sem, y_ok.at(lay, k + 1))
                    stt(arena[:, XBC + j, :], arena[:, XBC + j, :], pc("ssd_d", j), A[2 + j % 2][:, 0:S],
                        ALU.mult, ALU.add).then_inc(y_cp.sem, 1)
                    dve.wait_ge(y_cp.sem, y_cp.at(lay, j + 1))
                    ins = tt(arena[:, Z + j, :], arena[:, Z + j, :], arena[:, XBC + j, :], ALU.mult)
                    if k == SSD_H - 1:
                        ins.then_inc(yz_ok.sem, 1)
                elif kind == "ssd_norm":
                    dve.wait_ge(yrs.sem, yrs.at(lay, 1))
                    for c in range(KC):
                        ins = stt(arena[:, Z + c, :], arena[:, Z + c, :], pc("ssd_g", c), rstd[:, 1, c // 4, :],
                                  ALU.mult, ALU.mult)
                    ins.then_inc(ys_fin.sem, 1)
                elif kind == "hclamp":
                    dve.wait_ge(hsig.sem, hsig.at(lay, 1))
                    for c in range(16):
                        ts(arena[:, HK + c, :], arena[:, HK + c, :], lb[:, 1, c:c + 1], None, ALU.mult)
                        ins = ts(arena[:, HF + c, :], arena[:, HF + c, :], lb[:, 1, c:c + 1], lb[:, 0, c:c + 1],
                                 ALU.mult, ALU.add)
                    st.done(ins)
                    st.wait()
                    st.done(ts(flat(HE[0], 16), flat(HF, 16), TINY, LN_FLOOR, ALU.max, ALU.min))
                    st.wait()
                    ts(flat(HF, 16), flat(HF, 16), LN_FLOOR, None, ALU.max).then_inc(hclamp.sem, 1)
                elif kind == "hvt":
                    for q in range(4):
                        dve.wait_ge(hvT.sem, hvT.at(lay, q + 1))
                        V.tensor_copy(hvtok[:, q // 2, q % 2 * 512:q % 2 * 512 + 512], A[q][:, :]).then_inc(hvT_cp.sem, 1)
                elif kind == "hlog":
                    dve.wait_ge(hln.sem, hln.at(lay, 1))
                    st.done(tt(flat(HF, 16), flat(HF, 16), flat(HE[0], 16), ALU.add))
                    st.wait()
                elif kind == "hgA":
                    b, l = divmod(k, 9)
                    e = HE[k % 2]
                    pf, sbw = flat(HF + 4 * b, 4), flat(HF + 8 + 4 * b, 4)
                    if k >= 2:
                        dve.wait_ge(hprod.sem, hprod.at(lay, k - 1))
                    if l == 0:
                        return
                    m = 1 << (l - 1)
                    n = 4 * S // (2 * m)
                    if l >= 2:
                        dve.wait_ge(hexp.sem, hexp.at(lay, 8 * b + l - 1))
                        q = m // 2
                        st.done(tt(half(pf, q, 1), half(pf, q, 1), half(pf, q, 0)[:, :, q - 1:q].broadcast_to([P, 2 * n, q]), ALU.add))
                        st.done(tt(half(sbw, q, 0), half(sbw, q, 0), half(sbw, q, 1)[:, :, 0:1].broadcast_to([P, 2 * n, q]), ALU.add))
                        st.wait()
                    ek = flat(e + 4, 4)
                    tt(half(ek, m, 0), half(pf, m, 0)[:, :, m - 1:m].broadcast_to([P, n, m]), half(pf, m, 0), ALU.subtract)
                    tt(half(ek, m, 1), half(sbw, m, 1)[:, :, 0:1].broadcast_to([P, n, m]), half(sbw, m, 1), ALU.subtract)\
                        .then_inc(hargs.sem, 1)
                elif kind == "hgB":
                    b, l = divmod(k, 9)
                    e = HE[k % 2]
                    if l == 0:
                        if k == 0:
                            dve.wait_ge(hsilu.sem, hsilu.at(lay, 1))
                        else:
                            dve.wait_ge(hprod.sem, hprod.at(lay, k - 1))
                        tt(flat(e + 4, 4), flat(HK + 4 * b, 4), flat(HK + 8 + 4 * b, 4), ALU.add)\
                            .then_inc(hqk.sem, 1)
                        return
                    m = 1 << (l - 1)
                    dve.wait_ge(hexp.sem, hexp.at(lay, 8 * b + l))
                    tt(flat(e, 4), flat(e, 4), flat(HQ + 4 * b, 4), ALU.mult)
                    ek = flat(e + 4, 4)
                    tt(half(ek, m, 0), half(ek, m, 0), half(flat(HK + 4 * b, 4), m, 0), ALU.mult)
                    tt(half(ek, m, 1), half(ek, m, 1), half(flat(HK + 8 + 4 * b, 4), m, 1), ALU.mult).then_inc(hqk.sem, 1)
                elif kind == "hgC":
                    b, l = divmod(k, 9)
                    dve.wait_ge(hprod.sem, hprod.at(lay, k + 1))
                    if k == 9:
                        dve.wait_ge(ho_ok.sem, ho_ok.at(lay, 2))
                    if k:
                        dve.wait_ge(hcp.sem, hcp.at(lay, k))
                    for i in range(T):
                        j = 1 - i if l == 8 else i
                        o = hatt[:, i, :, j * P:(j + 1) * P]
                        src = A[k % 2 * 2 + i][:, :].rearrange("p (a s) -> p a s", a=4)
                        if l in (0, 8):
                            ins = V.tensor_copy(o, src)
                        else:
                            mask = cn("lev", (l - 1) * P, l * P).bitcast(U32).rearrange("p (a s) -> p a s", a=1)
                            ins = V.copy_predicated(o, mask.broadcast_to([P, 4, P]), src)
                    ins.then_inc(hcp.sem, 1)
                elif kind == "hnorm":
                    dve.wait_ge(hrs.sem, hrs.at(lay, 1))
                    for c in range(KC):
                        ins = stt(arena[:, HQ + c, :], arena[:, HQ + c, :], pc("hg_g", c), arena[:, HE[1] + c, :],
                                  ALU.mult, ALU.mult)
                    st.done(ins)
                    st.wait()
                    tt(flat(HQ, KC), flat(HQ, KC), flat(HG, KC), ALU.mult).then_inc(yh_fin.sem, 1)
                elif kind == "mvt":
                    V.memset(mvtok[:, :, :, P:P + 1], 1.0).then_inc(mvT_cp.sem, 1)
                    for q in range(4):
                        dve.wait_ge(mvT.sem, mvT.at(lay, q + 1))
                        V.tensor_copy(mvtok[:, q // 2, q % 2 * 4:q % 2 * 4 + 4, 0:P],
                                      A[q][:, :].rearrange("p (a s) -> p a s", a=4)).then_inc(mvT_cp.sem, 1)
                elif kind == "mlA":
                    if k >= 2:
                        dve.wait_ge(matt.sem, matt.at(lay, k - 1))
                    dve.wait_ge(mbc.sem, mbc.at(lay, k + 1))
                    decay_args(ME[k % 2], A[k % 2], lambda d: 32 + 8 * d + k, marg)
                elif kind == "mlB":
                    dve.wait_ge(mexp.sem, mexp.at(lay, k + 1))
                    dve.wait_ge(mqk.sem, mqk.at(lay, k + 1))
                    if k >= 2:
                        dve.wait_ge(mnum.sem, mnum.at(lay, k - 1))
                    e, w = flat(ME[k % 2], 3), flat(MA[k % 2], 3)
                    for at, src, n in ((0, 0, 256), (256, 0, 128), (384, S + 128, 128), (512, S, 256)):
                        ins = stt(w[:, at:at + n], e[:, at:at + n], float(P) ** -0.5, A[2][:, src:src + n], ALU.mult, ALU.mult)
                    ins.then_inc(matt.sem, 1)
                elif kind == "mlC":
                    dve.wait_ge(mnum.sem, mnum.at(lay, k + 1))
                    den = small[:, 0:4].rearrange("p (i d) -> p i d", i=T)
                    for i in range(T):
                        ins = V.tensor_copy(den[:, i, :], A[3 + i][:, 0:258].rearrange("p (d e) -> p d e", d=2)[:, :, P])
                    st.done(ins)
                    st.wait()
                    st.done(stt(small[:, 4:8], small[:, 0:4], -1.0, small[:, 0:4], ALU.mult, ALU.max))
                    st.wait()
                    st.done(tt(small[:, 8:12].rearrange("p (i d) -> p i d", i=T), small[:, 4:8].rearrange("p (i d) -> p i d", i=T),
                               etok[:, :, :, k], ALU.max))
                    st.wait()
                    st.done(V.reciprocal(small[:, 12:16], small[:, 8:12]))
                    st.wait()
                    for i in range(T):
                        ins = ts(hsum[:, i, k, :], A[3 + i][:, 0:P], small[:, 12 + 2 * i:13 + 2 * i], None, ALU.mult)
                    st.done(ins)
                    st.wait()
                    for i in range(T):
                        ins = stt(hsum[:, i, k, :], A[3 + i][:, 129:129 + P], small[:, 13 + 2 * i:14 + 2 * i],
                                  hsum[:, i, k, :], ALU.mult, ALU.add)
                    ins.then_inc(mh_cp.sem, 1)
                elif kind == "mlnorm":
                    dve.wait_ge(mh_cp.sem, mh_cp.at(lay, 8))
                    x = flat(HSUM, KC).rearrange("p (n e) -> p n e", n=16)
                    st.done(V.tensor_reduce(small[:, 0:16], x, AX_X, ALU.add))
                    st.wait()
                    st.done(ts(small[:, 0:16], small[:, 0:16], 1.0 / P, None, ALU.mult))
                    st.wait()
                    tt(x, x, small[:, 0:16].rearrange("p (n e) -> p n e", e=1).broadcast_to([P, 16, P]), ALU.subtract)\
                        .then_inc(mcen.sem, 1)
                    dve.wait_ge(msq.sem, msq.at(lay, 1))
                    V.tensor_reduce(small[:, 16:32], flat(SQ, KC).rearrange("p (n e) -> p n e", n=16), AX_X, ALU.add)\
                        .then_inc(mvar.sem, 1)
                    dve.wait_ge(mrs.sem, mrs.at(lay, 1))
                    tt(x, x, small[:, 48:64].rearrange("p (n e) -> p n e", e=1).broadcast_to([P, 16, P]), ALU.mult)\
                        .then_inc(mhn.sem, 1)
                elif kind == "mlturn":
                    dve.wait_ge(msig.sem, msig.at(lay, 1))
                    for q in range(4):
                        dve.wait_ge(mhT.sem, mhT.at(lay, q + 1))
                        for a in range(2):
                            c = 2 * q + a
                            ins = stt(arena[:, MO + c, :], A[q][:, a * S:(a + 1) * S], pc("ml_g", c), arena[:, MO + c, :],
                                      ALU.mult, ALU.mult)
                    ins.then_inc(ym_fin.sem, 1)
                elif kind == "split":
                    i = k - OF["up"]
                    dve.wait_ge(whi_ok.sem, whi_ok.at(lay, i + 1))
                    w = ring[:, k % RING, :]
                    tt(ring_r[:, k % RING, :], w, flat_r(WHI[i % 3], KC).bitcast(F32), ALU.subtract).then_inc(wlo_ok.sem, 1)
                elif kind == "hsplit":
                    dve.wait_ge(hhi_ok.sem, hhi_ok.at(lay, k + 1))
                    x = arena[:, HID + k, :]
                    tt(flat_r(HID + k, 1), x, flat_r(HIDHI + k, 1).bitcast(F32), ALU.subtract).then_inc(hlo_ok.sem, 1)
                elif kind == "hid":
                    dve.wait_ge(silu_ok.sem, silu_ok.at(lay, k + 1))
                    f = FT[k % 2]
                    tt(arena[:, HID + k, :], arena[:, f, :], arena[:, f + 1, :], ALU.mult).then_inc(hid_ok.sem, 1)
                elif kind == "ple_add":
                    dve.wait_ge(*evac(lay, OF["pleg"] + k))
                    dve.wait_ge(ple_cp.sem, ple_cp.at(lay, 1))
                    g = flat(PLG + 2 * k, 2)
                    st.done(tt(g, g, flat(PLE + 2 * k, 2), ALU.mult))
                    st.wait()
                    tt(g, g, h[:, 2 * k:2 * k + 2, :].rearrange("p c s -> p (c s)"), ALU.add).then_inc(h_new.sem, 1)

            def norm2(n, scale, shift):
                dve.wait_ge(rs_ready.sem, rs_ready.at(DEPTH, n))
                if shift is None:
                    for c in range(KC):
                        ins = stt(h[:, c, :] if n == 1 else arena[:, c, :], (chunks(PLG, KC) if n == 1 else h)[:, c, :], p2(scale, c), rstd[:, 1, 0, :],
                                  ALU.mult, ALU.mult)
                    ins.then_inc(*((u_ready.sem, 1) if n == 1 else (y2_fin, 1)))
                    return
                st.done(tt(u[:], h[:], rstd[:, 1, 0:1, :].broadcast_to([P, KC, S]), ALU.mult))
                st.wait()
                for c in range(KC):
                    ins = ts(u[:, c, :], u[:, c, :], mod[:, scale + c:scale + c + 1], mod[:, shift + c:shift + c + 1],
                             ALU.mult, ALU.add)
                ins.then_inc(u_ready.sem, 1)

            V.memset(eps[:], EPS).then_inc(eps_set, 1)
            dve.wait_ge(con_in, 16)
            for lay in range(DEPTH):
                for kind, k in sched:
                    item(kind, k, lay)
            dve.wait_ge(par2_in, 32)
            norm2(1, "fin1_g", None)
            st.wait()
            lam = p2("lam", 0, 4)
            st.done(tt(small[0:64, 0:1], lam[0:64, 0:1], lam[0:64, 1:2], ALU.mult))
            tt(small[0:64, 1:2], lam[0:64, 2:3], lam[0:64, 3:4], ALU.mult).then_inc(lam_in, 1)
            dve.wait_ge(ada_mm, ADA_UNITS // 2)
            st.done(tt(mod[:, 0:48], A[2][:, 0:48], p2("b_ada", 0, 48), ALU.add))
            st.wait()
            st.done(stt(mod[:, 48:56], mod[:, 8:16], 1.0, p2("n1_g", 0, 8), ALU.add, ALU.mult))
            st.done(stt(mod[:, 56:64], mod[:, 32:40], 1.0, p2("n2_g", 0, 8), ALU.add, ALU.mult))
            st.done(ts(mod[:, 73:74], p2("sub_g"), 1.0 - LAMBDA_INIT, None, ALU.mult))
            dve.wait_ge(lam_exp, 1)
            st.done(tt(small[:, 4:5], small[:, 3:4], small[:, 2:3], ALU.subtract))
            st.wait()
            st.done(ts(mod[:, 72:73], small[:, 4:5], -LAMBDA_INIT, None, ALU.add))
            st.wait()
            norm2(2, 48, 0)
            for j in (6, 7):
                b, before = use2(q_unit(j))
                dve.wait_ge(freed[b].sem, before + 1)
            W = S + 16
            pa = flat(PADA, 5)[:, 0:4 * W].rearrange("p (g w) -> p g w", g=4)
            pb = flat(PADB, 5)[:, 0:4 * W].rearrange("p (g w) -> p g w", g=4)
            st.done(V.memset(pa[:, :, 0:8], 0.0))
            st.done(V.memset(pa[:, :, W - 8:W], 0.0))
            st.done(V.tensor_copy(pa[:, :, 8:8 + S], chunks(U2, 4)))
            st.wait()
            st.done(tt(pb[:, :, 1:W], pa[:, :, 0:W - 1], pa[:, :, 1:W], ALU.add))
            st.wait()
            src, dst, lo = pb, pa, 1
            for g in range(4):
                st.done(tt(arena[:, RD + g, :], src[:, g, 8:8 + S], c2("cnt", g * S, (g + 1) * S), ALU.mult))
                st.wait()
                ins = tt(arena[:, RD + g, :], arena[:, RD + g, :], arena[:, U2 + g, :], ALU.subtract)
                if g == 3:
                    ins.then_inc(pool_d, 1)
                    break
                st.done(ins)
                k = 1 << g
                hi = W - lo if g else W
                st.done(tt(dst[:, g + 1:4, lo + k:hi - k], src[:, g + 1:4, lo:hi - 2 * k], src[:, g + 1:4, lo + 2 * k:hi], ALU.add))
                st.wait()
                src, dst, lo = dst, src, lo + k
            for n in range(2):
                dve.wait_ge(pool_mm, n + 1)
                for g in (2 * n, 2 * n + 1):
                    ins = ts(arena[:, P2 + g, :], A[4][:, g % 2 * S:g % 2 * S + S], p2("pool_s", g), None, ALU.mult)
                ins.then_inc(pool_fin, 1)
            for q in range(4):
                dve.wait_ge(rope_mm, q + 1)
                x = chunks(Q2 + 2 * q, 2)
                t = chunks(PADA + 2 * q, 2)
                sin, cos = (c2(n, 0, S).rearrange("p (c s) -> p c s", c=1).broadcast_to([P, 2, S]) for n in ("sin", "cos"))
                st.done(tt(t, A[q][:, :].rearrange("p (c s) -> p c s", c=2), sin, ALU.mult))
                st.done(tt(x, x, cos, ALU.mult))
                st.wait()
                tt(x, x, t, ALU.add).then_inc(rope_ok, 1)
            for i in range(T):
                dve.wait_ge(v2T, i + 1)
                V.tensor_copy(v2tok[:, i, :], A[i][:, :]).then_inc(v2T_cp, 1)

            def maxima(hd):
                dve.wait_ge(sc_ok, hd + 1)
                if hd >= 2:
                    dve.wait_ge(w2_ok, hd - 1)
                n = 4 * (hd % 2)
                for c in range(2):
                    ins = V.tensor_reduce(small[:, 24 + n + 2 * c:26 + n + 2 * c],
                                          A[hd % 2 * 2 + c][:, :].rearrange("p (c s) -> p c s", c=2), AX_X, ALU.max)
                st.done(ins)
                st.wait()
                ts(small[:, 8 + n:12 + n], small[:, 24 + n:28 + n], -(HD2 ** -0.5), None, ALU.mult).then_inc(sc_max, 1)

            def weights(hd):
                n = 4 * (hd % 2)
                dve.wait_ge(sc_exp, 4 * (hd + 1))
                if hd >= 2:
                    dve.wait_ge(w2T, hd - 1)
                r = small[:, 32 + n:36 + n]
                st.done(V.reciprocal(small[:, 32 + n:36 + n], small[:, 16 + n:20 + n]))
                st.wait()
                st.done(ts(r[:, 2:4], r[:, 2:4], mod[:, 72:73], None, ALU.mult))
                st.wait()
                for i in range(T):
                    ins = ts(arena[:, WA[hd % 2] + i, :], arena[:, EA[hd % 2] + i, :], r[:, i:i + 1], None, ALU.mult)
                st.done(ins)
                st.wait()
                for i in range(T):
                    ins = stt(arena[:, WA[hd % 2] + i, :], arena[:, EA[hd % 2] + 2 + i, :], r[:, 2 + i:3 + i],
                              arena[:, WA[hd % 2] + i, :], ALU.mult, ALU.add)
                ins.then_inc(w2_ok, 1)

            def turned(hd):
                dve.wait_ge(w2T, hd + 1)
                if hd >= 2:
                    dve.wait_ge(o2_ok, hd - 1)
                V.tensor_copy(flat(WAT[hd % 2], 2), A[4][:, :]).then_inc(w2T_cp, 1)

            maxima(0)
            maxima(1)
            for hd in range(HEADS2):
                weights(hd)
                turned(hd)
                if hd + 2 < HEADS2:
                    maxima(hd + 2)
            dve.wait_ge(o2_rs, 1)
            for hd in range(HEADS2):
                ins = stt(arena[:, O2 + hd, :], arena[:, O2 + hd, :], mod[:, 73:74], arena[:, RD + hd, :], ALU.mult, ALU.mult)
            ins.then_inc(o2_fin, 1)
            for m in range(WOUT2, ROUTER):
                b, before = use2(m)
                dve.wait_ge(*done2(m))
                for c in range(2):
                    n = 2 * (m - WOUT2) + c
                    ins = stt(h[:, n, :], G[b][:, c * S:(c + 1) * S], mod[:, 16 + n:17 + n], h[:, n, :], ALU.mult, ALU.add)
                ins.then_inc(freed[b].sem, 1)
            norm2(3, 56, 24)
            dve.wait_ge(*done2(ROUTER))
            lg = flat(RD, 1)[:, 0:T * 36].rearrange("p (i n) -> p i n", i=T)
            st.done(V.tensor_copy(lg, A[0][:, 0:128].rearrange("p (i n) -> p i n", i=T)[:, :, 0:36]))
            st.wait()
            scr = flat(RD + 1, 2)

            def view(at, *dims):
                n = int(np.prod(dims))
                v = scr[:, at:at + T * n]
                if len(dims) == 1:
                    return v.rearrange("p (i a) -> p i a", i=T)
                return v.rearrange("p (i a b) -> p i a b", i=T, a=dims[0])

            def op(ins):
                st.done(ins)
                st.wait()

            def first_max(x, n, at):
                mx, t, mn, oh = view(at, 1), view(at + 2, n), view(at + 2 + 2 * n, 1), view(at + 4 + 2 * n, n)
                io = c2("iota", 0, n).rearrange("p (i n) -> p i n", i=1).broadcast_to([P, T, n])
                op(V.tensor_reduce(mx, x, AX_X, ALU.max))
                op(tt(t, x, mx.broadcast_to([P, T, n]), ALU.is_equal))
                op(stt(t, t, -100.0, io, ALU.mult, ALU.add))
                op(V.tensor_reduce(mn, t, AX_X, ALU.min))
                op(ts(mn, mn, 100.0, None, ALU.add))
                op(tt(oh, io, mn.broadcast_to([P, T, n]), ALU.is_equal))
                return mx, oh

            gl = lg[:, :, 0:4]
            gmx, goh = first_max(gl, 4, 0)
            tt(small[:, 0:8].rearrange("p (i n) -> p i n", i=T), gl, gmx.broadcast_to([P, T, 4]), ALU.subtract).then_inc(r_sh, 1)
            el = lg[:, :, 4:36].rearrange("p i (g j) -> p i g j", g=4)
            pr = view(40, 4, 8)
            op(tt(pr, el, goh.rearrange("p i (g o) -> p i g o", o=1).broadcast_to([P, T, 4, 8]), ALU.mult))
            ein = view(110, 8)
            op(V.tensor_reduce(ein, pr.rearrange("p i g j -> p i j g"), AX_X, ALU.add))
            m1, oh1 = first_max(ein, 8, 130)
            rest = view(180, 8)
            op(stt(rest, oh1, NEG, ein, ALU.mult, ALU.add))
            m2, oh2 = first_max(rest, 8, 200)
            tt(small[:, 16:18].rearrange("p (i n) -> p i n", i=T), m2, m1, ALU.subtract).then_inc(r_sh, 1)
            dve.wait_ge(r_exp, 2)
            op(V.tensor_reduce(small[:, 20:22], small[:, 8:16].rearrange("p (i n) -> p i n", i=T), AX_X, ALU.add))
            op(ts(small[:, 22:24], small[:, 18:20], 1.0, None, ALU.add))
            op(V.reciprocal(small[:, 24:28], small[:, 20:24]))
            op(tt(small[:, 28:30], small[:, 24:26], small[:, 26:28], ALU.mult))
            op(tt(small[:, 30:32], small[:, 28:30], small[:, 18:20], ALU.mult))

            def col(at):
                return small[:, at:at + 2].rearrange("p (i n) -> p i n", i=T).broadcast_to([P, T, 8])

            hot8, slot = view(270, 8), view(300, 32)
            member = flat(MEMBER, 1)[:, 0:64].rearrange("p (i g j) -> p i g j", i=T, g=4)
            op(tt(hot8, oh1, oh2, ALU.add))
            for i in range(T):
                ins = tt(member[:, i], goh[:, i].rearrange("p (g o) -> p g o", o=1).broadcast_to([P, 4, 8]),
                         hot8[:, i:i + 1, :].broadcast_to([P, 4, 8]), ALU.mult)
                if i:
                    st.wait()
                    ins.then_inc(r_mem, 1)
                else:
                    st.done(ins)
            w8 = view(250, 8)
            op(tt(oh1, oh1, col(28), ALU.mult))
            op(tt(oh2, oh2, col(30), ALU.mult))
            op(tt(w8, oh1, oh2, ALU.add))
            wrow = small[:, 128:192].rearrange("p (i g j) -> p i g j", i=T, g=4)
            for i in range(T):
                ins = tt(wrow[:, i], goh[:, i].rearrange("p (g o) -> p g o", o=1).broadcast_to([P, 4, 8]),
                         w8[:, i:i + 1, :].broadcast_to([P, 4, 8]), ALU.mult)
                if i:
                    ins.then_inc(r_w, 1)
                else:
                    st.done(ins)
            st.wait()
            for q in range(4):
                dve.wait_ge(utT, q + 1)
                V.tensor_copy(utok[:, q // 2, q % 2 * 512:q % 2 * 512 + 512], A[1 + q][:, :]).then_inc(utT_cp, 1)
            dve.wait_ge(r_cum, 1)
            dve.wait_ge(r_mem, 1)
            op(V.tensor_reduce(small[:, 36:37], A[0][:, 320:352], AX_X, ALU.max))
            ts(path[:, 0:1], small[:, 36:37], SLOTS + 0.5, None, ALU.is_gt).then_inc(path_ok, 1)
            members = flat(MEMBER, 1)[:, 0:64].rearrange("p (i n) -> p i n", i=T)
            op(tt(slot, A[0][:, 256:320].rearrange("p (i n) -> p i n", i=T), members, ALU.mult))
            op(ts(slot, slot, -1.0, None, ALU.add))

            def dense():
                dve.wait_ge(r_T, 1)
                V.tensor_copy(rowt[:, :], A[1][0:32, 0:S]).then_inc(r_wT, 1)
                for q in range(EXPERTS // 2):
                    dve.wait_ge(wb_mm, q + 1)
                    V.tensor_copy(flat(WB + 2 * q, 2), A[q % 4][:, :]).then_inc(wb_cp, 1)
                dve.wait_ge(wb_cp, EXPERTS // 2)
                hidden(0, 0)
                hidden(1, 1)
                with dve.Fori(0, (EXPERTS - 2) // 2) as i:
                    for a in range(2):
                        dve.wait_ge(unit_done.sem, (i * 2 + a) * 6 + (B2 + MOE + 10))
                        hidden(i * 2 + (a + 2), a)
                dve.wait_ge(*done2(UNITS2 - 1))

            def hidden(e, parity):
                for j in range(4):
                    dve.wait_ge(gate_ok, e * 4 + (j + 1))
                    o = arena[:, HIDE[parity] + j, :]
                    if j < 3:
                        tt(o, arena[:, SG2 + j, :], E4[j][:, S:2 * S], ALU.mult).then_inc(freed[j].sem, 1)
                        dve.wait_ge(freed[j].sem, e + (G2 + 1))
                    else:
                        tt(o, arena[:, SG2 + j, :], E4[j][:, S:2 * S], ALU.mult).then_inc(e4_freed, 1)
                        dve.wait_ge(e4_freed, e + 1)
                    tt(o, o, wb[:, e, :], ALU.mult).then_inc(hide_ok, 1)

            wb = chunks(WB, EXPERTS)

            def slot_hidden(r, c):
                dve.wait_ge(sg_ok, r + (c + 1))
                if c or not isinstance(r, int):
                    dve.wait_ge(ht_mm, r + c)
                tt(flat(HSE, 2)[0:SLOTS], flat(SGE, 2)[0:SLOTS], G[0][64:64 + SLOTS, :], ALU.mult).then_inc(hs_ok, 1)

            def slot_turned(r, c):
                dve.wait_ge(ht_mm, r + (c + 1))
                V.tensor_copy(flat(HTE, 1), A[4][:, 0:4 * SLOTS]).then_inc(ht_cp, 1)
                if c >= 2 or not isinstance(r, int):
                    dve.wait_ge(s_sum, r + (c - 1))
                V.tensor_copy(arena[:, WNOW[c % 2], :], ws[:, r + c, :]).then_inc(wn_cp, 1)

            def compact():
                iota = c2("iota", 0, SLOTS).rearrange("p (e s) -> p e s", e=1).broadcast_to([P, EXPERTS, SLOTS])
                for i in range(T):
                    at = slot[:, i].rearrange("p (e s) -> p e s", s=1).broadcast_to([P, EXPERTS, SLOTS])
                    ins = tt(pick[:, i], at, iota, ALU.is_equal)
                ins.then_inc(pick_ok, 1)
                dve.wait_ge(pick_ok, 1)
                for i in range(T):
                    w = small[:, 128 + 32 * i:160 + 32 * i].rearrange("p (e s) -> p e s", s=1)
                    ins = tt(pickw[:, i], pick[:, i], w.broadcast_to([P, EXPERTS, SLOTS]), ALU.mult)
                ins.then_inc(pickw_ok, 1)
                slot_hidden(0, 0)
                dve.wait_ge(ws_cp, PAIRS)
                for e in range(2):
                    slot_turned(0, e)
                    slot_hidden(0, e + 1)
                with dve.Fori(0, PAIRS - 2) as i:
                    for a in range(2):
                        slot_turned(i * 2, 2 + a)
                        slot_hidden(i * 2, 3 + a)
                slot_turned(0, EXPERTS - 2)
                slot_hidden(0, EXPERTS - 1)
                slot_turned(0, EXPERTS - 1)
                dve.wait_ge(s_sum, EXPERTS)

            dve.wait_ge(path_ok, 1)
            some_over = dve.value_load(path[0:1, 0:1].bitcast(I32), min_val=0, max_val=ONE_BITS)
            with dve.If(some_over != 0):
                dense()
            with dve.Else():
                compact()
            for c in range(KC):
                ins = stt(h[:, c, :], A[c // 2][:, c % 2 * S:c % 2 * S + S], mod[:, 40 + c:41 + c], h[:, c, :], ALU.mult, ALU.add)
            ins.then_inc(y2_fin, 1)
            norm2(4, "fin2_g", None)




def units(w):
    n = w.shape[1]
    return w.reshape(KC, P, n // UC, UC).transpose(2, 1, 0, 3).reshape(n // UC, P, UNIT)


def by_channel(v):
    return v.reshape(-1, P).T


def layer_units(i, lay):
    sizes = (("z", D), ("xbc", 1536), ("dt", 32), ("hq", D), ("hf", 2 * D), ("hi", D), ("hg", D), ("mq", D), ("mk", D),
             ("mv", D), ("mi", 16), ("mf", 16), ("mo", D), ("gates", 3 * D))
    seg, at = {}, 0
    for name, n in sizes:
        seg[name] = i["w_in"][lay][:, at:at + n]
        at += n
    rows = np.zeros((D, UC), np.float32)
    rows[:, 0:32], rows[:, 32:48], rows[:, 64:80] = seg["dt"], seg["mi"], seg["mf"]
    g = seg["gates"]
    parts = [units(rows)] + [units(seg[k]) for k in ("z", "xbc", "hf", "hq", "hi", "hg", "mq", "mk", "mv", "mo")]
    parts.append(np.stack([units(g[:, :D]), units(i["w_br_ssd"][lay])], 1).reshape(8, P, UNIT))
    parts += [units(w) for w in (g[:, D:2 * D], g[:, 2 * D:], i["w_br_hg"][lay], i["w_br_ml"][lay], i["w_out"][lay])]
    parts.append(units(i["w_up"][lay].reshape(D, 2, FC, P).transpose(0, 2, 1, 3).reshape(D, FC * UC)))
    down = np.zeros((3 * D, D), np.float32)
    down[:FF] = i["w_down"][lay]
    parts.append(down.reshape(3, KC, P, 4, UC).transpose(3, 0, 2, 1, 4).reshape(12, P, UNIT))
    parts.append(i["w_ple"][lay].reshape(2, P, D).transpose(1, 0, 2).reshape(1, P, UNIT))
    parts.append(units(i["w_ple_gate"][lay]))
    return np.concatenate(parts)


def layer_parameters(i, lay):
    par = np.zeros((P, NPAR), np.float32)

    def put(name, a):
        par[:a.shape[0], PAR[name]:PAR[name] + a.shape[1]] = a

    put("mix_g", by_channel(i["norm_mix_g"][lay]))
    put("conv_w", i["ssd_conv_w"][lay].reshape(SSD_CONV, 12, P).transpose(2, 1, 0).reshape(P, 60))
    put("conv_b", by_channel(i["ssd_conv_b"][lay]))
    put("ssd_d", by_channel(np.repeat(i["ssd_d"][lay], 64)))
    put("ssd_g", by_channel(i["ssd_norm_g"][lay]))
    put("hg_g", by_channel(i["hg_norm_g"][lay]))
    put("ml_g", by_channel(i["ml_norm_g"][lay]))
    put("ffn_g", by_channel(i["norm_ffn_g"][lay]))
    put("fconv_w", i["ffn_conv_w"][lay].reshape(FFN_CONV, 2 * FC, P).transpose(2, 1, 0).reshape(P, 132))
    put("fconv_b", by_channel(i["ffn_conv_b"][lay]))
    row_b = np.zeros((P, 1), np.float32)
    row_b[:32, 0] = i["ssd_dt_bias"][lay].ravel()
    row_b[32:48, 0] = i["ml_i_bias"][lay].ravel()
    row_b[64:80, 0] = i["ml_f_bias"][lay].ravel()
    put("row_b", row_b)
    put("a_log", i["ssd_a_log"][lay].reshape(32, 1))
    put("lb_raw", np.concatenate([by_channel(i["hg_lb_raw"][j].ravel()) for j in range(DEPTH)], 1))
    put("lb_mask", np.tile(np.array([[1.0, float(lay >= 1)]], np.float32), (P, 1)))
    put("p", i["p"][lay, 0].T.reshape(2, P, S).transpose(1, 0, 2).reshape(P, 2 * S))
    return par


def second_units(i):
    router = np.zeros((D, UC), np.float32)
    router[:, 0:GROUPS] = i["w_router_group_2"][0]
    router[:, GROUPS:GROUPS + EXPERTS] = i["w_router_expert_2"][0]
    gate_up = np.concatenate([i["w_gate_2"][0], i["w_up_2"][0]], 2)
    gate_up = gate_up.reshape(EXPERTS, 4, 2, P, D).transpose(0, 1, 3, 2, 4).reshape(EXPERTS, 4, P, UNIT)
    down = i["w_down_2"][0].reshape(EXPERTS, 2, 2, P, D).transpose(0, 1, 3, 2, 4).reshape(EXPERTS, 2, P, UNIT)
    experts = np.concatenate([gate_up, down], 1)
    order = moe_order()
    return np.concatenate([units(i["w_ada_2"][0]), units(i["w_in_2"][0])[list(WIN_ORDER)], units(i["w_out_2"][0]), units(router),
                           experts[[e for e, _ in order], [j for _, j in order]]])


def second_parameters(i):
    par = np.zeros((P, NPAR2), np.float32)

    def put(name, a):
        par[:a.shape[0], PAR2[name]:PAR2[name] + a.shape[1]] = a

    for name, key in (("c", "c_2"), ("b_ada", "b_ada_2"), ("n1_g", "norm1_g_2"), ("n2_g", "norm2_g_2"),
                      ("sub_g", "subln_g_2")):
        put(name, by_channel(i[key][0]))
    put("fin1_g", by_channel(i["final_norm_g"]))
    put("fin2_g", by_channel(i["final_g_2"]))
    put("pool_s", i["pool_scale_2"][0].T)
    put("lam", np.stack([i[f"lambda_{k}_2"][0] for k in ("q1", "k1", "q2", "k2")], 1))
    put("w_pool", i["w_pool_2"][0].transpose(1, 0, 2).reshape(P, 4 * P))
    put("b_route", np.concatenate([i["b_router_group_2"][0], i["b_router_expert_2"][0]])[None])
    return par


def kernel(**inputs):
    import concourse.bacc as _bacc
    from concourse.bass_utils import run_bass_kernel_spmd as _run

    i = {k: np.asarray(v) for k, v in inputs.items()}
    x = i["x"][0].T.reshape(KC, P, S).transpose(1, 0, 2).reshape(P, KC * S)
    arrays = {
        "stream": np.concatenate([layer_units(i, 0), layer_units(i, 1), second_units(i)]),
        "par_d": np.stack([layer_parameters(i, lay) for lay in range(DEPTH)]),
        "con_d": constants(),
        "x_d": np.ascontiguousarray(x),
        "par2_d": second_parameters(i),
        "con2_d": constants2(),
    }
    nc = _bacc.Bacc("TRN2", target_bir_lowering=False, num_devices=1)
    args = [nc.dram_tensor(name, a.shape, F32, kind="ExternalInput").ap() for name, a in arrays.items()]
    out = nc.dram_tensor("out", (P, KC * S), F32, kind="ExternalOutput").ap()
    program(nc, *args, out)
    r = _run(nc, [arrays], core_ids=[0])
    return r.results[0]["out"].reshape(P, KC, S).transpose(2, 1, 0).reshape(1, S, D)
```
